# Optimizing a Trainium2 kernel written in Bass

```python
import math
import jax, jax.numpy as jnp
from jax import lax
import numpy as np

D_MODEL = 1024
BATCH = 1
SEQ = 256
DEPTH = 1

PLE_DIM = 256
N_DIFF_HEADS = 8
DIFF_HEAD_DIM = 64
DIFF_V_DIM = 2 * DIFF_HEAD_DIM
N_RET_HEADS = 4
RET_KEY_DIM = 128
RET_VAL_DIM = 2 * RET_KEY_DIM
D_FF = 4 * D_MODEL
Q_BLOCK = 128
RET_CHUNK = 128
EPS = 1e-6

DIFF_QK_W = N_DIFF_HEADS * 2 * DIFF_HEAD_DIM
DIFF_V_W = N_DIFF_HEADS * DIFF_V_DIM
RET_QK_W = N_RET_HEADS * RET_KEY_DIM
RET_V_W = N_RET_HEADS * RET_VAL_DIM
IN_SPLITS = (DIFF_QK_W, DIFF_QK_W, DIFF_V_W,
             RET_QK_W, RET_QK_W, RET_V_W, RET_V_W,
             D_MODEL, D_MODEL)
D_IN = sum(IN_SPLITS)


def rms_norm(x, g):
    xf = x.astype(jnp.float32)
    y = xf * lax.rsqrt(jnp.mean(xf * xf, axis=-1, keepdims=True) + EPS)
    return (y * g.astype(jnp.float32)).astype(x.dtype)

def alibi_slopes(n_heads):
    return 2.0 ** (-8.0 * jnp.arange(1, n_heads + 1, dtype=jnp.float32) / n_heads)

def diff_attention(q, k, v, lam):
    B, S, H, _, d = q.shape
    e = v.shape[-1]
    n_blocks = S // Q_BLOCK
    scale = d ** -0.5
    kpos = jnp.arange(S)
    slopes = alibi_slopes(H)[:, None, None, None]

    def block(i):
        start = i * Q_BLOCK
        qb = lax.dynamic_slice_in_dim(q, start, Q_BLOCK, axis=1)
        s = jnp.einsum('bqhcd,bkhcd->bhcqk', qb, k).astype(jnp.float32) * scale
        qpos = start + jnp.arange(Q_BLOCK)
        dist = (qpos[:, None] - kpos[None, :]).astype(jnp.float32)
        logits = jnp.where(dist >= 0, s - slopes * dist, -jnp.inf)
        probs = jax.nn.softmax(logits, axis=-1)
        a = probs[:, :, 0] - lam * probs[:, :, 1]
        return jnp.einsum('bhqk,bkhe->bqhe', a.astype(v.dtype), v)

    out = lax.map(block, jnp.arange(n_blocks))
    return out.transpose(1, 0, 2, 3, 4).reshape(B, S, H, e)

def retention(q, k, v):
    B, S, H, dk = q.shape
    dv = v.shape[-1]
    C = RET_CHUNK
    n_chunks = S // C
    dt = q.dtype
    log_gamma = jnp.log(1.0 - 2.0 ** (-5.0 - jnp.arange(H, dtype=jnp.float32)))
    pos = jnp.arange(C, dtype=jnp.float32)
    rel = pos[:, None] - pos[None, :]
    decay_intra = jnp.where(rel >= 0, jnp.exp(log_gamma[:, None, None] * rel), 0.0).astype(dt)
    q_decay = jnp.exp(log_gamma[None, :] * (pos[:, None] + 1.0)).astype(dt)
    k_decay = jnp.exp(log_gamma[:, None] * (C - 1.0 - pos[None, :])).astype(dt)
    chunk_decay = jnp.exp(log_gamma * C).astype(dt)

    k = k * (dk ** -0.5)
    to_chunks = lambda t: t.reshape(B, n_chunks, C, H, t.shape[-1]).transpose(1, 0, 2, 3, 4)
    qc, kc, vc = to_chunks(q), to_chunks(k), to_chunks(v)

    def step(R, inp):
        qi, ki, vi = inp
        s = jnp.einsum('bnhk,bmhk->bhnm', qi, ki) * decay_intra
        intra = jnp.einsum('bhnm,bmhv->bnhv', s, vi)
        cross = jnp.einsum('bnhk,bhkv->bnhv', qi, R) * q_decay[None, :, :, None]
        R_new = R * chunk_decay[None, :, None, None] + jnp.einsum('bmhk,bmhv,hm->bhkv', ki, vi, k_decay)
        return R_new, intra + cross

    R0 = jnp.zeros((B, H, dk, dv), dt)
    _, out = lax.scan(step, R0, (qc, kc, vc))
    return out.transpose(1, 0, 2, 3, 4).reshape(B, S, H, dv)

def first_inputs(seed: int = 0) -> dict:
    key = jax.random.key(seed)
    ks = jax.random.split(key, 24)
    f32 = jnp.float32
    nrm = lambda k, shape, s: (jax.random.normal(k, shape, f32) * s)
    gain = lambda k, shape: 1.0 + 0.02 * jax.random.normal(k, shape, f32)
    L = DEPTH
    return {
        "x": nrm(ks[0], (BATCH, SEQ, D_MODEL), 1.0),
        "p": nrm(ks[1], (DEPTH, BATCH, SEQ, PLE_DIM), 1.0),
        "g_mix": gain(ks[2], (L, D_MODEL)),
        "w_in": nrm(ks[3], (L, D_MODEL, D_IN), D_MODEL ** -0.5),
        "lam_q1": nrm(ks[4], (L, DIFF_HEAD_DIM), 0.1),
        "lam_k1": nrm(ks[5], (L, DIFF_HEAD_DIM), 0.1),
        "lam_q2": nrm(ks[6], (L, DIFF_HEAD_DIM), 0.1),
        "lam_k2": nrm(ks[7], (L, DIFF_HEAD_DIM), 0.1),
        "g_diff_sub": gain(ks[8], (L, DIFF_V_DIM)),
        "g_ret_sub": gain(ks[9], (L, N_RET_HEADS, RET_VAL_DIM)),
        "w_branch_diff": nrm(ks[10], (L, DIFF_V_W, D_MODEL), DIFF_V_W ** -0.5),
        "w_branch_ret": nrm(ks[11], (L, RET_V_W, D_MODEL), RET_V_W ** -0.5),
        "w_out": nrm(ks[12], (L, D_MODEL, D_MODEL), D_MODEL ** -0.5),
        "g_mlp": gain(ks[13], (L, D_MODEL)),
        "w_ff1": nrm(ks[14], (L, D_MODEL, D_FF), D_MODEL ** -0.5),
        "w_ff2": nrm(ks[15], (L, D_FF, D_MODEL), D_FF ** -0.5),
        "g_ple": gain(ks[16], (L, D_MODEL)),
        "w_ple_gate": nrm(ks[17], (L, D_MODEL, D_MODEL), D_MODEL ** -0.5),
        "w_ple": nrm(ks[18], (L, PLE_DIM, D_MODEL), PLE_DIM ** -0.5),
        "g_final": gain(ks[19], (D_MODEL,)),
    }

def first_block(x, p, g_mix, w_in, lam_q1, lam_k1, lam_q2, lam_k2, g_diff_sub, g_ret_sub,
              w_branch_diff, w_branch_ret, w_out, g_mlp, w_ff1, w_ff2, g_ple, w_ple_gate,
              w_ple, g_final):
    B, S, _ = x.shape
    split_idx = list(np.cumsum(IN_SPLITS)[:-1])
    for i in range(DEPTH):
        h = rms_norm(x, g_mix[i])
        proj = h @ w_in[i]
        qa, ka, va, qr, kr, vr, gr, gate_a, gate_r = jnp.split(proj, split_idx, axis=-1)

        lam_init = 0.8 - 0.6 * math.exp(-0.3 * i)
        lam = (jnp.exp(jnp.sum(lam_q1[i] * lam_k1[i]).astype(jnp.float32))
               - jnp.exp(jnp.sum(lam_q2[i] * lam_k2[i]).astype(jnp.float32)) + lam_init)
        qa = qa.reshape(B, S, N_DIFF_HEADS, 2, DIFF_HEAD_DIM)
        ka = ka.reshape(B, S, N_DIFF_HEADS, 2, DIFF_HEAD_DIM)
        va = va.reshape(B, S, N_DIFF_HEADS, DIFF_V_DIM)
        ya = diff_attention(qa, ka, va, lam)
        ya = (rms_norm(ya, g_diff_sub[i]) * (1.0 - lam_init)).reshape(B, S, DIFF_V_W)

        qr = qr.reshape(B, S, N_RET_HEADS, RET_KEY_DIM)
        kr = kr.reshape(B, S, N_RET_HEADS, RET_KEY_DIM)
        vr = vr.reshape(B, S, N_RET_HEADS, RET_VAL_DIM)
        yr = rms_norm(retention(qr, kr, vr), g_ret_sub[i]).reshape(B, S, RET_V_W)
        yr = jax.nn.silu(gr) * yr

        mixed = (jax.nn.sigmoid(gate_a) * (ya @ w_branch_diff[i])
                 + jax.nn.sigmoid(gate_r) * (yr @ w_branch_ret[i]))
        x = x + mixed @ w_out[i]

        h2 = rms_norm(x, g_mlp[i])
        x = x + jnp.square(jax.nn.relu(h2 @ w_ff1[i])) @ w_ff2[i]

        gate_p = jax.nn.sigmoid(rms_norm(x, g_ple[i]) @ w_ple_gate[i])
        x = x + gate_p * (p[i] @ w_ple[i])
    return rms_norm(x, g_final)


D_MIX = D_MODEL
MLA_HEADS = 8
MLA_NOPE = 64
MLA_ROPE = 32
MLA_V = 64
MLA_Q_RANK = 384
MLA_KV_RANK = 256
ROPE_BASE = 10000.0
MOBA_HEADS = 8
MOBA_HEAD_DIM = 64
MOBA_BLOCK = 256
MOBA_TOPK = 3
D_FF_2 = 2816
FFN_RES = 0.5
NEG_INF = -1e30

IN_SPLITS_2 = (MLA_Q_RANK, MLA_KV_RANK, MLA_ROPE,
             MOBA_HEADS * MOBA_HEAD_DIM, MOBA_HEADS * MOBA_HEAD_DIM, MOBA_HEADS * MOBA_HEAD_DIM)
D_IN_2 = sum(IN_SPLITS_2)
D_CAT = MLA_HEADS * MLA_V + MOBA_HEADS * MOBA_HEAD_DIM


def rms_norm_2(x, g):
    xf = x.astype(jnp.float32)
    y = xf * lax.rsqrt(jnp.mean(xf * xf, axis=-1, keepdims=True) + EPS)
    return (y * g.astype(jnp.float32)).astype(x.dtype)

def swiglu(x, w_gate, w_up, w_down):
    return (jax.nn.silu(x @ w_gate) * (x @ w_up)) @ w_down

def apply_rope(x, pos):
    r = x.shape[-1]
    half = r // 2
    inv = jnp.power(ROPE_BASE, -jnp.arange(half, dtype=jnp.float32) * 2.0 / r)
    ang = pos.astype(jnp.float32)[:, :, None, None] * inv
    cos, sin = jnp.cos(ang), jnp.sin(ang)
    xf = x.astype(jnp.float32)
    x1, x2 = xf[..., :half], xf[..., half:]
    out = jnp.concatenate([x1 * cos - x2 * sin, x1 * sin + x2 * cos], axis=-1)
    return out.astype(x.dtype)

def alibi_slopes_2(n_heads):
    return jnp.exp2(-8.0 * jnp.arange(1, n_heads + 1, dtype=jnp.float32) / n_heads)

def mla_attention(c_q, c_kv, k_rope, pos, q_norm, w_uq, kv_norm, w_ukv):
    B, S, _ = c_q.shape
    H = MLA_HEADS
    q = (rms_norm_2(c_q, q_norm) @ w_uq).reshape(B, S, H, MLA_NOPE + MLA_ROPE)
    q = jnp.concatenate([q[..., :MLA_NOPE], apply_rope(q[..., MLA_NOPE:], pos)], axis=-1)
    kv = (rms_norm_2(c_kv, kv_norm) @ w_ukv).reshape(B, S, H, MLA_NOPE + MLA_V)
    k_nope, v = kv[..., :MLA_NOPE], kv[..., MLA_NOPE:]
    k_r = apply_rope(k_rope[:, :, None, :], pos)
    k = jnp.concatenate([k_nope, jnp.broadcast_to(k_r, (B, S, H, MLA_ROPE))], axis=-1)
    scale = (MLA_NOPE + MLA_ROPE) ** -0.5
    key_idx = jnp.arange(S)

    def one_block(start):
        qb = lax.dynamic_slice_in_dim(q, start, Q_BLOCK, axis=1)
        s = jnp.einsum('bqhd,bkhd->bhqk', qb, k).astype(jnp.float32) * scale
        q_idx = start + jnp.arange(Q_BLOCK)
        s = jnp.where(key_idx[None, :] <= q_idx[:, None], s, NEG_INF)
        p = jax.nn.softmax(s, axis=-1).astype(v.dtype)
        return jnp.einsum('bhqk,bkhd->bqhd', p, v)

    out = lax.map(one_block, jnp.arange(0, S, Q_BLOCK))
    return jnp.moveaxis(out, 0, 1).reshape(B, S, H * MLA_V)

def moba_attention(q, k, v, pos):
    B, S, H, D = q.shape
    L = MOBA_BLOCK
    NB = -(-S // L)
    pad = NB * L - S
    kp = jnp.pad(k, ((0, 0), (0, pad), (0, 0), (0, 0)))
    vp = jnp.pad(v, ((0, 0), (0, pad), (0, 0), (0, 0)))
    pp = jnp.pad(pos, ((0, 0), (0, pad)))
    k_sel = min(MOBA_TOPK, NB)
    scale = D ** -0.5
    slopes = alibi_slopes_2(H)
    kb = kp.reshape(B, NB, L, H, D)
    k_mean = jnp.mean(kb.astype(jnp.float32), axis=2).astype(k.dtype)
    kb_h = kb.transpose(0, 3, 1, 2, 4)
    vb_h = vp.reshape(B, NB, L, H, D).transpose(0, 3, 1, 2, 4)
    pos_b = pp.reshape(B, NB, L)
    bi = jnp.arange(B)[:, None, None, None]
    hi = jnp.arange(H)[None, :, None, None]

    def one_block(start):
        qb = lax.dynamic_slice_in_dim(q, start, Q_BLOCK, axis=1)
        pq = lax.dynamic_slice_in_dim(pos, start, Q_BLOCK, axis=1)
        own = start // L
        gate = jnp.einsum('bqhd,bnhd->bhqn', qb, k_mean).astype(jnp.float32)
        gate = jnp.where((jnp.arange(NB) < own)[None, None, None, :], gate, NEG_INF)
        _, idx = lax.top_k(gate, k_sel)
        valid = jnp.arange(k_sel) < own
        kg = kb_h[bi, hi, idx]
        vg = vb_h[bi, hi, idx]
        pg = pos_b[bi, idx]
        dist_sel = jnp.abs(pq[:, None, :, None, None] - pg).astype(jnp.float32)
        s_sel = jnp.einsum('bqhd,bhqkld->bhqkl', qb, kg).astype(jnp.float32) * scale
        s_sel = s_sel - slopes[None, :, None, None, None] * dist_sel
        s_sel = jnp.where(valid[None, None, None, :, None], s_sel, NEG_INF)
        k_own = lax.dynamic_slice_in_dim(kp, own * L, L, axis=1)
        v_own = lax.dynamic_slice_in_dim(vp, own * L, L, axis=1)
        p_own_pos = lax.dynamic_slice_in_dim(pp, own * L, L, axis=1)
        dist_own = jnp.abs(pq[:, None, :, None] - p_own_pos[:, None, None, :]).astype(jnp.float32)
        s_own = jnp.einsum('bqhd,blhd->bhql', qb, k_own).astype(jnp.float32) * scale
        s_own = s_own - slopes[None, :, None, None] * dist_own
        causal = (own * L + jnp.arange(L))[None, :] <= (start + jnp.arange(Q_BLOCK))[:, None]
        s_own = jnp.where(causal[None, None], s_own, NEG_INF)
        s = jnp.concatenate([s_sel.reshape(B, H, Q_BLOCK, k_sel * L), s_own], axis=-1)
        p = jax.nn.softmax(s, axis=-1).astype(v.dtype)
        p_sel = p[..., :k_sel * L].reshape(B, H, Q_BLOCK, k_sel, L)
        p_o = p[..., k_sel * L:]
        return (jnp.einsum('bhqkl,bhqkld->bqhd', p_sel, vg)
                + jnp.einsum('bhql,blhd->bqhd', p_o, v_own))

    out = lax.map(one_block, jnp.arange(0, S, Q_BLOCK))
    return jnp.moveaxis(out, 0, 1).reshape(B, S, H * D)

def second_inputs(seed: int = 0) -> dict:
    key = jax.random.key(seed)
    ks = jax.random.split(key, 20)

    def dense(k, fan_in, fan_out):
        return jax.random.normal(k, (DEPTH, fan_in, fan_out), jnp.float32) * fan_in ** -0.5

    def gain(k, n):
        return 1.0 + 0.02 * jax.random.normal(k, (DEPTH, n), jnp.float32)

    x = jax.random.normal(ks[0], (BATCH, SEQ, D_MODEL), jnp.float32)
    positions = jnp.broadcast_to(jnp.arange(SEQ, dtype=jnp.int32)[None, :], (BATCH, SEQ))
    return {
        "x": x,
        "positions": positions,
        "ffn1_norm": gain(ks[1], D_MODEL),
        "ffn1_w_gate": dense(ks[2], D_MODEL, D_FF_2),
        "ffn1_w_up": dense(ks[3], D_MODEL, D_FF_2),
        "ffn1_w_down": dense(ks[4], D_FF_2, D_MODEL),
        "mix_norm": gain(ks[5], D_MODEL),
        "w_in": dense(ks[6], D_MODEL, D_IN_2),
        "mla_q_norm": gain(ks[7], MLA_Q_RANK),
        "mla_w_uq": dense(ks[8], MLA_Q_RANK, MLA_HEADS * (MLA_NOPE + MLA_ROPE)),
        "mla_kv_norm": gain(ks[9], MLA_KV_RANK),
        "mla_w_ukv": dense(ks[10], MLA_KV_RANK, MLA_HEADS * (MLA_NOPE + MLA_V)),
        "w_out": dense(ks[11], D_CAT, D_MODEL),
        "ffn2_norm": gain(ks[12], D_MODEL),
        "ffn2_w_gate": dense(ks[13], D_MODEL, D_FF_2),
        "ffn2_w_up": dense(ks[14], D_MODEL, D_FF_2),
        "ffn2_w_down": dense(ks[15], D_FF_2, D_MODEL),
        "final_norm": 1.0 + 0.02 * jax.random.normal(ks[16], (D_MODEL,), jnp.float32),
    }

def second_block(x, positions, ffn1_norm, ffn1_w_gate, ffn1_w_up, ffn1_w_down, mix_norm, w_in,
              mla_q_norm, mla_w_uq, mla_kv_norm, mla_w_ukv, w_out, ffn2_norm, ffn2_w_gate,
              ffn2_w_up, ffn2_w_down, final_norm):
    B, S, _ = x.shape
    cuts = np.cumsum(IN_SPLITS_2)[:-1].tolist()
    for l in range(DEPTH):
        x = x + FFN_RES * swiglu(rms_norm_2(x, ffn1_norm[l]), ffn1_w_gate[l], ffn1_w_up[l], ffn1_w_down[l])
        u = rms_norm_2(x, mix_norm[l]) @ w_in[l]
        c_q, c_kv, k_rope, mq, mk, mv = jnp.split(u, cuts, axis=-1)
        a_out = mla_attention(c_q, c_kv, k_rope, positions, mla_q_norm[l], mla_w_uq[l],
                              mla_kv_norm[l], mla_w_ukv[l])
        shp = (B, S, MOBA_HEADS, MOBA_HEAD_DIM)
        b_out = moba_attention(mq.reshape(shp), mk.reshape(shp), mv.reshape(shp), positions)
        x = x + jnp.concatenate([a_out, b_out], axis=-1) @ w_out[l]
        x = x + FFN_RES * swiglu(rms_norm_2(x, ffn2_norm[l]), ffn2_w_gate[l], ffn2_w_up[l], ffn2_w_down[l])
    return rms_norm_2(x, final_norm)


def setup_inputs(seed=0):
    out = dict(first_inputs(seed))
    for name, value in second_inputs(seed + 1).items():
        if name != "x":
            out[name + "_2"] = value
    return out


def reference(
    x, p, g_mix, w_in, lam_q1, lam_k1, lam_q2, lam_k2, g_diff_sub, g_ret_sub, w_branch_diff,
    w_branch_ret, w_out, g_mlp, w_ff1, w_ff2, g_ple, w_ple_gate, w_ple, g_final, positions_2,
    ffn1_norm_2, ffn1_w_gate_2, ffn1_w_up_2, ffn1_w_down_2, mix_norm_2, w_in_2, mla_q_norm_2,
    mla_w_uq_2, mla_kv_norm_2, mla_w_ukv_2, w_out_2, ffn2_norm_2, ffn2_w_gate_2, ffn2_w_up_2,
    ffn2_w_down_2, final_norm_2,
):
    x = first_block(
        x, p, g_mix, w_in, lam_q1, lam_k1, lam_q2, lam_k2, g_diff_sub, g_ret_sub, w_branch_diff,
        w_branch_ret, w_out, g_mlp, w_ff1, w_ff2, g_ple, w_ple_gate, w_ple, g_final,
    )
    return second_block(
        x, positions_2, ffn1_norm_2, ffn1_w_gate_2, ffn1_w_up_2, ffn1_w_down_2, mix_norm_2,
        w_in_2, mla_q_norm_2, mla_w_uq_2, mla_kv_norm_2, mla_w_ukv_2, w_out_2, ffn2_norm_2,
        ffn2_w_gate_2, ffn2_w_up_2, ffn2_w_down_2, final_norm_2,
    )


_drawn_inputs = setup_inputs


def setup_inputs(seed=0):
    import zlib

    import numpy as np

    out = dict(_drawn_inputs(seed))
    spreads = {}
    factors = {'g_mix': 2.747,
     'lam_k1': 4.012,
     'lam_q2': 4.191,
     'g_diff_sub': 6.138,
     'g_ret_sub': 8.0,
     'g_mlp': 3.106,
     'g_ple': 200.0,
     'ffn1_norm_2': 6.52,
     'mix_norm_2': 6.453,
     'mla_q_norm_2': 8.0,
     'mla_kv_norm_2': 8.0,
     'ffn2_norm_2': 7.572,
     'final_norm_2': 20.45}
    for name, (base, spread) in spreads.items():
        noise = np.random.default_rng([zlib.crc32(name.encode()), seed]).standard_normal(out[name].shape)
        drawn = base * np.exp(spread * noise) if base else spread * noise
        out[name] = __import__('jax').numpy.asarray(drawn.astype(out[name].dtype))
    for name, factor in factors.items():
        out[name] = (out[name] * factor).astype(out[name].dtype)
    return out
```

```python
import math
from contextlib import ExitStack

import numpy as np
import concourse.bass as bass
from concourse import mybir

P = 128
D, TB, SEQ = 1024, 2, 256
KT = D // P
EPS = 1e-6
BIG = 1e30
SLOTS = 3
UNIT = 2048
HALF = 512

DH, DHD = 8, 64
RH, RK, RV = 4, 128, 256
DFF = 4096
LAM_INIT = 0.8 - 0.6 * math.exp(-0.3 * 0)
IN_CB = 16
FF2 = 2816
SUB = 256
MH, NOPE, ROPE, MV = 8, 64, 32, 64
QR, KVR = 384, 256
BH, BD = 8, 64
MQ = NOPE + ROPE

UNITS = [("in", 32), ("bd", 4), ("br", 4), ("out", 4), ("ff", 32), ("pl", 1), ("pg", 4),
         ("f1", 33), ("in2", 10), ("uq", 2), ("ukv", 1), ("o2", 4), ("f2", 33)]
U0, _n = {}, 0
for _name, _count in UNITS:
    U0[_name] = _n
    _n += _count
N_UNITS = _n

IN2 = [(QR + KVR + ROPE, 512), (QR + KVR + ROPE + 512, 512), (QR + KVR + ROPE + 1024, 512),
       (0, QR), (QR, KVR + ROPE)]
CB_IN2, CB_UQ, CB_UKV = IN_CB, IN_CB + len(IN2), IN_CB + len(IN2) + 2

ACC = {name: n for n, name in enumerate(["bd", "br", "out", "ff", "pg", "f1", "o2", "f2"])}
NORMS = ["mix", "mlp", "ple", "mid", "ffn1", "mix2", "ffn2", "final"]
NORM_X = {"mlp": "out", "ple": "ff", "mid": "pg", "mix2": "f1", "ffn2": "o2", "final": "f2"}


def unit_width(u):
    if U0["in2"] + 6 <= u < U0["in2"] + 8:
        return 4 * QR
    if U0["in2"] + 8 <= u < U0["uq"]:
        return 4 * (KVR + ROPE)
    if U0["uq"] <= u < U0["ukv"]:
        return 3 * QR
    return UNIT


def work_batches():
    order = [("mix", 0, 0), ("mix", 0, 1), ("mix", 1, 0), ("mix", 1, 1), ("p",)]
    for k in range(IN_CB):
        if 6 <= k < 14:
            order += [("a", k - 6), ("v", k - 6)]
        if 12 <= k:
            order += [("rv", k - 12)]
        if k in (1, 2, 3, 4, 7, 8):
            order += [("qk", k - 1, tb) for tb in range(TB)]
    order += [("ya", tb, h) for tb in range(TB) for h in range(2)]
    order += [("yr", tb, h) for tb in range(TB) for h in range(2)]
    order += [("m", tb, h) for tb in range(TB) for h in range(2)]
    order += [("mlp", tb, h) for tb in range(TB) for h in range(2)]
    order += [("ff", i, tb) for i in range(DFF // HALF) for tb in range(TB)]
    order += [("ple", tb, h) for tb in range(TB) for h in range(2)]
    order += [("ffn1", tb, h) for tb in range(TB) for h in range(2)]
    order += [("f1", i, tb) for i in range(FF2 // SUB) for tb in range(TB)]
    order += [("mix2", tb, h) for tb in range(TB) for h in range(2)]
    order += [("mq", tb) for tb in range(TB)] + [("mk", tb) for tb in range(TB)]
    order += pair_batches("b", 0) + pair_batches("b", 1)
    order += [("cq", 0), ("cq", 1), ("ckv",)]
    order += pair_batches("b", 2) + pair_batches("b", 3)
    order += [("q", j) for j in range(MH // 2)] + [("k", j) for j in range(MH // 2)]
    for j in range(MH // 2):
        order += pair_batches("l", j)
    order += [("cat", tb, h) for tb in range(TB) for h in range(2)]
    order += [("ffn2", tb, h) for tb in range(TB) for h in range(2)]
    order += [("f2", i, tb) for i in range(FF2 // SUB) for tb in range(TB)]
    return {name: n for n, name in enumerate(order)}


def pair_batches(kind, j):
    return [(kind + "a", 2 * j), (kind + "a", 2 * j + 1), (kind + "v", 2 * j), (kind + "v", 2 * j + 1)]


def score_maps():
    order = [("d", 0, 0), ("d", 0, 1)]
    for k in range(6, IN_CB):
        if k - 5 < DH:
            order += [("d", k - 5, 0), ("d", k - 5, 1)]
        if 11 <= k < 15:
            order += [("r", k - 11)]
    order += [("b", h) for h in range(BH)] + [("l", h) for h in range(MH)]
    return {name: n for n, name in enumerate(order)}


WB, SM = work_batches(), score_maps()
SRC = {name: 2 * n for n, name in enumerate(["mix", "ya", "m", "mlp", "ple", "ffn1", "mix2", "ffn2", "final"])}
GAIN = {name: 16 * n for n, name in enumerate(["mix", "ret", "mlp", "ple", "mid", "ffn1", "mix2"], 1)}
GAIN |= {"c": GAIN["mix2"] + 32, "ffn2": GAIN["mix2"] + 48, "final": GAIN["mix2"] + 64}
SOFT = {("d", h, c): 2 * h + c for h in range(DH) for c in range(2)}
SOFT.update({("b", h): 2 * DH + h for h in range(BH)})
SOFT.update({("l", h): 2 * DH + BH + h for h in range(MH)})
SPLIT = {name: n for n, name in enumerate(
    [x for x in WB if x[0] in ("p", "ya", "yr", "m", "ff", "f1", "f2", "cq", "ckv", "cat", *NORMS)])}


def alibi(h):
    return 2.0 ** (-8.0 * (h + 1) / 8)


def two_blocks(nc, x_d, p_d, g_mix, w_in, lam_q1, lam_k1, lam_q2, lam_k2, g_diff, g_ret, w_bd, w_br, w_out,
               g_mlp, w_ff1, w_ff2, g_ple, w_pg, w_pl, g_fin1, pos_d, g_ffn1, w_g1, w_u1, w_d1, g_mix2,
               w_in2, g_q, w_uq, g_kv, w_ukv, w_out2, g_ffn2, w_g2, w_u2, w_d2, g_final,
               masks_d, decay_d, freq_d, out_d):
    f32, f32r, bf16, i32 = mybir.dt.float32, mybir.dt.float32r, mybir.dt.bfloat16, mybir.dt.int32
    ALU, ACT, AX = mybir.AluOpType, mybir.ActivationFunctionType, mybir.AxisListType

    at = [-(-nc.sbuf_base // 128) * 128]
    named = {}

    def sb(name, shape, dt=f32, where=None):
        size = (2 if dt == bf16 else 4) * int(np.prod(shape[1:]))
        if where is None:
            where = at[0]
            at[0] += -(-size // 32) * 32
        named[name] = where
        return nc.alloc_sbuf_tensor_at(name, shape, dt, offset=where)

    raw = [sb(f"raw{s}", [P, UNIT]) for s in range(SLOTS)]
    w_hi = [sb(f"w_hi{s}", [P, UNIT], f32r) for s in range(SLOTS)]
    w_lo = [sb(f"w_lo{s}", [P, UNIT], f32r) for s in range(SLOTS)]
    hA = [sb(f"hA_{s}", [P, KT, SEQ], f32r) for s in ("hi", "lo")]
    hB = [sb(f"hB_{s}", [P, KT, SEQ], f32r) for s in ("hi", "lo")]
    x = sb("x", [P, TB, D])
    src = sb("src", [P, TB, D])
    gain = sb("gain", [P, D])
    junk = sb("junk", [P, D], bf16)
    vjunk = sb("vjunk", [P, P], bf16)
    masks = sb("masks", [P, P + 2 * 384])
    ident, mask, negdist = masks[:, 0:P], masks[:, P:P + 384], masks[:, P + 384:P + 768]
    ss = sb("ss", [P, 2 * len(NORMS)])
    rs = sb("rs", [P, 2 * len(NORMS)])
    ms = sb("ms", [P, 2 * len(NORMS)])
    nhalf = sb("nhalf", [P, 16])
    lam_v = sb("lam_v", [P, 4, DHD])
    lam_w = sb("lam_w", [P, 2, DHD])
    rjunk = sb("rjunk", [P, RV], bf16, named["lam_w"])
    lam_s = sb("lam_s", [P, 4])
    neglam = sb("neglam", [P, 1])
    ssy, msy, rsy = (sb(n, [P, TB * DH]) for n in ("ssy", "msy", "rsy"))
    ssr, msr, rsr = (sb(n, [P, TB * RH]) for n in ("ssr", "msr", "rsr"))
    ssc, msc, rsc = (sb(n, [P, 4]) for n in ("ssc", "msc", "rsc"))
    mn = sb("mn", [P, 32, TB])
    sm = sb("sm", [P, 32, TB])
    rsm = sb("rsm", [P, 32, TB])
    qc = sb("qc", [P, DH, TB])
    gd = sb("gd", [P, P])
    pT = [sb(f"pT_{s}", [P, 2, SEQ], f32r) for s in ("hi", "lo")]
    arena = at[0]

    def lay(start, *parts):
        out = []
        for name, shape, *dt in parts:
            out.append(sb(name, shape, dt[0] if dt else f32, start))
            start += -(-4 * int(np.prod(shape[1:])) // 32) * 32
        assert start <= nc.sbuf_usable_end, (name, start)
        return out

    qaT, kaT, va, qrT, krT, vr, gr, ga, yr, p_sb, decay0, decay1, sT0 = lay(
        arena, ("qaT", [P, DH, SEQ]), ("kaT", [P, DH, SEQ]), ("va", [P, TB, D]), ("qrT", [P, RH, SEQ]),
        ("krT", [P, RH, SEQ]), ("vr", [P, TB, D]), ("gr", [P, TB, D]), ("ga", [P, TB, D]),
        ("yr", [P, TB, D]), ("p_sb", [P, TB, 256]), ("decay0", [P, 384]), ("decay1", [P, 384]),
        ("sT0", [P, 384]))
    (gg,) = lay(arena, ("gg", [P, TB, D]))
    qk_tm = lay(named["yr"], ("qk_tm0", [P, TB, HALF]), ("qk_tm1", [P, TB, HALF]))
    (sT1,) = lay(named["p_sb"], ("sT1", [P, 384]))
    decay, sT = [decay0, decay1], [sT0, sT1]
    L, aT0, aT1, bias0, bias1 = lay(named["hB_hi"], ("L", [P, 4, 384]), ("aT0", [P, 384]), ("aT1", [P, 384]),
                                    ("bias0", [P, 384]), ("bias1", [P, 384]))
    aT, bias = [aT0, aT1], [bias0, bias1]
    fT0, fT1, act_r, act_f, pl_s, sg = lay(
        arena, ("fT_hi", [P, 4, SEQ], f32r), ("fT_lo", [P, 4, SEQ], f32r), ("act_r", [P, TB, HALF]),
        ("act_f", [P, TB, HALF]), ("pl_s", [P, TB, D]), ("sg", [P, TB, D]))
    fT = [fT0, fT1]
    (mix_t,) = lay(named["va"], ("mix_t", [P, TB, D]))
    (mq_tm, mk_tm, mv, mqT, mkT, cq, ckv, q_tm, k_tm, v_tm, qT, kT, pos_k, posdist, kr) = lay(
        arena, ("mq_tm", [P, TB, 512]), ("mk_tm", [P, TB, 512]), ("mv", [P, TB, 512]), ("mqT", [P, 4, SEQ]),
        ("mkT", [P, 4, SEQ]), ("cq", [P, TB, QR]), ("ckv", [P, TB, KVR + ROPE]),
        ("q_tm", [P, TB, MH, MQ]), ("k_tm", [P, TB, MH, MQ]), ("v_tm", [P, TB, MH, MV]),
        ("qT", [MQ, MH, SEQ]), ("kT", [MQ, MH, SEQ]), ("pos_k", [P, SEQ]), ("posdist", [P, 384]),
        ("kr", [P, TB, ROPE]))
    (rope_t, rot_t) = lay(named["kr"] + 4 * TB * ROPE, ("rope_t", [P, TB, ROPE]), ("rot_t", [P, TB, MH, ROPE]))
    cos2, sin2, ang, turns_ = lay(named["rot_t"] + 4 * TB * MH * ROPE, ("cos2", [P, TB, ROPE]), ("sin2", [P, TB, ROPE]),
                                  ("ang", [P, TB, 16]), ("turns_", [P, TB, 16]))
    pos_ki, pos_qi, pos_q, freq = lay(named["turns_"] + 4 * TB * 16, ("pos_ki", [P, SEQ], i32), ("pos_qi", [P, TB], i32),
                                      ("pos_q", [P, TB]), ("freq", [P, 16]))

    ctx = ExitStack()
    bank = [ctx.enter_context(nc.psum_tensor(f"bank{i}", [P, HALF], f32)) for i in range(8)]
    acc = lambda tb, c: bank[2 * tb + c]
    proj = lambda cb, tb: bank[2 * (cb % 2) + tb]
    up = lambda tb: bank[4 + tb]
    score = lambda name: bank[4 + SM[name] % 2]
    work = lambda name: bank[6 + WB[name] % 2]

    sems = {}

    def sem(name):
        sems[name] = ctx.enter_context(nc.semaphore(name))
        return sems[name]

    raw_in = [sem(f"raw_in{s}") for s in range(SLOTS)]
    hi_ready = sem("hi_ready")
    lo_ready = sem("lo_ready")
    unit_used = sem("unit_used")
    x_in = [sem("x_in0"), sem("x_in1")]
    p_in, mask_in, lam_in, gd_in = (sem(n) for n in ("p_in", "mask_in", "lam_in", "gd_in"))
    gain_in = sem("gain_in")
    decay_in, pos_in = [sem("decay_in0"), sem("decay_in1")], sem("pos_in")
    square_sum = sem("square_sum")
    rstd_ready = sem("rstd_ready")
    mid_ready = sem("mid_ready")
    src_ready = sem("src_ready")
    work_done = sem("work_done")
    work_out = [sem("work_out0"), sem("work_out1")]
    split_hi = sem("split_hi")
    proj_done, proj_out = sem("proj_done"), sem("proj_out")
    acc_done, acc_out = sem("acc_done"), sem("acc_out")
    up_done, act_ready, up_out = sem("up_done"), sem("act_ready"), sem("up_out")
    score_done, score_out = sem("score_done"), sem("score_out")
    bias_ready = sem("bias_ready")
    exp_ready = sem("exp_ready")
    comb_ready = sem("comb_ready")
    ysq, rsq = sem("ysq"), sem("rsq")
    ystd, rstd_r, cstd = sem("ystd"), sem("rstd_r"), sem("cstd")
    gates_ready = sem("gates_ready")
    gsg_ready = sem("gsg_ready")
    yr_src = sem("yr_src")
    lam_prod, lam_exp, lam_ready = sem("lam_prod"), sem("lam_exp"), sem("lam_ready")
    pl_done, pl_out, pg_sig = sem("pl_done"), sem("pl_out"), sem("pg_sig")
    csq, c_src = sem("csq"), sem("c_src")
    pos_ready, ang_ready, trig_ready = sem("pos_ready"), sem("ang_ready"), sem("trig_ready")
    rsm_ready = sem("rsm_ready")
    rot_ready, kr_ready = sem("rot_ready"), sem("kr_ready")
    k_full = sem("k_full")
    vec_step, act_step, pool_step = sem("vec_step"), sem("act_step"), sem("pool_step")
    out_done = sem("out_done")

    def unit_view(buf, n, cols):
        return buf[:, 0:n * cols].rearrange("p (t n) -> p t n", n=cols)

    block = ctx.enter_context(nc.Block())

    @block.sync
    def _(sp):
        def load(u, pieces, turns=0):
            if u >= SLOTS:
                sp.wait_ge(lo_ready, u - SLOTS + 1 + SLOTS * turns)
            for dst, w in pieces:
                sp.dma_start(dst, w).then_inc(raw_in[u % SLOTS], 16)

        def narrow(u, w, kt0, n, c0, cols, turns=0):
            view = unit_view(raw[u % SLOTS], n, cols)
            h = -(-n // 2)
            load(u, [(view[:, a:b, :], w[(kt0 + a) * P:(kt0 + b) * P, bass.ds(c0, cols)]
                      .rearrange("(t p) n -> p t n", p=P)) for a, b in ((0, h), (h, n))], turns)

        def wide(u, w, row0, turns=0):
            view = unit_view(raw[u % SLOTS], 2, D)
            load(u, [(view[:, j, :], w[bass.ds(row0 + j * P, P), :]) for j in range(2)], turns)

        def gate_up(u, w_g, w_u, kt0, c0, turns=0):
            view = unit_view(raw[u % SLOTS], 4, 2 * SUB)
            load(u, [(view[:, :, s * SUB:(s + 1) * SUB], w[kt0 * P:(kt0 + 4) * P, bass.ds(c0, SUB)]
                      .rearrange("(t p) n -> p t n", p=P)) for s, w in enumerate((w_g, w_u))], turns)

        for tb in range(TB):
            sp.dma_start(x[:, tb, :], x_d[tb * P:(tb + 1) * P, :]).then_inc(x_in[tb], 16)
        for cb in range(IN_CB):
            for j in range(2):
                narrow(U0["in"] + 2 * cb + j, w_in, 4 * j, 4, cb * HALF, HALF)
        for name, w in (("bd", w_bd), ("br", w_br), ("out", w_out)):
            for j in range(4):
                wide(U0[name] + j, w, 2 * j * P)

        u = U0["ff"]
        for j in range(2):
            narrow(u + j, w_ff1, 4 * j, 4, 0, HALF)

        def ff_step(u, i, turns=0):
            for j in range(2):
                narrow(u + j, w_ff1, 4 * j, 4, i * HALF, HALF, turns)
            for j in range(2):
                wide(u + 2 + j, w_ff2, i * HALF - HALF + 2 * j * P, turns)
        ff_step(u + 2, 1)
        with sp.Fori(0, 2) as r:
            for j in range(3):
                ff_step(u + 6 + 4 * j, 3 * r + 2 + j, 4 * r)
        for j in range(2):
            wide(u + 30 + j, w_ff2, DFF - HALF + 2 * j * P)

        wide(U0["pl"], w_pl, 0)
        for j in range(4):
            wide(U0["pg"] + j, w_pg, 2 * j * P)

        def gated(u, w_g, w_u, w_d):
            for j in range(2):
                gate_up(u + j, w_g, w_u, 4 * j, 0)
            with sp.Fori(0, FF2 // SUB - 1) as i:
                for j in range(2):
                    gate_up(u + 2 + j, w_g, w_u, 4 * j, i * SUB + SUB, i)
                wide(u + 4, w_d, i * SUB, i)
            wide(u + 32, w_d, FF2 - SUB)

        gated(U0["f1"], w_g1, w_u1, w_d1)
        for n, (c0, cols) in enumerate(IN2):
            for j in range(2):
                narrow(U0["in2"] + 2 * n + j, w_in2, 4 * j, 4, c0, cols)
        for j in range(2):
            narrow(U0["uq"] + j, w_uq, 0, 3, j * QR, QR)
        wide(U0["ukv"], w_ukv, 0)
        for j in range(4):
            wide(U0["o2"] + j, w_out2, 2 * j * P)
        gated(U0["f2"], w_g2, w_u2, w_d2)

        for tb in range(TB):
            sp.wait_ge(src_ready, SRC["final"] + tb + 1)
            sp.dma_start(out_d[tb * P:(tb + 1) * P, :], src[:, tb, :]).then_inc(out_done, 16)
        sp.wait_ge(out_done, 16 * TB)

    def rows_of(name):
        kind, b = name[0], work(name)
        if kind == "p":
            return [t[:, :, :] for t in pT], b[:, :].rearrange("p (k t) -> p k t", t=SEQ)
        if kind == "ckv":
            return [t[:, 3:5, :] for t in hA], b[:, :].rearrange("p (k t) -> p k t", t=SEQ)
        if kind in ("ff", "f1", "f2"):
            tb, k0, n, pair = name[2], 0, 4 if kind == "ff" else 2, fT
        elif kind == "cq":
            tb, k0, n, pair = name[1], 0, 3, hA
        else:
            tb, k0, n, pair = name[1], 4 * name[2], 4, hB if kind in ("ya", "m", "ple", "cat") else hA
        return ([t[:, k0:k0 + n, tb * P:(tb + 1) * P] for t in pair],
                b[:, 0:n * P].rearrange("p (k t) -> p k t", t=P))

    @block.tensor
    def _(pe):
        def product(outs, h, kt, tb, u, col):
            hi, lo = (t[:, kt, tb * P:(tb + 1) * P] for t in h)
            spans = [(o, slice(col + n * HALF, col + n * HALF + o.shape[-1])) for n, o in enumerate(outs)]
            return [(o, x_part, w[u % SLOTS][:, c]) for x_part, w in ((hi, w_hi), (hi, w_lo), (lo, w_hi))
                    for o, c in spans]

        def products(outs, h, kt0, n, tb, u, cols, first, last, du=0):
            pe.wait_ge(lo_ready, u + 1 + du)
            for t in range(n):
                todo = product(outs, h, kt0 + t, tb, u, t * cols)
                for m, (o, a, w) in enumerate(todo):
                    mm = pe.matmul(o, a, w, start=first and t == 0 and m < len(outs),
                                   stop=last and t == n - 1 and m >= len(todo) - len(outs))
            return mm

        def work_free(n, dw=0):
            if n >= 2:
                pe.wait_ge(work_out[n % 2], n // 2 + dw)

        def turn(name, blocks, dw=0):
            work_free(WB[name], dw)
            col = 0
            for blk in blocks:
                rows, cols = blk.shape[0], blk.shape[-1]
                mm = pe.transpose(work(name)[0:cols, col:col + rows], blk, ident)
                col += rows
            mm.then_inc(work_done, 1)

        def turned(name, dw=0):
            n = WB[name]
            pe.wait_ge(work_out[n % 2], n // 2 + 1 + dw)

        def turn_rows(name, buf, tb):
            for h in range(2):
                turn((name, tb, h), [buf[:, tb, (4 * h + j) * P:(4 * h + j + 1) * P] for j in range(4)])

        def turned_rows(name, tb):
            for h in range(2):
                turned((name, tb, h))

        def src_turn(name, tb):
            pe.wait_ge(src_ready, SRC[name] + tb + 1)
            turn_rows(name, src, tb)

        def scores(name, q, k, h):
            m, b = SM[name], score(name)
            if m >= 2:
                pe.wait_ge(score_out, m - 1)
            pe.matmul(b[:, 0:P], q[:, h, 0:P], k[:, h, 0:P], start=True, stop=True)
            pe.matmul(b[:, P:384], q[:, h, P:SEQ], k[:, h, :], start=True, stop=True).then_inc(score_done, 1)

        def diff_scores(h):
            for c in range(2):
                half = slice(c * DHD, (c + 1) * DHD)
                scores(("d", h, c), qaT[half], kaT[half], h)

        def apply_weights(name, a, v, cols):
            b = work(name)
            work_free(WB[name])
            pe.matmul(b[:, 0:cols], a[:, 0:P], v[0], start=True, stop=True)
            pe.matmul(b[:, cols:2 * cols], a[:, P:2 * P], v[0], start=True, stop=False)
            pe.matmul(b[:, cols:2 * cols], a[:, 2 * P:384], v[1], start=False, stop=True).then_inc(work_done, 1)

        def diff_turn(h):
            pe.wait_ge(comb_ready, h + 1)
            w = L[:, SOFT["d", h, 1] % 4, :]
            turn(("a", h), [w[:, j * P:(j + 1) * P] for j in range(3)])

        def diff_out(h):
            pe.wait_ge(proj_out, 12)
            turned(("a", h))
            apply_weights(("v", h), aT[h % 2], [va[:, tb, h * P:(h + 1) * P] for tb in range(TB)], P)

        def ret_scores(h):
            if h == 0:
                turned(("qk", 6, 1))
                turned(("qk", 7, 1))
            pe.wait_ge(score_out, SM["r", h] - 1)
            b = score(("r", h))
            pe.matmul(b[:, 0:SEQ], krT[:, h, 0:P], qrT[:, h, :], start=True, stop=True)
            pe.matmul(b[:, SEQ:384], krT[:, h, P:SEQ], qrT[:, h, P:SEQ], start=True, stop=True)\
              .then_inc(score_done, 1)

        def ret_out(h):
            pe.wait_ge(score_out, SM["r", h] + 1)
            pe.wait_ge(proj_out, 20)
            apply_weights(("rv", h), sT[h % 2], [vr[:, tb, h * RV:(h + 1) * RV] for tb in range(TB)], RV)

        pe.wait_ge(mask_in, 16)
        for cb in range(IN_CB):
            u = U0["in"] + 2 * cb
            if cb >= 2:
                pe.wait_ge(proj_out, 2 * cb - 2)
            if cb == 0:
                for tb in range(TB):
                    src_turn("mix", tb)
                    turned_rows("mix", tb)
                    for j in range(2):
                        mm = products([proj(cb, tb)[:, :]], hA, 4 * j, 4, tb, u + j, HALF, j == 0, j == 1)
                        if tb:
                            mm.then_inc(unit_used, 1)
                    if tb == 0:
                        mm.then_inc(proj_done, 1)
                pe.wait_ge(p_in, 16)
                turn(("p",), [p_sb[:, tb, k * P:(k + 1) * P] for k in range(2) for tb in range(TB)])
            else:
                for j in range(2):
                    for tb in range(TB):
                        mm = products([proj(cb, tb)[:, :]], hA, 4 * j, 4, tb, u + j, HALF, j == 0, j == 1)
                        if j and tb == 0:
                            mm.then_inc(proj_done, 1)
                    mm.then_inc(unit_used, 1)
            if cb == 5:
                turned(("qk", 3, 0))
                turned(("qk", 3, 1))
                diff_scores(0)
            if 6 <= cb < 14:
                diff_turn(cb - 6)
                if cb < 13:
                    diff_scores(cb - 5)
                diff_out(cb - 6)
            if cb >= 12:
                ret_out(cb - 12)
            if 11 <= cb < 15:
                ret_scores(cb - 11)
            if cb in (1, 2, 3, 4, 7, 8):
                pe.wait_ge(proj_out, 2 * cb)
                for tb in range(TB):
                    turn(("qk", cb - 1, tb),
                         [qk_tm[(cb - 1) % 2][:, tb, j * P:(j + 1) * P] for j in range(4)])

        def acc_free(name, tb):
            if n := 2 * ACC[name]:
                pe.wait_ge(acc_out, n - 1 + tb)

        def unit(h, u0, j, tb):
            return products([acc(tb, c)[:, :] for c in range(2)], h, 2 * j, 2, tb, u0 + j, D, j == 0, j == 3)

        def branch(name, h, u0, before, after):
            for tb in range(TB):
                before(tb)
                mm = unit(h, u0, 0, tb)
            mm.then_inc(unit_used, 1)
            for tb in range(TB):
                for j in (1, 2, 3):
                    mm = unit(h, u0, j, tb)
                    if tb:
                        mm.then_inc(unit_used, 1)
                if tb == 0:
                    mm.then_inc(acc_done, 1)
                after(tb)

        def output(name, h, u0, before):
            for tb in range(TB):
                before(tb)
                acc_free(name, tb)
                for j in (0, 1, 2):
                    mm = unit(h, u0, j, tb)
                    if tb:
                        mm.then_inc(unit_used, 1)
            for tb in range(TB):
                mm = unit(h, u0, 3, tb)
                mm.then_inc(unit_used if tb else acc_done, 1)

        def before_bd(tb):
            src_turn("ya", tb)
            turned_rows("ya", tb)

        def after_bd(tb):
            pe.wait_ge(yr_src, tb + 1)
            turn_rows("yr", yr, tb)

        def before_br(tb):
            acc_free("br", tb)
            turned_rows("yr", tb)

        def before_src(name):
            def before(tb):
                src_turn(name, tb)
                turned_rows(name, tb)
            return before

        pe.wait_ge(proj_out, 2 * IN_CB)
        branch("bd", hB, U0["bd"], before_bd, after_bd)
        branch("br", hA, U0["br"], before_br, lambda tb: None)
        output("out", hB, U0["out"], before_src("m"))

        def ff_up0(u0, name, norm):
            for tb in range(TB):
                src_turn(norm, tb)
                turned_rows(norm, tb)
                for j in range(2):
                    mm = products([up(tb)[:, :]], hA, 4 * j, 4, tb, u0 + j, HALF, j == 0, j == 1)
                    if tb:
                        mm.then_inc(unit_used, 1)
                if tb == 0:
                    mm.then_inc(up_done, 1)

        def ff_turn(name, i, done, cols, di=0):
            for tb in range(TB):
                pe.wait_ge(up_out, done - 1 + tb + 2 * di)
                turn((name, i, tb), [act_f[:, tb, j * P:(j + 1) * P] for j in range(cols // P)], di)

        def ff_up(u, name, i, steps, cols, du=0, di=0):
            pe.wait_ge(up_out, 2 * steps + 2 * di)
            for j in range(2):
                for tb in range(TB):
                    mm = products([up(tb)[:, :]], hA, 4 * j, 4, tb, u + j, HALF, j == 0, j == 1, du)
                    if j and tb == 0:
                        mm.then_inc(up_done, 1)
                mm.then_inc(unit_used, 1)
                if j == 0:
                    ff_turn(name, i - 1, 2 * steps, cols, di)

        u = U0["ff"]
        ff_up0(u, "ff", "mlp")

        def relu_step(i, r=0, start=False):
            v = U0["ff"] + 2 + 4 * (i - 1)
            ff_up(v, "ff", i, i, HALF, 12 * r, 3 * r)
            for j in range(2):
                for tb in range(TB):
                    if j == 0:
                        turned(("ff", i - 1, tb), 3 * r)
                    if start and j == 0:
                        acc_free("ff", tb)
                    mm = products([acc(tb, c)[:, :] for c in range(2)], fT, 2 * j, 2, tb, v + 2 + j, D,
                                  start and j == 0, False, 12 * r)
                mm.then_inc(unit_used, 1)
        relu_step(1, start=True)
        with pe.Fori(0, 2) as r:
            for j in range(3):
                relu_step(2 + j, r)
        last = DFF // HALF - 1
        ff_turn("ff", last, 2 * (last + 1), HALF)
        for tb in range(TB):
            turned(("ff", last, tb))
            for j in range(2):
                mm = products([acc(tb, c)[:, :] for c in range(2)], fT, 2 * j, 2, tb, u + 30 + j, D, False, j == 1)
                if tb:
                    mm.then_inc(unit_used, 1)
            if tb == 0:
                mm.then_inc(acc_done, 1)

        for tb in range(TB):
            if tb:
                pe.wait_ge(acc_out, 2 * ACC["ff"] + 1)
            turned(("p",))
            outs = [bank[(4, 0)[tb] + c][:, :] for c in range(2)]
            mm = products(outs, pT, 0, 2, tb, U0["pl"], D, True, True)
            mm.then_inc(unit_used if tb else pl_done, 1)

        def before_pg(tb):
            src_turn("ple", tb)
            turned_rows("ple", tb)
            pe.wait_ge(pl_out, 2)
        output("pg", hB, U0["pg"], before_pg)

        def gated(name, norm, base):
            u, n = U0[name], FF2 // SUB
            ff_up0(u, name, norm)

            def down(v, i, tb, r=0, first=False, last=False):
                turned((name, i, tb), r)
                return products([acc(tb, c)[:, :] for c in range(2)], fT, 0, 2, tb, v, D, first, last, 3 * r)

            def step(i, r=0):
                v = u + 2 + 3 * (i - 1)
                ff_up(v, name, i, base + i, SUB, 3 * r, r)
                for tb in range(TB):
                    if i == 1:
                        acc_free(name, tb)
                    mm = down(v + 2, i - 1, tb, r, i == 1)
                    if i == n - 1 and tb == 0:
                        ff_turn(name, i, 2 * (base + n), SUB)
                mm.then_inc(unit_used, 1)
            step(1)
            with pe.Fori(0, n - 3) as r:
                step(2, r)
            step(n - 1)
            down(u + 32, n - 1, 0, last=True).then_inc(acc_done, 1)
            down(u + 32, n - 1, 1, last=True).then_inc(unit_used, 1)

        gated("f1", "ffn1", DFF // HALF)

        def pair_scores(kind, j):
            for h in (2 * j, 2 * j + 1):
                if kind == "b":
                    half = slice(h % 2 * BD, h % 2 * BD + BD)
                    scores(("b", h), mqT[half], mkT[half], h // 2)
                else:
                    scores(("l", h), qT, kT, h)

        def pair(kind, j):
            for h in (2 * j, 2 * j + 1):
                m = SOFT[kind, h]
                pe.wait_ge(exp_ready, m + 1)
                turn((kind + "a", h), [L[:, m % 4, b * P:(b + 1) * P] for b in range(3)])
            if 2 * j + 2 < BH:
                pair_scores(kind, j + 1)
            for h in (2 * j, 2 * j + 1):
                turned((kind + "a", h))
                v = [mv[:, tb, h * BD:(h + 1) * BD] if kind == "b" else v_tm[:, tb, h, :] for tb in range(TB)]
                apply_weights((kind + "v", h), aT[h % 2], v, BD)

        for n, (_, cols) in enumerate(IN2):
            cb, u = CB_IN2 + n, U0["in2"] + 2 * n
            if n >= 2:
                pe.wait_ge(proj_out, 2 * cb - 2)
            if n == 0:
                for tb in range(TB):
                    src_turn("mix2", tb)
                    turned_rows("mix2", tb)
                    pe.wait_ge(acc_out, 2 * ACC["f1"] + 1 + tb)
                    for j in range(2):
                        mm = products([proj(cb, tb)[:, 0:cols]], hA, 4 * j, 4, tb, u + j, cols, j == 0, j == 1)
                        if tb:
                            mm.then_inc(unit_used, 1)
                    if tb == 0:
                        mm.then_inc(proj_done, 1)
            else:
                for j in range(2):
                    for tb in range(TB):
                        mm = products([proj(cb, tb)[:, 0:cols]], hA, 4 * j, 4, tb, u + j, cols, j == 0, j == 1)
                        if j and tb == 0:
                            mm.then_inc(proj_done, 1)
                    mm.then_inc(unit_used, 1)
            if n in (1, 2):
                name, buf = (("mq", mq_tm), ("mk", mk_tm))[n - 1]
                pe.wait_ge(proj_out, 2 * cb)
                for tb in range(TB):
                    turn((name, tb), [buf[:, tb, b * P:(b + 1) * P] for b in range(4)])
            if n == 3:
                for tb in range(TB):
                    turned(("mk", tb))
                pair_scores("b", 0)
            if n == 4:
                pe.wait_ge(proj_out, 2 * (CB_IN2 + 3))
                pair("b", 0)
        pair("b", 1)

        pe.wait_ge(c_src, 4)
        for tb in range(TB):
            turn(("cq", tb), [cq[:, tb, k * P:(k + 1) * P] for k in range(3)])
        turn(("ckv",), [ckv[:, tb, k * P:(k + 1) * P] for k in range(2) for tb in range(TB)])
        for n in range(2):
            cb = CB_UQ + n
            pe.wait_ge(proj_out, 2 * cb - 2)
            for tb in range(TB):
                turned(("cq", tb))
                mm = products([proj(cb, tb)[:, 0:QR]], hA, 0, 3, tb, U0["uq"] + n, QR, True, True)
                mm.then_inc(unit_used if tb else proj_done, 1)
        pair("b", 2)
        pe.wait_ge(proj_out, 2 * CB_UKV)
        turned(("ckv",))
        for tb in range(TB):
            mm = products([acc(tb, c)[:, :] for c in range(2)], [t[:, 3:5, :] for t in hA], 0, 2, tb, U0["ukv"], D,
                          True, True)
            mm.then_inc(unit_used if tb else proj_done, 1)
        pair("b", 3)
        pe.wait_ge(rot_ready, 1)
        for j in range(MH // 2):
            turn(("q", j), [q_tm[:, tb, h, :] for h in (2 * j, 2 * j + 1) for tb in range(TB)])
        pe.wait_ge(k_full, 1)
        for j in range(MH // 2):
            turn(("k", j), [k_tm[:, tb, h, :] for h in (2 * j, 2 * j + 1) for tb in range(TB)])
        turned(("k", MH // 2 - 2))
        turned(("k", MH // 2 - 1))
        pair_scores("l", 0)
        for j in range(MH // 2):
            pair("l", j)

        def before_o2(tb):
            turned(("lv", MH - 2))
            turned(("lv", MH - 1))
            turn_rows("cat", src, tb)
            turned_rows("cat", tb)
            pe.wait_ge(proj_out, 2 * CB_UKV + 2)
        output("o2", hB, U0["o2"], before_o2)
        gated("f2", "ffn2", DFF // HALF + FF2 // SUB)

    @block.scalar
    def _(act):
        def hi(u, du=0, turns=0):
            if u >= N_UNITS:
                return
            if u >= SLOTS:
                act.wait_ge(unit_used, u - SLOTS + 1 + du)
            act.wait_ge(raw_in[u % SLOTS], 32 * (u // SLOTS + 1) + 32 * turns)
            w = unit_width(u)
            act.activation(w_hi[u % SLOTS][:, 0:w], raw[u % SLOTS][:, 0:w], ACT.Copy).then_inc(hi_ready, 1)

        def split(name, di=0):
            act.wait_ge(work_done, WB[name] + 1 + 2 * di)
            (dst, _), b = rows_of(name)
            act.activation(dst, b, ACT.Copy).then_inc(split_hi, 1)

        def split_rows(name, tb):
            for h in range(2):
                split((name, tb, h))

        def squares(name, tb):
            n = 2 * NORMS.index(name) + tb
            if name == "mix":
                act.wait_ge(x_in[tb], 16)
            elif name == "ffn1":
                act.wait_ge(mid_ready, tb + 1)
            else:
                act.wait_ge(acc_out, 2 * ACC[NORM_X[name]] + tb + 1)
            if n:
                act.wait_ge(square_sum, n)
            act.activation(junk[:, :], x[:, tb, :], ACT.Square, accum_out=ss[:, n:n + 1]).then_inc(square_sum, 1)

        def proj_ready(cb, tb, last_unit):
            if tb == 0:
                act.wait_ge(proj_done, cb + 1)
            else:
                act.wait_ge(unit_used, last_unit + 1)

        def proj_copy(cb):
            dst = [(qk_tm[cb % 2], 0)] * 4 + [(va, 0), (va, HALF)] + [(qk_tm[cb % 2], 0)] * 2
            dst += [(b, c) for b in (vr, gr, ga, gg) for c in (0, HALF)]
            buf, c0 = dst[cb]
            for tb in range(TB):
                proj_ready(cb, tb, U0["in"] + 2 * cb + 1)
                act.activation(buf[:, tb, c0:c0 + HALF], proj(cb, tb)[:, :], ACT.Copy).then_inc(proj_out, 1)

        def exps(m, ready):
            act.wait_ge(score_out, ready + 1)
            for tb, c in enumerate((slice(0, P), slice(P, 384))):
                e = act.activation(L[:, m % 4, c], L[:, m % 4, c], ACT.Exp, bias=mn[:, m, tb:tb + 1], scale=-1.0,
                                   accum_out=sm[:, m, tb:tb + 1])
            e.then_inc(exp_ready, 1)

        def weights_copy(name, h):
            n = WB[name, h]
            act.wait_ge(work_done, n + 1)
            act.activation(aT[h % 2][:, :], work((name, h))[:, 0:384], ACT.Copy).then_inc(work_out[n % 2], 1)

        def diff_y(h):
            n = WB["v", h]
            act.wait_ge(work_done, n + 1)
            for tb in range(TB):
                y = act.activation(src[:, tb, h * P:(h + 1) * P], work(("v", h))[:, tb * P:(tb + 1) * P], ACT.Copy,
                                   scale=rsm[:, 2 * h, tb:tb + 1])
            y.then_inc(work_out[n % 2], 1)

        def ret_y(h):
            n = WB["rv", h]
            act.wait_ge(work_done, n + 1)
            act.activation(yr[:, :, h * RV:(h + 1) * RV], work(("rv", h))[:, :].rearrange("p (t n) -> p t n", n=RV),
                           ACT.Copy).then_inc(work_out[n % 2], 1)

        act.dma_start(masks[:, :], masks_d).then_inc(mask_in, 16)
        for n, lam in enumerate((lam_q1, lam_k1, lam_q2, lam_k2)):
            act.dma_start(lam_v[:, n, :], lam[0].partition_broadcast(P)).then_inc(lam_in, 16)
        for tb in range(TB):
            squares("mix", tb)
        for j in range(2):
            hi(j)
            split_rows("mix", j)
        act.wait_ge(lam_prod, 2)
        act.activation(lam_s[:, 2:4], lam_s[:, 0:2], ACT.Exp).then_inc(lam_exp, 1)
        for k in range(IN_CB + 1):
            step = k - 1
            if 6 <= step < 14:
                weights_copy("a", step - 6)
            if step >= 0:
                proj_copy(step)
            if k == 1:
                split(("p",))
            if k < IN_CB:
                hi(2 * k + 2)
            if 6 <= step < 14:
                diff_y(step - 6)
            if step >= 12:
                ret_y(step - 12)
            if 5 <= step < 13:
                for c in range(2):
                    exps(SOFT["d", step - 5, c], SM["d", step - 5, c])
            if k == 14:
                act.wait_ge(proj_out, 24)
                act.activation(gr[:, :, :], gr[:, :, :], ACT.Silu).then_inc(gates_ready, 1)
            if k < IN_CB:
                hi(2 * k + 3)
        for tb in range(TB):
            split_rows("ya", tb)
        act.wait_ge(proj_out, 2 * IN_CB)
        act.activation(ga[:, :, :], ga[:, :, :], ACT.Sigmoid).then_inc(gates_ready, 1)
        hi(34)
        act.activation(gg[:, :, :], gg[:, :, :], ACT.Sigmoid).then_inc(gates_ready, 1)
        hi(35)
        split_rows("yr", 0)
        hi(36)
        hi(37)
        split_rows("yr", 1)
        for n in range(38, 43):
            hi(n)
        for tb in range(TB):
            split_rows("m", tb)
        for n in range(43, 46):
            hi(n)
        for tb in range(TB):
            squares("mlp", tb)
        hi(46)

        def step_ready(i, tb, last_unit, di=0, du=0):
            if tb == 0:
                act.wait_ge(up_done, i + 1 + di)
            else:
                act.wait_ge(unit_used, last_unit + 1 + du)

        def relu(i, tb, r=0):
            step_ready(i, tb, U0["ff"] + 1 + (4 * i - 2 if i else 0), 3 * r, 12 * r)
            act.activation(act_r[:, tb, :], up(tb)[:, :], ACT.Relu).then_inc(act_ready, 1)

        for tb in range(TB):
            split_rows("mlp", tb)
        relu(0, 0)
        hi(47)
        relu(0, 1)

        def relu_step(i, r=0):
            v = U0["ff"] + 2 + 4 * (i - 1)
            hi(v + 2, 12 * r, 4 * r)
            for tb in range(TB):
                split(("ff", i - 1, tb), 3 * r)
            hi(v + 3, 12 * r, 4 * r)
            for tb in range(TB):
                relu(i, tb, r)
            hi(v + 4, 12 * r, 4 * r)
            hi(v + 5, 12 * r, 4 * r)
        relu_step(1)
        with act.Fori(0, 2) as r:
            for j in range(3):
                relu_step(2 + j, r)
        for tb in range(TB):
            split(("ff", 7, tb))
        hi(76)
        for tb in range(TB):
            squares("ple", tb)
            hi(77 + tb)
        for tb in range(TB):
            if tb == 0:
                act.wait_ge(pl_done, 1)
            else:
                act.wait_ge(unit_used, U0["pl"] + 1)
            for c in range(2):
                mm = act.activation(pl_s[:, tb, c * HALF:(c + 1) * HALF], bank[(4, 0)[tb] + c][:, :], ACT.Copy)
            mm.then_inc(pl_out, 1)
        hi(79)
        for tb in range(TB):
            split_rows("ple", tb)
        for n in range(80, 83):
            hi(n)
        for tb in range(TB):
            if tb == 0:
                act.wait_ge(acc_done, ACC["pg"] + 1)
            else:
                act.wait_ge(unit_used, U0["pg"] + 4)
            for c in range(2):
                s = act.activation(sg[:, tb, c * HALF:(c + 1) * HALF], acc(tb, c)[:, :], ACT.Sigmoid)
            s.then_inc(pg_sig, 1)
        hi(83)
        for name in ("mid", "ffn1"):
            for tb in range(TB):
                squares(name, tb)

        def gated(name, norm, base):
            u, n = U0[name], FF2 // SUB

            def silu(i, tb, r=0):
                step_ready(base + i, tb, u + 1 + (3 * i - 1 if i else 0), r, 3 * r)
                act.activation(act_r[:, tb, 0:SUB], up(tb)[:, 0:SUB], ACT.Silu).then_inc(act_ready, 1)

            for tb in range(TB):
                split_rows(norm, tb)
            silu(0, 0)
            hi(u + 3)
            silu(0, 1)

            def step(i, r=0):
                v = u + 2 + 3 * (i - 1)
                hi(v + 2, 3 * r, r)
                for tb in range(TB):
                    split((name, i - 1, tb), r)
                hi(v + 3, 3 * r, r)
                for tb in range(TB):
                    silu(i, tb, r)
                hi(v + 4, 3 * r, r)
            step(1)
            with act.Fori(0, n - 3) as r:
                step(2, r)
            step(n - 1)
            split((name, n - 1, 0))
            act.wait_ge(unit_used, u + 32)
            split((name, n - 1, 1))
            hi(u + 34)
            for tb in range(TB):
                squares("mix2" if name == "f1" else "final", tb)
            hi(u + 35)

        gated("f1", "ffn1", DFF // HALF)

        def in2_copy(n):
            buf, cols = [(mq_tm, 512), (mk_tm, 512), (mv, 512), (cq, QR), (ckv, KVR + ROPE)][n]
            for tb in range(TB):
                proj_ready(CB_IN2 + n, tb, U0["in2"] + 2 * n + 1)
                act.activation(buf[:, tb, :], proj(CB_IN2 + n, tb)[:, 0:cols], ACT.Copy).then_inc(proj_out, 1)

        def head_y(kind, h):
            n, m = WB[kind + "v", h], SOFT[kind, h]
            act.wait_ge(work_done, n + 1)
            act.wait_ge(rsm_ready, m - 2 * DH + 1)
            c0 = (h + (MH if kind == "b" else 0)) * BD
            for tb in range(TB):
                y = act.activation(src[:, tb, c0:c0 + BD], work((kind + "v", h))[:, tb * BD:(tb + 1) * BD], ACT.Copy,
                                   scale=rsm[:, m, tb:tb + 1])
            y.then_inc(work_out[n % 2], 1)

        def pair(kind, j):
            for h in (2 * j, 2 * j + 1):
                weights_copy(kind + "a", h)
            for h in (2 * j, 2 * j + 1):
                head_y(kind, h)
            if 2 * j + 2 < BH:
                for h in (2 * j + 2, 2 * j + 3):
                    exps(SOFT[kind, h], SM[kind, h])

        for tb in range(TB):
            split_rows("mix2", tb)
        hi(117)
        for n in range(1, 5):
            in2_copy(n - 1)
            hi(116 + 2 * n)
            if n == 1:
                act.wait_ge(ang_ready, 1)
                act.activation(sin2[:, :, 16:32], sin2[:, :, 16:32], ACT.Sin).then_inc(trig_ready, 1)
                act.activation(cos2[:, :, 0:16], cos2[:, :, 0:16], ACT.Sin).then_inc(trig_ready, 1)
            if n == 4:
                for h in range(2):
                    exps(SOFT["b", h], SM["b", h])
            hi(117 + 2 * n)
        in2_copy(4)
        hi(126)
        act.wait_ge(proj_out, 2 * (CB_IN2 + 5))
        for tb in range(TB):
            for n, (buf, cols) in enumerate(((cq, QR), (ckv, KVR))):
                k = 2 * n + tb
                if tb or n:
                    act.wait_ge(csq, 2 * tb + n)
                act.activation(junk[:, 0:cols], buf[:, tb, 0:cols], ACT.Square, accum_out=ssc[:, k:k + 1])\
                   .then_inc(csq, 1)
        pair("b", 0)
        pair("b", 1)
        split(("cq", 0))
        split(("cq", 1))
        split(("ckv",))
        for n in range(2):
            for tb in range(TB):
                proj_ready(CB_UQ + n, tb, U0["uq"] + n)
                act.activation(q_tm[:, tb, 4 * n:4 * n + 4, :],
                               proj(CB_UQ + n, tb)[:, 0:QR].rearrange("p (h c) -> p h c", c=MQ), ACT.Copy)\
                   .then_inc(proj_out, 1)
            hi(127 + n)
        pair("b", 2)
        for tb in range(TB):
            proj_ready(CB_UKV, tb, U0["ukv"])
            for c in range(2):
                heads = acc(tb, c)[:, :].rearrange("p (h c) -> p h c", c=NOPE + MV)
                act.activation(k_tm[:, tb, 4 * c:4 * c + 4, 0:NOPE], heads[:, :, 0:NOPE], ACT.Copy)
                kv = act.activation(v_tm[:, tb, 4 * c:4 * c + 4, :], heads[:, :, NOPE:NOPE + MV], ACT.Copy)
            kv.then_inc(proj_out, 1)
        hi(129)
        act.wait_ge(kr_ready, 1)
        for tb in range(TB):
            k = act.activation(k_tm[:, tb, :, NOPE:MQ], kr[:, tb, :].unsqueeze(1).to_broadcast([P, MH, ROPE]), ACT.Copy)
        k.then_inc(k_full, 1)
        pair("b", 3)
        for name, buf in (("q", qT), ("k", kT)):
            for j in (1, 3):
                n = WB[name, j]
                act.wait_ge(work_done, n + 1)
                act.activation(buf[:, 2 * j:2 * j + 2, :],
                               work((name, j))[0:MQ, :].rearrange("p (h t) -> p h t", t=SEQ), ACT.Copy)\
                   .then_inc(work_out[n % 2], 1)
        for h in range(2):
            exps(SOFT["l", h], SM["l", h])
        for j in range(MH // 2):
            pair("l", j)
        for tb in range(TB):
            split_rows("cat", tb)
        for n in range(130, 133):
            hi(n)
        for tb in range(TB):
            squares("ffn2", tb)
        hi(133)
        gated("f2", "ffn2", DFF // HALF + FF2 // SUB)

    @block.vector
    def _(vec):
        chain = [0]

        def link(ins):
            chain[0] += 1
            ins.then_inc(vec_step, 1)
            vec.wait_ge(vec_step, chain[0])

        def lo(u, du=0):
            if u >= N_UNITS:
                return
            vec.wait_ge(hi_ready, u + 1 + du)
            w = unit_width(u)
            vec.tensor_tensor(w_lo[u % SLOTS][:, 0:w], raw[u % SLOTS][:, 0:w],
                              w_hi[u % SLOTS][:, 0:w].bitcast(f32), ALU.subtract).then_inc(lo_ready, 1)

        def split(name, di=0):
            vec.wait_ge(split_hi, SPLIT[name] + 1 + 2 * di)
            (hi, dst), b = rows_of(name)
            vec.tensor_tensor(dst, b, hi.bitcast(f32), ALU.subtract).then_inc(work_out[WB[name] % 2], 1)

        def split_rows(name, tb):
            for h in range(2):
                split((name, tb, h))

        def sums_ready(name, tb):
            if tb == 0:
                vec.wait_ge(acc_done, ACC[name] + 1)
            else:
                vec.wait_ge(unit_used, U0[name] + dict(UNITS)[name])

        def x_add(name, tb, scale):
            sums_ready(name, tb)
            for c in range(2):
                xs = x[:, tb, c * HALF:(c + 1) * HALF]
                a = vec.scalar_tensor_tensor(out=xs, in0=acc(tb, c)[:, :], scalar=scale, in1=xs,
                                             op0=ALU.mult, op1=ALU.add)
            a.then_inc(acc_out, 1)

        def norm(name, tb):
            n = 2 * NORMS.index(name) + tb
            vec.wait_ge(rstd_ready, n + 1)
            vec.wait_ge(gain_in, GAIN[name])
            if name == "ffn1":
                vec.wait_ge(mid_ready, tb + 1)
            elif name != "mix":
                vec.wait_ge(acc_out, 2 * ACC[NORM_X[name]] + tb + 1)
            vec.scalar_tensor_tensor(out=src[:, tb, :], in0=x[:, tb, :], scalar=rs[:, n:n + 1], in1=gain[:, :],
                                     op0=ALU.mult, op1=ALU.mult).then_inc(src_ready, 1)

        def logits(name, b, scale):
            m = SOFT[name]
            vec.wait_ge(score_done, SM[name] + 1)
            for tb, c in enumerate((slice(0, P), slice(P, 384))):
                t = vec.tensor_tensor_reduce(out=L[:, m % 4, c], in0=score(name)[:, c], in1=b[:, c], scale=-scale,
                                             scalar=3e38, op0=ALU.add, op1=ALU.min, accum_out=mn[:, m, tb:tb + 1])
            t.then_inc(score_out, 1)

        def diff_logits(h):
            vec.wait_ge(bias_ready, h + 1)
            for c in range(2):
                logits(("d", h, c), bias[h % 2], DHD ** -0.5)

        def combine(h):
            m = 2 * h
            vec.wait_ge(exp_ready, m + 2)
            link(vec.reciprocal(rsm[:, m:m + 2, :], sm[:, m:m + 2, :]))
            link(vec.scalar_tensor_tensor(out=qc[:, h, :], in0=rsm[:, m + 1, :], scalar=neglam[:, 0:1],
                                          in1=sm[:, m, :], op0=ALU.mult, op1=ALU.mult))
            for tb, c in enumerate((slice(0, P), slice(P, 384))):
                t = vec.scalar_tensor_tensor(out=L[:, (m + 1) % 4, c], in0=L[:, (m + 1) % 4, c],
                                             scalar=qc[:, h, tb:tb + 1], in1=L[:, m % 4, c],
                                             op0=ALU.mult, op1=ALU.add)
            t.then_inc(comb_ready, 1)

        def head_squares(name, h, buf, width, heads, sums, counter, scratch):
            n = WB[name, h]
            vec.wait_ge(work_out[n % 2], n // 2 + 1)
            for tb in range(TB):
                y = buf[:, tb, h * width:(h + 1) * width]
                k = 2 * h + tb
                if k:
                    vec.wait_ge(counter, k)
                vec.tensor_tensor_reduce(out=scratch[:, 0:width], in0=y, in1=y, scale=1.0, scalar=0.0, op0=ALU.mult,
                                         op1=ALU.add, accum_out=sums[:, tb * heads + h:tb * heads + h + 1])\
                   .then_inc(counter, 1)

        for tb in range(TB):
            norm("mix", tb)
        for j in range(2):
            lo(j)
            split_rows("mix", j)
        vec.wait_ge(lam_in, 64)
        for n in range(2):
            vec.tensor_tensor_reduce(out=lam_w[:, n, :], in0=lam_v[:, 2 * n, :], in1=lam_v[:, 2 * n + 1, :], scale=1.0,
                                     scalar=0.0, op0=ALU.mult, op1=ALU.add, accum_out=lam_s[:, n:n + 1])\
               .then_inc(lam_prod, 1)
        vec.wait_ge(lam_exp, 1)
        link(vec.tensor_tensor(lam_s[:, 0:1], lam_s[:, 3:4], lam_s[:, 2:3], ALU.subtract))
        link(vec.tensor_scalar(neglam[:, :], lam_s[:, 0:1], -LAM_INIT, None, ALU.add))
        for k in range(IN_CB):
            step = k - 1
            if k == 1:
                split(("p",))
            if 5 <= step < 13:
                diff_logits(step - 5)
            if 11 <= step < 15:
                h = step - 11
                vec.wait_ge(decay_in[h % 2], 16 * (h // 2 + 1))
                vec.wait_ge(score_done, SM["r", h] + 1)
                vec.tensor_tensor(sT[h % 2][:, :], score(("r", h))[:, 0:384], decay[h % 2][:, :], ALU.mult)\
                   .then_inc(score_out, 1)
            if step in (1, 2, 3, 4, 7, 8):
                cb = step - 1
                dst, b0 = {0: (qaT, 0), 1: (qaT, 4), 2: (kaT, 0), 3: (kaT, 4), 6: (qrT, 0), 7: (krT, 0)}[cb]
                for tb in range(TB):
                    n = WB["qk", cb, tb]
                    vec.wait_ge(work_done, n + 1)
                    vec.tensor_copy(dst[:, b0:b0 + 4, tb * P:(tb + 1) * P],
                                    bank[6 + n % 2][:, :].rearrange("p (b t) -> p b t", t=P))\
                       .then_inc(work_out[n % 2], 1)
            lo(2 * k + 2)
            if 6 <= step < 14:
                head_squares("v", step - 6, src, P, DH, ssy, ysq, vjunk)
            if step >= 12:
                head_squares("rv", step - 12, yr, RV, RH, ssr, rsq, rjunk)
            if 5 <= step < 13:
                combine(step - 5)
            if k == 15:
                vec.wait_ge(ystd, 1)
                vec.wait_ge(gd_in, 16)
                for tb in range(TB):
                    y = src[:, tb, :].rearrange("p (h c) -> p h c", c=P)
                    r = rsy[:, tb * DH:(tb + 1) * DH]
                    link(vec.tensor_tensor(y, y, r.unsqueeze(2).to_broadcast([P, DH, P]), ALU.mult))
                    vec.scalar_tensor_tensor(out=y, in0=y, scalar=1.0 - LAM_INIT,
                                             in1=gd[:, :].unsqueeze(1).to_broadcast([P, DH, P]),
                                             op0=ALU.mult, op1=ALU.mult).then_inc(src_ready, 1)
            lo(2 * k + 3)
        head_squares("rv", 3, yr, RV, RH, ssr, rsq, rjunk)
        for tb in range(TB):
            split_rows("ya", tb)
        lo(34)
        vec.wait_ge(rstd_r, 1)
        vec.wait_ge(gsg_ready, 1)
        for tb in range(TB):
            y = yr[:, tb, :].rearrange("p (h c) -> p h c", c=RV)
            r = rsr[:, tb * RH:(tb + 1) * RH]
            link(vec.tensor_tensor(y, y, r.unsqueeze(2).to_broadcast([P, RH, RV]), ALU.mult))
            vec.tensor_tensor(yr[:, tb, :], yr[:, tb, :], gr[:, tb, :], ALU.mult).then_inc(yr_src, 1)
        lo(35)

        def gate(name, tb, g, dst):
            sums_ready(name, tb)
            for c in range(2):
                cols = slice(c * HALF, (c + 1) * HALF)
                t = vec.tensor_tensor(dst[:, tb, cols], acc(tb, c)[:, :], g[:, tb, cols], ALU.mult)
            t.then_inc(acc_out, 1)

        def mix(tb):
            gate("br", tb, gg, mix_t)
            vec.wait_ge(acc_out, 2 * ACC["br"] + tb + 1)
            vec.tensor_tensor(src[:, tb, :], src[:, tb, :], mix_t[:, tb, :], ALU.add).then_inc(src_ready, 1)

        vec.wait_ge(gates_ready, 3)
        gate("bd", 0, ga, src)
        split_rows("yr", 0)
        lo(36)
        lo(37)
        split_rows("yr", 1)
        gate("bd", 1, ga, src)
        lo(38)
        lo(39)
        mix(0)
        for n in range(40, 43):
            lo(n)
        split_rows("m", 0)
        mix(1)
        split_rows("m", 1)
        for n in range(43, 46):
            lo(n)
        for tb in range(TB):
            x_add("out", tb, 1.0)
        for tb in range(TB):
            norm("mlp", tb)
        lo(46)

        def square(i, tb, r=0):
            vec.wait_ge(act_ready, 2 * i + tb + 1 + 6 * r)
            vec.scalar_tensor_tensor(out=act_f[:, tb, :], in0=up(tb)[:, :], scalar=0.0, in1=act_r[:, tb, :],
                                     op0=ALU.max, op1=ALU.mult).then_inc(up_out, 1)

        for tb in range(TB):
            split_rows("mlp", tb)
        square(0, 0)
        lo(47)
        square(0, 1)

        def relu_step(i, r=0):
            v = U0["ff"] + 2 + 4 * (i - 1)
            lo(v + 2, 12 * r)
            for tb in range(TB):
                split(("ff", i - 1, tb), 3 * r)
            lo(v + 3, 12 * r)
            for tb in range(TB):
                square(i, tb, r)
            lo(v + 4, 12 * r)
            lo(v + 5, 12 * r)
        relu_step(1)
        with vec.Fori(0, 2) as r:
            for j in range(3):
                relu_step(2 + j, r)
        for tb in range(TB):
            split(("ff", 7, tb))
        lo(76)
        for tb in range(TB):
            x_add("ff", tb, 1.0)
            lo(77 + tb)
        for tb in range(TB):
            norm("ple", tb)
        lo(79)
        for tb in range(TB):
            split_rows("ple", tb)
        for n in range(80, 83):
            lo(n)
        for tb in range(TB):
            vec.wait_ge(pg_sig, tb + 1)
            link(vec.tensor_tensor(sg[:, tb, :], sg[:, tb, :], pl_s[:, tb, :], ALU.mult))
            vec.tensor_tensor(x[:, tb, :], x[:, tb, :], sg[:, tb, :], ALU.add).then_inc(acc_out, 1)
        for tb in range(TB):
            n = 2 * NORMS.index("mid") + tb
            vec.wait_ge(rstd_ready, n + 1)
            vec.wait_ge(gain_in, GAIN["mid"])
            vec.wait_ge(acc_out, 2 * ACC["pg"] + tb + 1)
            vec.wait_ge(square_sum, n + 1)
            vec.scalar_tensor_tensor(out=x[:, tb, :], in0=x[:, tb, :], scalar=rs[:, n:n + 1], in1=gain[:, :],
                                     op0=ALU.mult, op1=ALU.mult).then_inc(mid_ready, 1)
        for tb in range(TB):
            norm("ffn1", tb)
        lo(83)

        def gated(name, norm_in, base, norm_out):
            u, n = U0[name], FF2 // SUB

            def multiply(i, tb, r=0):
                vec.wait_ge(act_ready, 2 * (base + i) + tb + 1 + 2 * r)
                vec.tensor_tensor(act_f[:, tb, 0:SUB], up(tb)[:, SUB:2 * SUB], act_r[:, tb, 0:SUB], ALU.mult)\
                   .then_inc(up_out, 1)

            for tb in range(TB):
                split_rows(norm_in, tb)
            multiply(0, 0)
            lo(u + 3)
            multiply(0, 1)

            def step(i, r=0):
                v = u + 2 + 3 * (i - 1)
                lo(v + 2, 3 * r)
                for tb in range(TB):
                    split((name, i - 1, tb), r)
                lo(v + 3, 3 * r)
                for tb in range(TB):
                    multiply(i, tb, r)
                lo(v + 4, 3 * r)
            step(1)
            with vec.Fori(0, n - 3) as r:
                step(2, r)
            step(n - 1)
            for tb in range(TB):
                split((name, n - 1, tb))
            lo(u + 34)
            for tb in range(TB):
                x_add(name, tb, 0.5)
            for tb in range(TB):
                norm(norm_out, tb)
            lo(u + 35)

        gated("f1", "ffn1", DFF // HALF, "mix2")

        def positions():
            vec.wait_ge(pos_in, 64)
            link(vec.tensor_copy(pos_k[:, :], pos_ki[:, :]))
            link(vec.tensor_copy(pos_q[:, :], pos_qi[:, :]))
            vec.tensor_scalar(posdist[:, 0:P], pos_k[:, 0:P], pos_q[:, 0:1], None, ALU.subtract)
            link(vec.tensor_scalar(posdist[:, P:384], pos_k[:, :], pos_q[:, 1:2], None, ALU.subtract))
            link(vec.scalar_tensor_tensor(out=posdist[:, :], in0=posdist[:, :], scalar=-1.0, in1=posdist[:, :],
                                          op0=ALU.mult, op1=ALU.min))
            vec.tensor_tensor(posdist[:, :], posdist[:, :], mask, ALU.add).then_inc(pos_ready, 1)
            for tb in range(TB):
                link(vec.tensor_scalar(ang[:, tb, :], freq[:, :], pos_q[:, tb:tb + 1], None, ALU.mult))
            link(vec.tensor_scalar(turns_[:, :, :], ang[:, :, :], 1 / (2 * math.pi), None, ALU.mult))
            link(vec.tensor_scalar(turns_[:, :, :], turns_[:, :, :], 1.5 * 2 ** 23, None, ALU.add))
            link(vec.tensor_scalar(turns_[:, :, :], turns_[:, :, :], -1.5 * 2 ** 23, None, ALU.add))
            part1 = 6.28125
            part2 = float(np.float32(round((2 * math.pi - part1) * 2 ** 21) / 2 ** 21))
            for part in (part1, part2, 2 * math.pi - part1 - part2):
                link(vec.scalar_tensor_tensor(out=ang[:, :, :], in0=turns_[:, :, :], scalar=-part, in1=ang[:, :, :],
                                              op0=ALU.mult, op1=ALU.add))
            edge = float(np.nextafter(np.float32(math.pi), np.float32(0)))
            link(vec.tensor_scalar(sin2[:, :, 16:32], ang[:, :, :], edge, -edge, ALU.min, ALU.max))
            link(vec.scalar_tensor_tensor(out=cos2[:, :, 0:16], in0=sin2[:, :, 16:32], scalar=-1.0,
                                          in1=sin2[:, :, 16:32], op0=ALU.mult, op1=ALU.min))
            vec.tensor_scalar(cos2[:, :, 0:16], cos2[:, :, 0:16], math.pi / 2, None, ALU.add).then_inc(ang_ready, 1)

        def trig_pairs():
            vec.wait_ge(trig_ready, 2)
            link(vec.tensor_copy(cos2[:, :, 16:32], cos2[:, :, 0:16]))
            link(vec.tensor_scalar(sin2[:, :, 0:16], sin2[:, :, 16:32], -1.0, None, ALU.mult))

        def rotate(v, out, t, cos, sin):
            half = ROPE // 2
            link(vec.tensor_tensor(t[..., 0:half], v[..., half:ROPE], sin[..., 0:half], ALU.mult))
            link(vec.tensor_tensor(t[..., half:ROPE], v[..., 0:half], sin[..., half:ROPE], ALU.mult))
            link(vec.tensor_tensor(out, v, cos, ALU.mult))
            return vec.tensor_tensor(out, out, t, ALU.add)

        def block_logits(kind, h):
            if kind == "b":
                vec.wait_ge(bias_ready, DH + h + 1)
                logits(("b", h), bias[h % 2], BD ** -0.5)
            else:
                logits(("l", h), mask, MQ ** -0.5)

        def reciprocals(kind, h):
            m = SOFT[kind, h]
            vec.wait_ge(exp_ready, m + 1)
            vec.reciprocal(rsm[:, m, :], sm[:, m, :]).then_inc(rsm_ready, 1)

        def next_pair(kind, j):
            for h in (2 * j, 2 * j + 1):
                block_logits(kind, h)

        def turned_copy(name, dst):
            n = WB[name]
            vec.wait_ge(work_done, n + 1)
            rows = dst.shape[0]
            vec.tensor_copy(dst, work(name)[0:rows, :].rearrange("p (b t) -> p b t", t=dst.shape[-1]))\
               .then_inc(work_out[n % 2], 1)

        for tb in range(TB):
            split_rows("mix2", tb)
        positions()
        lo(117)
        lo(118)
        trig_pairs()
        lo(119)
        for n, (name, dst) in enumerate((("mq", mqT), ("mk", mkT))):
            for tb in range(TB):
                turned_copy((name, tb), dst[:, :, tb * P:(tb + 1) * P])
            lo(120 + 2 * n)
            lo(121 + 2 * n)
        next_pair("b", 0)
        lo(124)
        for h in range(2):
            reciprocals("b", h)
        lo(125)
        next_pair("b", 1)
        lo(126)
        vec.wait_ge(cstd, 1)
        vec.wait_ge(gain_in, GAIN["c"])
        for tb in range(TB):
            for n, (buf, c0, cols) in enumerate(((cq, 0, QR), (ckv, QR, KVR))):
                k = 2 * n + tb
                vec.scalar_tensor_tensor(out=buf[:, tb, 0:cols], in0=buf[:, tb, 0:cols], scalar=rsc[:, k:k + 1],
                                         in1=gain[:, c0:c0 + cols], op0=ALU.mult, op1=ALU.mult).then_inc(c_src, 1)
        for h in range(2, 4):
            reciprocals("b", h)
        next_pair("b", 2)
        vec.wait_ge(proj_out, 2 * (CB_IN2 + 5))
        rotate(ckv[:, :, KVR:KVR + ROPE], kr[:, :, :], rope_t[:, :, :], cos2[:, :, :], sin2[:, :, :])\
            .then_inc(kr_ready, 1)
        for h in range(4, 6):
            reciprocals("b", h)
        split(("cq", 0))
        split(("cq", 1))
        split(("ckv",))
        lo(127)
        lo(128)
        next_pair("b", 3)
        vec.wait_ge(proj_out, 2 * CB_UKV)
        heads = lambda t: t[:, :, :].unsqueeze(2).to_broadcast([P, TB, MH, ROPE])
        q_rot = q_tm[:, :, :, NOPE:MQ]
        rotate(q_rot, q_rot, rot_t[:, :, :, :], heads(cos2), heads(sin2)).then_inc(rot_ready, 1)
        for h in range(6, 8):
            reciprocals("b", h)
        lo(129)
        for name, buf in (("q", qT), ("k", kT)):
            for j in (0, 2):
                turned_copy((name, j), buf[:, 2 * j:2 * j + 2, :])
        for j in range(MH // 2):
            next_pair("l", j)
            for h in (2 * j, 2 * j + 1):
                reciprocals("l", h)
        for tb in range(TB):
            split_rows("cat", tb)
        for n in range(130, 133):
            lo(n)
        for tb in range(TB):
            x_add("o2", tb, 1.0)
        for tb in range(TB):
            norm("ffn2", tb)
        lo(133)
        gated("f2", "ffn2", DFF // HALF + FF2 // SUB, "final")

    @block.gpsimd
    def _(pool):
        chain = [0]

        def link(ins):
            chain[0] += 1
            ins.then_inc(pool_step, 1)
            pool.wait_ge(pool_step, chain[0])

        def load_gain(name, *parts):
            c0 = 0
            for g in parts:
                n = g.shape[-1]
                pool.dma_start(gain[:, c0:c0 + n], g.partition_broadcast(P)).then_inc(gain_in, 16)
                c0 += n

        def inverse_rms(s, m, r, width):
            link(pool.tensor_scalar(m, s, 1.0 / width, EPS, ALU.mult, ALU.add))
            return pool.tensor_tensor(r, m, nhalf[:, 0:r.shape[-1]], ALU.pow)

        def rstd(name):
            for tb in range(TB):
                n = 2 * NORMS.index(name) + tb
                pool.wait_ge(square_sum, n + 1)
                inverse_rms(ss[:, n:n + 1], ms[:, n:n + 1], rs[:, n:n + 1], D).then_inc(rstd_ready, 1)

        def head_bias(k, base, slope, scale):
            pool.tensor_scalar(bias[k % 2][:, :], base, slope / scale, 1.0, ALU.mult, ALU.mult).then_inc(bias_ready, 1)

        load_gain("mix", g_mix[0])
        link(pool.memset(nhalf[:, :], -0.5))
        pool.dma_start(p_sb[:, :, :], p_d.rearrange("(b p) n -> p b n", p=P)).then_inc(p_in, 16)
        pool.dma_start(gd[:, :], g_diff[0].partition_broadcast(P)).then_inc(gd_in, 16)
        pool.dma_start(decay[0][:, :], decay_d[0]).then_inc(decay_in[0], 16)
        pool.dma_start(decay[1][:, :], decay_d[1]).then_inc(decay_in[1], 16)
        rstd("mix")
        pool.wait_ge(mask_in, 16)
        for h in range(DH):
            if h >= 2:
                pool.wait_ge(score_out, SM["d", h - 2, 1] + 1)
            head_bias(h, negdist, alibi(h), DHD ** -0.5)
        pool.wait_ge(src_ready, SRC["mix"] + TB)
        load_gain("ret", g_ret[0])
        for h in (2, 3):
            pool.wait_ge(score_out, SM["r", h - 2] + 1)
            pool.dma_start(decay[h % 2][:, :], decay_d[h]).then_inc(decay_in[h % 2], 16)
        pool.wait_ge(ysq, TB * DH)
        inverse_rms(ssy[:, :], msy[:, :], rsy[:, :], P).then_inc(ystd, 1)
        pool.wait_ge(gates_ready, 1)
        pool.wait_ge(gain_in, GAIN["ret"])
        pool.tensor_tensor(gr[:, :, :], gr[:, :, :], gain[:, :].unsqueeze(1).to_broadcast([P, TB, D]), ALU.mult)\
            .then_inc(gsg_ready, 1)
        pool.wait_ge(rsq, TB * RH)
        inverse_rms(ssr[:, :], msr[:, :], rsr[:, 0:TB * RH], RV).then_inc(rstd_r, 1)
        pool.wait_ge(gsg_ready, 1)
        load_gain("mlp", g_mlp[0])
        rstd("mlp")
        pool.wait_ge(src_ready, SRC["mlp"] + TB)
        load_gain("ple", g_ple[0])
        pool.dma_start(pos_ki[:, :], pos_d[0].partition_broadcast(P)).then_inc(pos_in, 16)
        for tb in range(TB):
            pool.dma_start(pos_qi[:, tb:tb + 1], pos_d[0, tb * P:(tb + 1) * P].rearrange("(p o) -> p o", o=1))\
                .then_inc(pos_in, 16)
        pool.dma_start(freq[:, :], freq_d.partition_broadcast(P)).then_inc(pos_in, 16)
        rstd("ple")
        pool.wait_ge(src_ready, SRC["ple"] + TB)
        load_gain("mid", g_fin1)
        rstd("mid")
        pool.wait_ge(mid_ready, TB)
        load_gain("ffn1", g_ffn1[0])
        rstd("ffn1")
        pool.wait_ge(src_ready, SRC["ffn1"] + TB)
        load_gain("mix2", g_mix2[0])
        rstd("mix2")
        pool.wait_ge(src_ready, SRC["mix2"] + TB)
        load_gain("c", g_q[0], g_kv[0])
        pool.wait_ge(pos_ready, 1)

        def block_bias(h):
            if h >= 2:
                pool.wait_ge(score_out, SM["b", h - 2] + 1)
            head_bias(DH + h, posdist[:, :], alibi(h), BD ** -0.5)
        for h in range(4):
            block_bias(h)
        pool.wait_ge(csq, 4)
        for n, cols in enumerate((QR, KVR)):
            r = inverse_rms(ssc[:, 2 * n:2 * n + 2], msc[:, 2 * n:2 * n + 2], rsc[:, 2 * n:2 * n + 2], cols)
        r.then_inc(cstd, 1)
        for h in range(4, BH):
            block_bias(h)
        pool.wait_ge(c_src, 4)
        load_gain("ffn2", g_ffn2[0])
        rstd("ffn2")
        pool.wait_ge(src_ready, SRC["ffn2"] + TB)
        load_gain("final", g_final)
        rstd("final")

    ctx.close()


_INS = ["x", "p", "g_mix", "w_in", "lam_q1", "lam_k1", "lam_q2", "lam_k2", "g_diff_sub", "g_ret_sub",
        "w_branch_diff", "w_branch_ret", "w_out", "g_mlp", "w_ff1", "w_ff2", "g_ple", "w_ple_gate", "w_ple", "g_final",
        "positions_2", "ffn1_norm_2", "ffn1_w_gate_2", "ffn1_w_up_2", "ffn1_w_down_2", "mix_norm_2",
        "w_in_2", "mla_q_norm_2", "mla_w_uq_2", "mla_kv_norm_2", "mla_w_ukv_2", "w_out_2", "ffn2_norm_2",
        "ffn2_w_gate_2", "ffn2_w_up_2", "ffn2_w_down_2", "final_norm_2"]


def _constants():
    t = np.arange(SEQ)
    dist = t[:, None] - t[None, :]
    causal = lambda m: np.concatenate([m[0:P, 0:P], m[P:SEQ, :]], 1)
    mask = causal(np.where(dist >= 0, 0.0, -BIG))
    negdist = causal(np.where(dist >= 0, -dist, -BIG))
    masks = np.concatenate([np.eye(P), mask, negdist], 1).astype(np.float32)
    log_gamma = np.log(1.0 - 2.0 ** (-5.0 - np.arange(RH)))
    decay = []
    for h in range(RH):
        m = np.where(dist >= 0, np.exp(log_gamma[h] * dist), 0.0).T * RK ** -0.5
        decay.append(np.concatenate([m[0:P, :], m[P:SEQ, P:SEQ]], 1))
    half = ROPE // 2
    freq = np.power(np.float32(10000.0), -np.arange(half, dtype=np.float32) * np.float32(2.0) / np.float32(ROPE))
    return {"masks": masks, "decay": np.stack(decay).astype(np.float32), "freq": freq.astype(np.float32)}


def kernel(**inputs):
    import concourse.bacc as bacc
    from concourse.bass_utils import run_bass_kernel_spmd

    nc = bacc.Bacc("TRN2", target_bir_lowering=False, num_devices=1)
    arrays = {}
    for name in _INS:
        a = np.asarray(inputs[name])
        if name in ("x", "p") or name.startswith(("w_", "ffn1_w", "ffn2_w", "mla_w")) or name == "g_ret_sub":
            a = a.reshape(-1, a.shape[-1]) if name != "g_ret_sub" else a.reshape(1, -1)
        arrays[f"in_{name}"] = np.ascontiguousarray(a)
    for name, a in _constants().items():
        arrays[f"const_{name}"] = a
    d = {n: nc.dram_tensor(n, a.shape, mybir.dt.from_np(a.dtype), kind="ExternalInput").ap() for n, a in arrays.items()}
    out = nc.dram_tensor("out", (SEQ, D), mybir.dt.float32, kind="ExternalOutput").ap()
    args = [d[f"in_{n}"] for n in _INS] + [d["const_masks"], d["const_decay"], d["const_freq"], out]
    two_blocks(nc, *args)
    r = run_bass_kernel_spmd(nc, [arrays], core_ids=[0])
    return r.results[0]["out"].reshape(1, SEQ, D)
```

```python
import math
from contextlib import ExitStack

import numpy as np
import concourse.bass as bass
from concourse import mybir

P = 128
D, TB, SEQ = 1024, 2, 256
KT = D // P
EPS = 1e-6
BIG = 1e30
RAW_SLOTS, HI_SLOTS = 6, 4
UNIT = 2048
HALF = 512

DH, DHD = 8, 64
RH, RK, RV = 4, 128, 256
DFF = 4096
LAM_INIT = 0.8 - 0.6 * math.exp(-0.3 * 0)
IN_CB = 16
FF2 = 2816
SUB = 256
MH, NOPE, ROPE, MV = 8, 64, 32, 64
QR, KVR = 384, 256
BH, BD = 8, 64
MQ = NOPE + ROPE

UNITS = [("in", 32), ("bd", 4), ("br", 4), ("out", 4), ("ff", 32), ("pl", 1), ("pg", 4),
         ("f1", 33), ("in2", 10), ("uq", 2), ("ukv", 1), ("o2", 4), ("f2", 33)]
U0, _n = {}, 0
for _name, _count in UNITS:
    U0[_name] = _n
    _n += _count
N_UNITS = _n

IN2 = [(QR + KVR + ROPE, 512), (QR + KVR + ROPE + 512, 512), (QR + KVR + ROPE + 1024, 512),
       (0, QR), (QR, KVR + ROPE)]
CB_IN2, CB_UQ, CB_UKV = IN_CB, IN_CB + len(IN2), IN_CB + len(IN2) + 2

ACC = {name: n for n, name in enumerate(["bd", "br", "out", "ff", "pg", "f1", "o2", "f2"])}
NORMS = ["mix", "mlp", "ple", "mid", "ffn1", "mix2", "ffn2", "final"]
NORM_X = {"mlp": "out", "ple": "ff", "mid": "pg", "mix2": "f1", "ffn2": "o2", "final": "f2"}


SQ = {item: n for n, item in enumerate(
    [(name, tb) for name in NORMS[:3] for tb in range(TB)]
    + [(name, tb) for tb in range(TB) for name in ("mid", "ffn1")]
    + [(name, tb) for name in NORMS[5:] for tb in range(TB)])}


def unit_width(u):
    if U0["in2"] + 6 <= u < U0["in2"] + 8:
        return 4 * QR
    if U0["in2"] + 8 <= u < U0["uq"]:
        return 4 * (KVR + ROPE)
    if U0["uq"] <= u < U0["ukv"]:
        return 3 * QR
    return UNIT


def work_batches():
    order = [("mix", 0, 0), ("mix", 0, 1), ("mix", 1, 0), ("mix", 1, 1)]
    for k in range(IN_CB):
        if 6 <= k < 14:
            order += [("a", k - 6), ("v", k - 6)]
        if 12 <= k:
            order += [("rv", k - 12)]
        if k in (1, 2, 3, 4, 7, 8):
            order += [("qk", k - 1, tb) for tb in range(TB)]
    order += [("ya", tb, h) for tb in range(TB) for h in range(2)]
    order += [("yr", tb, h) for tb in range(TB) for h in range(2)]
    order += [("m", tb, h) for tb in range(TB) for h in range(2)]
    order += [("mlp", tb, h) for tb in range(TB) for h in range(2)]
    order += [("p",)]
    order += [("ff", i, tb) for i in range(DFF // HALF) for tb in range(TB)]
    order += [("ple", tb, h) for tb in range(TB) for h in range(2)]
    order += [("ffn1", tb, h) for tb in range(TB) for h in range(2)]
    order += [("f1", i, tb) for i in range(FF2 // SUB) for tb in range(TB)]
    order += [("mix2", tb, h) for tb in range(TB) for h in range(2)]
    order += [("mq", tb) for tb in range(TB)] + [("mk", tb) for tb in range(TB)]
    order += pair_batches("b", 0) + pair_batches("b", 1)
    order += [("cq", 0), ("cq", 1), ("ckv",)]
    order += pair_batches("b", 2) + pair_batches("b", 3)
    order += [("q", j) for j in range(MH // 2)] + [("k", j) for j in range(MH // 2)]
    for j in range(MH // 2):
        order += pair_batches("l", j)
    order += [("cat", tb, h) for tb in range(TB) for h in range(2)]
    order += [("ffn2", tb, h) for tb in range(TB) for h in range(2)]
    order += [("f2", i, tb) for i in range(FF2 // SUB) for tb in range(TB)]
    return {name: n for n, name in enumerate(order)}


def pair_batches(kind, j):
    return [(kind + "a", 2 * j), (kind + "a", 2 * j + 1), (kind + "v", 2 * j), (kind + "v", 2 * j + 1)]


def score_maps():
    order = [("d", 0, 0), ("d", 0, 1)]
    for k in range(6, IN_CB):
        if k - 5 < DH:
            order += [("d", k - 5, 0), ("d", k - 5, 1)]
        if 11 <= k < 15:
            order += [("r", k - 11)]
    order += [("b", h) for h in range(BH)] + [("l", h) for h in range(MH)]
    return {name: n for n, name in enumerate(order)}


WB, SM = work_batches(), score_maps()
SRC = {name: 4 * n for n, name in enumerate(["mix", "ya", "m", "mlp", "ple", "ffn1", "mix2", "ffn2", "final"])}
GAIN = {name: 16 * n for n, name in enumerate(["mix", "ret", "mlp", "ple", "ffn1", "mix2"], 1)}
GAIN |= {"c": GAIN["mix2"] + 32, "ffn2": GAIN["mix2"] + 48, "final": GAIN["mix2"] + 64}
SOFT = {("d", h, c): 2 * h + c for h in range(DH) for c in range(2)}
SOFT.update({("b", h): 2 * DH + h for h in range(BH)})
SOFT.update({("l", h): 2 * DH + BH + h for h in range(MH)})
SPLIT = {name: n for n, name in enumerate(
    [x for x in WB if x[0] in ("p", "ya", "yr", "m", "ff", "f1", "f2", "cq", "ckv", "cat", *NORMS)])}


def alibi(h):
    return 2.0 ** (-8.0 * (h + 1) / 8)


def two_blocks(nc, x_d, p_d, g_mix, w_in, lam_q1, lam_k1, lam_q2, lam_k2, g_diff, g_ret, w_bd, w_br, w_out,
               g_mlp, w_ff1, w_ff2, g_ple, w_pg, w_pl, g_fin1, pos_d, g_ffn1, w_g1, w_u1, w_d1, g_mix2,
               w_in2, g_q, w_uq, g_kv, w_ukv, w_out2, g_ffn2, w_g2, w_u2, w_d2, g_final,
               masks_d, decay_d, freq_d, out_d):
    f32, f32r, bf16, i32 = mybir.dt.float32, mybir.dt.float32r, mybir.dt.bfloat16, mybir.dt.int32
    ALU, ACT, AX = mybir.AluOpType, mybir.ActivationFunctionType, mybir.AxisListType

    at = [-(-nc.sbuf_base // 128) * 128]
    named = {}

    def sb(name, shape, dt=f32, where=None):
        size = (2 if dt == bf16 else 4) * int(np.prod(shape[1:]))
        if where is None:
            where = at[0]
            at[0] += -(-size // 32) * 32
        named[name] = where
        return nc.alloc_sbuf_tensor_at(name, shape, dt, offset=where)

    raw = [sb(f"raw{s}", [P, UNIT]) for s in range(RAW_SLOTS)]
    w_lo = [sb(f"w_lo{s}", [P, UNIT], f32r, named[f"raw{s}"]) for s in range(RAW_SLOTS)]
    w_hi = [sb(f"w_hi{s}", [P, UNIT], f32r) for s in range(HI_SLOTS)]
    hA = [sb(f"hA_{s}", [P, KT, SEQ], f32r) for s in ("hi", "lo")]
    hB = [sb(f"hB_{s}", [P, KT, SEQ], f32r) for s in ("hi", "lo")]
    x = sb("x", [P, TB, D])
    src = sb("src", [P, TB, D])
    gain = sb("gain", [P, D])
    junk = sb("junk", [P, D], bf16)
    vjunk = sb("vjunk", [P, P], bf16)
    rjunk = sb("rjunk", [P, RV], bf16)
    masks = sb("masks", [P, P + 2 * 384])
    ident, mask, negdist = masks[:, 0:P], masks[:, P:P + 384], masks[:, P + 384:P + 768]
    ss = sb("ss", [P, 2 * len(NORMS)])
    rs = sb("rs", [P, 2 * len(NORMS)])
    ms = sb("ms", [P, 2 * len(NORMS)])
    rs2 = sb("rs2", [P, TB])
    nhalf = sb("nhalf", [P, 16])
    lam_s = sb("lam_s", [P, 4])
    neglam = sb("neglam", [P, 1])
    ssy, msy, rsy = (sb(n, [P, TB * DH]) for n in ("ssy", "msy", "rsy"))
    ssr, msr, rsr = (sb(n, [P, TB * RH]) for n in ("ssr", "msr", "rsr"))
    ssc, msc, rsc = (sb(n, [P, 4]) for n in ("ssc", "msc", "rsc"))
    mn = sb("mn", [P, 32, TB])
    sm = sb("sm", [P, 32, TB])
    rsm = sb("rsm", [P, 32, TB])
    qc = sb("qc", [P, DH, TB])
    gd = sb("gd", [P, P])
    arena = at[0]

    def lay(start, *parts):
        out = []
        for name, shape, *dt in parts:
            out.append(sb(name, shape, dt[0] if dt else f32, start))
            start += -(-4 * int(np.prod(shape[1:])) // 32) * 32
        assert start <= nc.sbuf_usable_end, (name, start)
        return out

    qaT, kaT, va, qrT, krT, vr, gr, ga, yr, sT0, sT1 = lay(
        arena, ("qaT", [P, DH, SEQ]), ("kaT", [P, DH, SEQ]), ("va", [P, TB, D]), ("qrT", [P, RH, SEQ]),
        ("krT", [P, RH, SEQ]), ("vr", [P, TB, D]), ("gr", [P, TB, D]), ("ga", [P, TB, D]),
        ("yr", [P, TB, D]), ("sT0", [P, 384]), ("sT1", [P, 384]))
    (gg,) = lay(arena, ("gg", [P, TB, D]))
    qk_tm = lay(named["yr"], ("qk_tm0", [P, TB, HALF]), ("qk_tm1", [P, TB, HALF]))
    lam_v, lam_w = lay(named["ga"], ("lam_v", [P, 4, DHD]), ("lam_w", [P, 2, DHD]))
    L, aT0, aT1, bias0, bias1 = lay(named["hB_hi"], ("L", [P, 4, 384]), ("aT0", [P, 384]), ("aT1", [P, 384]),
                                    ("bias0", [P, 384]), ("bias1", [P, 384]))
    decay0, decay1 = lay(named["bias1"] + 4 * 384, ("decay0", [P, 384]), ("decay1", [P, 384]))
    aT, bias, decay, sT = [aT0, aT1], [bias0, bias1], [decay0, decay1], [sT0, sT1]
    fT0, fT1, act_r, act_f, pl_s, sg, pT0, pT1, p_sb, gain_mid = lay(
        arena, ("fT_hi", [P, 4, SEQ], f32r), ("fT_lo", [P, 4, SEQ], f32r), ("act_r", [P, TB, HALF]),
        ("act_f", [P, TB, HALF]), ("pl_s", [P, TB, D]), ("sg", [P, TB, D]),
        ("pT_hi", [P, 2, SEQ], f32r), ("pT_lo", [P, 2, SEQ], f32r), ("p_sb", [P, TB, 256]), ("gain_mid", [P, D]))
    fT, pT = [fT0, fT1], [pT0, pT1]
    (mix_t,) = lay(named["va"], ("mix_t", [P, TB, D]))
    (mq_tm, mk_tm, mv, mqT, mkT, cq, ckv, q_tm, k_tm, v_tm, qT, kT, pos_k, posdist, kr) = lay(
        arena, ("mq_tm", [P, TB, 512]), ("mk_tm", [P, TB, 512]), ("mv", [P, TB, 512]), ("mqT", [P, 4, SEQ]),
        ("mkT", [P, 4, SEQ]), ("cq", [P, TB, QR]), ("ckv", [P, TB, KVR + ROPE]),
        ("q_tm", [P, TB, MH, MQ]), ("k_tm", [P, TB, MH, MQ]), ("v_tm", [P, TB, MH, MV]),
        ("qT", [MQ, MH, SEQ]), ("kT", [MQ, MH, SEQ]), ("pos_k", [P, SEQ]), ("posdist", [P, 384]),
        ("kr", [P, TB, ROPE]))
    (rope_t, rot_t) = lay(named["kr"] + 4 * TB * ROPE, ("rope_t", [P, TB, ROPE]), ("rot_t", [P, TB, MH, ROPE]))
    cos2, sin2, ang, turns_ = lay(named["rot_t"] + 4 * TB * MH * ROPE, ("cos2", [P, TB, ROPE]), ("sin2", [P, TB, ROPE]),
                                  ("ang", [P, TB, 16]), ("turns_", [P, TB, 16]))
    pos_ki, pos_qi, pos_q, freq = lay(named["turns_"] + 4 * TB * 16, ("pos_ki", [P, SEQ], i32), ("pos_qi", [P, TB], i32),
                                      ("pos_q", [P, TB]), ("freq", [P, 16]))

    ctx = ExitStack()
    bank = [ctx.enter_context(nc.psum_tensor(f"bank{i}", [P, HALF], f32)) for i in range(8)]
    acc = lambda tb, c: bank[2 * tb + c]
    proj = lambda cb, tb: bank[2 * (cb % 2) + tb]
    up = lambda tb: bank[4 + tb]
    score = lambda name: bank[4 + SM[name] % 2]
    work = lambda name: bank[6 + WB[name] % 2]

    sems = {}

    def sem(name):
        sems[name] = ctx.enter_context(nc.semaphore(name))
        return sems[name]

    raw_in = [sem(f"raw_in{s}") for s in range(RAW_SLOTS)]
    hi_ready = sem("hi_ready")
    lo_ready = sem("lo_ready")
    unit_used = sem("unit_used")
    x_in = [sem("x_in0"), sem("x_in1")]
    p_in, mask_in, lam_in, gd_in = (sem(n) for n in ("p_in", "mask_in", "lam_in", "gd_in"))
    gain_in = sem("gain_in")
    mid_in, gains_ready = sem("mid_in"), sem("gains_ready")
    rs2_ready = sem("rs2_ready")
    decay_in, pos_in = [sem("decay_in0"), sem("decay_in1")], sem("pos_in")
    square_sum = sem("square_sum")
    rstd_ready = sem("rstd_ready")
    mid_ready = sem("mid_ready")
    src_ready = sem("src_ready")
    work_done = sem("work_done")
    work_out = [sem("work_out0"), sem("work_out1")]
    split_hi = sem("split_hi")
    proj_done, proj_out = sem("proj_done"), sem("proj_out")
    acc_done, acc_out = sem("acc_done"), sem("acc_out")
    up_done, act_ready, up_out = sem("up_done"), sem("act_ready"), sem("up_out")
    score_done, score_out = sem("score_done"), sem("score_out")
    bias_ready = sem("bias_ready")
    exp_ready = sem("exp_ready")
    comb_ready = sem("comb_ready")
    ysq, rsq = sem("ysq"), sem("rsq")
    ystd, rstd_r, cstd = sem("ystd"), sem("rstd_r"), sem("cstd")
    gates_ready = sem("gates_ready")
    gsg_ready = sem("gsg_ready")
    yr_src = sem("yr_src")
    lam_prod, lam_exp, lam_ready = sem("lam_prod"), sem("lam_exp"), sem("lam_ready")
    pl_done, pl_out, pg_sig = sem("pl_done"), sem("pl_out"), sem("pg_sig")
    csq, c_src = sem("csq"), sem("c_src")
    pos_ready, ang_ready, trig_ready = sem("pos_ready"), sem("ang_ready"), sem("trig_ready")
    rsm_ready = sem("rsm_ready")
    rot_ready, kr_ready = sem("rot_ready"), sem("kr_ready")
    k_full = sem("k_full")
    vec_step, act_step, pool_step = sem("vec_step"), sem("act_step"), sem("pool_step")
    out_done = sem("out_done")

    def unit_view(buf, n, cols):
        return buf[:, 0:n * cols].rearrange("p (t n) -> p t n", n=cols)

    block = ctx.enter_context(nc.Block())

    @block.sync
    def _(sp):
        def load(u, pieces, turns=0):
            if u >= RAW_SLOTS:
                sp.wait_ge(unit_used, u - RAW_SLOTS + 1 + 12 * turns)
            for dst, w in pieces:
                sp.dma_start(dst, w).then_inc(raw_in[u % RAW_SLOTS], 16)

        def narrow(u, w, kt0, n, c0, cols, turns=0):
            view = unit_view(raw[u % RAW_SLOTS], n, cols)
            h = -(-n // 2)
            load(u, [(view[:, a:b, :], w[(kt0 + a) * P:(kt0 + b) * P, bass.ds(c0, cols)]
                      .rearrange("(t p) n -> p t n", p=P)) for a, b in ((0, h), (h, n))], turns)

        def wide(u, w, row0, turns=0):
            view = unit_view(raw[u % RAW_SLOTS], 2, D)
            load(u, [(view[:, j, :], w[bass.ds(row0 + j * P, P), :]) for j in range(2)], turns)

        def gate_up(u, w_g, w_u, kt0, c0, turns=0):
            view = unit_view(raw[u % RAW_SLOTS], 4, 2 * SUB)
            load(u, [(view[:, :, s * SUB:(s + 1) * SUB], w[kt0 * P:(kt0 + 4) * P, bass.ds(c0, SUB)]
                      .rearrange("(t p) n -> p t n", p=P)) for s, w in enumerate((w_g, w_u))], turns)

        for cb in range(IN_CB):
            for j in range(2):
                if cb == 0:
                    sp.dma_start(x[:, j, :], x_d[j * P:(j + 1) * P, :]).then_inc(x_in[j], 16)
                narrow(U0["in"] + 2 * cb + j, w_in, 4 * j, 4, cb * HALF, HALF)
        for name, w in (("bd", w_bd), ("br", w_br), ("out", w_out)):
            for j in range(4):
                wide(U0[name] + j, w, 2 * j * P)

        u = U0["ff"]
        for j in range(2):
            narrow(u + j, w_ff1, 4 * j, 4, 0, HALF)

        def ff_step(u, i, turns=0):
            for j in range(2):
                narrow(u + j, w_ff1, 4 * j, 4, i * HALF, HALF, turns)
            for j in range(2):
                wide(u + 2 + j, w_ff2, i * HALF - HALF + 2 * j * P, turns)
        ff_step(u + 2, 1)
        with sp.Fori(0, 2) as r:
            for j in range(3):
                ff_step(u + 6 + 4 * j, 3 * r + 2 + j, r)
        for j in range(2):
            wide(u + 30 + j, w_ff2, DFF - HALF + 2 * j * P)

        wide(U0["pl"], w_pl, 0)
        for j in range(4):
            wide(U0["pg"] + j, w_pg, 2 * j * P)

        def gated(u, w_g, w_u, w_d):
            for j in range(2):
                gate_up(u + j, w_g, w_u, 4 * j, 0)

            def step(i, r=0, turns=0):
                v = u + 2 + 3 * (i - 1)
                for j in range(2):
                    gate_up(v + j, w_g, w_u, 4 * j, r * (4 * SUB) + i * SUB, turns)
                wide(v + 2, w_d, r * (4 * SUB) + (i - 1) * SUB, turns)
            step(1)
            with sp.Fori(0, 2) as r:
                for i in range(2, 6):
                    step(i, r, r)
            step(FF2 // SUB - 1)
            wide(u + 32, w_d, FF2 - SUB)

        gated(U0["f1"], w_g1, w_u1, w_d1)
        for n, (c0, cols) in enumerate(IN2):
            for j in range(2):
                narrow(U0["in2"] + 2 * n + j, w_in2, 4 * j, 4, c0, cols)
        for j in range(2):
            narrow(U0["uq"] + j, w_uq, 0, 3, j * QR, QR)
        wide(U0["ukv"], w_ukv, 0)
        for j in range(4):
            wide(U0["o2"] + j, w_out2, 2 * j * P)
        gated(U0["f2"], w_g2, w_u2, w_d2)

        for tb in range(TB):
            sp.wait_ge(src_ready, SRC["final"] + 2 * tb + 2)
            sp.dma_start(out_d[tb * P:(tb + 1) * P, :], src[:, tb, :]).then_inc(out_done, 16)
        sp.wait_ge(out_done, 16 * TB)

    def rows_of(name):
        kind, b = name[0], work(name)
        if kind == "p":
            return [t[:, :, :] for t in pT], b[:, :].rearrange("p (k t) -> p k t", t=SEQ)
        if kind == "ckv":
            return [t[:, 3:5, :] for t in hA], b[:, :].rearrange("p (k t) -> p k t", t=SEQ)
        if kind in ("ff", "f1", "f2"):
            tb, k0, n, pair = name[2], 0 if kind == "ff" else 2 * (name[1] % 2), 4 if kind == "ff" else 2, fT
        elif kind == "cq":
            tb, k0, n, pair = name[1], 0, 3, hA
        else:
            tb, k0, n, pair = name[1], 4 * name[2], 4, hB if kind in ("ya", "m", "ple", "cat") else hA
        return ([t[:, k0:k0 + n, tb * P:(tb + 1) * P] for t in pair],
                b[:, 0:n * P].rearrange("p (k t) -> p k t", t=P))

    @block.tensor
    def _(pe):
        def product(outs, h, kt, tb, u, col):
            hi, lo = (t[:, kt, tb * P:(tb + 1) * P] for t in h)
            spans = [(o, slice(col + n * HALF, col + n * HALF + o.shape[-1])) for n, o in enumerate(outs)]
            part = {"hi": w_hi[u % HI_SLOTS], "lo": w_lo[u % RAW_SLOTS]}
            return [(o, x_part, part[p][:, c]) for x_part, p in ((hi, "hi"), (hi, "lo"), (lo, "hi"))
                    for o, c in spans]

        def products(outs, h, kt0, n, tb, u, cols, first, last, du=0):
            pe.wait_ge(lo_ready, u + 1 + du)
            for t in range(n):
                todo = product(outs, h, kt0 + t, tb, u, t * cols)
                for m, (o, a, w) in enumerate(todo):
                    mm = pe.matmul(o, a, w, start=first and t == 0 and m < len(outs),
                                   stop=last and t == n - 1 and m >= len(todo) - len(outs))
            return mm

        def work_free(n, dw=0):
            if n >= 2:
                pe.wait_ge(work_out[n % 2], n // 2 + dw)

        def turn(name, blocks, dw=0):
            work_free(WB[name], dw)
            col = 0
            for blk in blocks:
                rows, cols = blk.shape[0], blk.shape[-1]
                mm = pe.transpose(work(name)[0:cols, col:col + rows], blk, ident)
                col += rows
            mm.then_inc(work_done, 1)

        def turned(name, dw=0):
            n = WB[name]
            pe.wait_ge(work_out[n % 2], n // 2 + 1 + dw)

        def turn_rows(name, buf, tb):
            for h in range(2):
                if name in SRC:
                    pe.wait_ge(src_ready, SRC[name] + 2 * tb + h + 1)
                turn((name, tb, h), [buf[:, tb, (4 * h + j) * P:(4 * h + j + 1) * P] for j in range(4)])

        def src_turn(name, tb):
            turn_rows(name, src, tb)

        def narrow_block(out, name, u, tb, cols, middle=None):
            for j in range(2):
                if name:
                    turned((name, tb, j))
                mm = products([out], hA, 4 * j, 4, tb, u + j, cols, j == 0, j == 1)
                if tb:
                    mm.then_inc(unit_used, 1)
                if middle and j == 0:
                    middle()
            return mm

        def scores(name, q, k, h):
            m, b = SM[name], score(name)
            if m >= 2:
                pe.wait_ge(score_out, m - 1)
            pe.matmul(b[:, 0:P], q[:, h, 0:P], k[:, h, 0:P], start=True, stop=True)
            pe.matmul(b[:, P:384], q[:, h, P:SEQ], k[:, h, :], start=True, stop=True).then_inc(score_done, 1)

        def diff_scores(h):
            for c in range(2):
                half = slice(c * DHD, (c + 1) * DHD)
                scores(("d", h, c), qaT[half], kaT[half], h)

        def apply_weights(name, a, v, cols):
            b = work(name)
            work_free(WB[name])
            pe.matmul(b[:, 0:cols], a[:, 0:P], v[0], start=True, stop=True)
            pe.matmul(b[:, cols:2 * cols], a[:, P:2 * P], v[0], start=True, stop=False)
            pe.matmul(b[:, cols:2 * cols], a[:, 2 * P:384], v[1], start=False, stop=True).then_inc(work_done, 1)

        def diff_turn(h):
            pe.wait_ge(comb_ready, h + 1)
            w = L[:, SOFT["d", h, 1] % 4, :]
            turn(("a", h), [w[:, j * P:(j + 1) * P] for j in range(3)])

        def diff_out(h):
            pe.wait_ge(proj_out, 12)
            turned(("a", h))
            apply_weights(("v", h), aT[h % 2], [va[:, tb, h * P:(h + 1) * P] for tb in range(TB)], P)

        def ret_scores(h):
            if h == 0:
                turned(("qk", 6, 1))
                turned(("qk", 7, 1))
            pe.wait_ge(score_out, SM["r", h] - 1)
            b = score(("r", h))
            pe.matmul(b[:, 0:SEQ], krT[:, h, 0:P], qrT[:, h, :], start=True, stop=True)
            pe.matmul(b[:, SEQ:384], krT[:, h, P:SEQ], qrT[:, h, P:SEQ], start=True, stop=True)\
              .then_inc(score_done, 1)

        def ret_out(h):
            pe.wait_ge(score_out, SM["r", h] + 1)
            pe.wait_ge(proj_out, 20)
            apply_weights(("rv", h), sT[h % 2], [vr[:, tb, h * RV:(h + 1) * RV] for tb in range(TB)], RV)

        pe.wait_ge(mask_in, 16)
        for cb in range(IN_CB):
            u = U0["in"] + 2 * cb
            if cb >= 2:
                pe.wait_ge(proj_out, 2 * cb - 2)
            if cb == 0:
                src_turn("mix", 0)
                narrow_block(proj(cb, 0)[:, :], "mix", u, 0, HALF, lambda: src_turn("mix", 1)).then_inc(proj_done, 1)
                narrow_block(proj(cb, 1)[:, :], "mix", u, 1, HALF)
            else:
                for j in range(2):
                    for tb in range(TB):
                        mm = products([proj(cb, tb)[:, :]], hA, 4 * j, 4, tb, u + j, HALF, j == 0, j == 1)
                        if j and tb == 0:
                            mm.then_inc(proj_done, 1)
                    mm.then_inc(unit_used, 1)
            if cb == 5:
                turned(("qk", 3, 0))
                turned(("qk", 3, 1))
                diff_scores(0)
            if 6 <= cb < 14:
                diff_turn(cb - 6)
                if cb < 13:
                    diff_scores(cb - 5)
                diff_out(cb - 6)
            if cb >= 12:
                ret_out(cb - 12)
            if 11 <= cb < 15:
                ret_scores(cb - 11)
            if cb in (1, 2, 3, 4, 7, 8):
                pe.wait_ge(proj_out, 2 * cb)
                for tb in range(TB):
                    turn(("qk", cb - 1, tb),
                         [qk_tm[(cb - 1) % 2][:, tb, j * P:(j + 1) * P] for j in range(4)])

        def acc_free(name, tb):
            if n := 2 * ACC[name]:
                pe.wait_ge(acc_out, n - 1 + tb)

        def unit(h, u0, j, tb):
            return products([acc(tb, c)[:, :] for c in range(2)], h, 2 * j, 2, tb, u0 + j, D, j == 0, j == 3)

        def square_product(name, h, u0, operand, before=None, steps=()):
            steps = dict(steps)
            for tb in range(TB):
                acc_free(name, tb)
                for j in range(4):
                    if j % 2 == 0:
                        turned((operand, tb, j // 2))
                    if j == 0 and before:
                        before(tb)
                    mm = unit(h, u0, j, tb)
                    if tb:
                        mm.then_inc(unit_used, 1)
                    elif j == 3:
                        mm.then_inc(acc_done, 1)
                    if (tb, j) in steps:
                        steps[tb, j]()

        def yr_turn(tb):
            pe.wait_ge(yr_src, tb + 1)
            turn_rows("yr", yr, tb)

        pe.wait_ge(proj_out, 2 * IN_CB)
        src_turn("ya", 0)
        square_product("bd", hB, U0["bd"], "ya",
                       steps={(0, 1): lambda: src_turn("ya", 1), (1, 1): lambda: yr_turn(0)})
        square_product("br", hA, U0["br"], "yr", steps={(0, 1): lambda: yr_turn(1)})
        src_turn("m", 0)
        square_product("out", hB, U0["out"], "m", steps={(0, 2): lambda: src_turn("m", 1)})

        def ff_up0(u0, norm):
            src_turn(norm, 0)
            narrow_block(up(0)[:, :], norm, u0, 0, HALF, lambda: src_turn(norm, 1)).then_inc(up_done, 1)
            narrow_block(up(1)[:, :], norm, u0, 1, HALF)

        def ff_turn(name, i, done, cols, di=0, blocks=range(TB)):
            for tb in blocks:
                pe.wait_ge(up_out, done - 1 + tb + 2 * di)
                turn((name, i, tb), [act_f[:, tb, j * P:(j + 1) * P] for j in range(cols // P)], di)

        def ff_up(u, name, i, steps, cols, du=0, di=0):
            pe.wait_ge(up_out, 2 * steps + 2 * di)
            for j in range(2):
                for tb in range(TB):
                    mm = products([up(tb)[:, :]], hA, 4 * j, 4, tb, u + j, HALF, j == 0, j == 1, du)
                    if j and tb == 0:
                        mm.then_inc(up_done, 1)
                mm.then_inc(unit_used, 1)
                if j == 0:
                    ff_turn(name, i - 1, 2 * steps, cols, di)

        u = U0["ff"]
        ff_up0(u, "mlp")
        pe.wait_ge(p_in, 16)
        turn(("p",), [p_sb[:, tb, k * P:(k + 1) * P] for k in range(2) for tb in range(TB)])

        def relu_step(i, r=0, start=False):
            v = U0["ff"] + 2 + 4 * (i - 1)
            ff_up(v, "ff", i, i, HALF, 12 * r, 3 * r)
            for j in range(2):
                for tb in range(TB):
                    if j == 0:
                        turned(("ff", i - 1, tb), 3 * r)
                    if start and j == 0:
                        acc_free("ff", tb)
                    mm = products([acc(tb, c)[:, :] for c in range(2)], fT, 2 * j, 2, tb, v + 2 + j, D,
                                  start and j == 0, False, 12 * r)
                mm.then_inc(unit_used, 1)
        relu_step(1, start=True)
        with pe.Fori(0, 2) as r:
            for j in range(3):
                relu_step(2 + j, r)
        last = DFF // HALF - 1
        ff_turn("ff", last, 2 * (last + 1), HALF)
        for tb in range(TB):
            turned(("ff", last, tb))
            for j in range(2):
                mm = products([acc(tb, c)[:, :] for c in range(2)], fT, 2 * j, 2, tb, u + 30 + j, D, False, j == 1)
                if tb:
                    mm.then_inc(unit_used, 1)
            if tb == 0:
                mm.then_inc(acc_done, 1)

        for tb in range(TB):
            if tb:
                pe.wait_ge(acc_out, 2 * ACC["ff"] + 2)
            turned(("p",))
            outs = [bank[(4, 2)[tb] + c][:, :] for c in range(2)]
            mm = products(outs, pT, 0, 2, tb, U0["pl"], D, True, True)
            mm.then_inc(unit_used if tb else pl_done, 1)

        src_turn("ple", 0)
        square_product("pg", hB, U0["pg"], "ple",
                       before=lambda tb: tb and pe.wait_ge(pl_out, 2),
                       steps={(0, 1): lambda: src_turn("ple", 1)})

        def gated(name, norm, base):
            u, n = U0[name], FF2 // SUB
            ff_up0(u, norm)

            def down(v, i, tb, r=0, first=False, last=False):
                turned((name, i, tb), 4 * r)
                return products([acc(tb, c)[:, :] for c in range(2)], fT, 2 * (i % 2), 2, tb, v, D, first, last,
                                12 * r)

            def step(i, r=0):
                v = u + 2 + 3 * (i - 1)
                ff_up(v, name, i, base + i, SUB, 12 * r, 4 * r)
                for tb in range(TB):
                    if i == 1:
                        acc_free(name, tb)
                    mm = down(v + 2, i - 1, tb, r, i == 1)
                mm.then_inc(unit_used, 1)
            step(1)
            with pe.Fori(0, 2) as r:
                for i in range(2, 6):
                    step(i, r)
            v, i = u + 2 + 3 * (n - 2), n - 1
            pe.wait_ge(up_out, 2 * (base + i))
            narrow_block(up(0)[:, :], None, v, 0, HALF, lambda: ff_turn(name, i - 1, 2 * (base + i), SUB))\
                .then_inc(up_done, 1)
            narrow_block(up(1)[:, :], None, v, 1, HALF, lambda: ff_turn(name, i, 2 * (base + n), SUB, blocks=(0,)))
            down(v + 2, i - 1, 0)
            ff_turn(name, i, 2 * (base + n), SUB, blocks=(1,))
            down(v + 3, i, 0, last=True).then_inc(acc_done, 1)
            down(v + 2, i - 1, 1).then_inc(unit_used, 1)
            down(v + 3, i, 1, last=True).then_inc(unit_used, 1)

        gated("f1", "ffn1", DFF // HALF)

        def pair_scores(kind, j):
            for h in (2 * j, 2 * j + 1):
                if kind == "b":
                    half = slice(h % 2 * BD, h % 2 * BD + BD)
                    scores(("b", h), mqT[half], mkT[half], h // 2)
                else:
                    scores(("l", h), qT, kT, h)

        def pair(kind, j):
            for h in (2 * j, 2 * j + 1):
                m = SOFT[kind, h]
                pe.wait_ge(exp_ready, m + 1)
                turn((kind + "a", h), [L[:, m % 4, b * P:(b + 1) * P] for b in range(3)])
            if 2 * j + 2 < BH:
                pair_scores(kind, j + 1)
            for h in (2 * j, 2 * j + 1):
                turned((kind + "a", h))
                v = [mv[:, tb, h * BD:(h + 1) * BD] if kind == "b" else v_tm[:, tb, h, :] for tb in range(TB)]
                apply_weights((kind + "v", h), aT[h % 2], v, BD)

        for n, (_, cols) in enumerate(IN2):
            cb, u = CB_IN2 + n, U0["in2"] + 2 * n
            if n >= 2:
                pe.wait_ge(proj_out, 2 * cb - 2)
            if n == 0:
                src_turn("mix2", 0)
                pe.wait_ge(acc_out, 2 * ACC["f1"] + 1)
                narrow_block(proj(cb, 0)[:, :], "mix2", u, 0, cols, lambda: src_turn("mix2", 1))\
                    .then_inc(proj_done, 1)
                pe.wait_ge(acc_out, 2 * ACC["f1"] + 2)
                narrow_block(proj(cb, 1)[:, :], "mix2", u, 1, cols)
            else:
                for j in range(2):
                    for tb in range(TB):
                        mm = products([proj(cb, tb)[:, 0:cols]], hA, 4 * j, 4, tb, u + j, cols, j == 0, j == 1)
                        if j and tb == 0:
                            mm.then_inc(proj_done, 1)
                    mm.then_inc(unit_used, 1)
            if n in (1, 2):
                name, buf = (("mq", mq_tm), ("mk", mk_tm))[n - 1]
                pe.wait_ge(proj_out, 2 * cb)
                for tb in range(TB):
                    turn((name, tb), [buf[:, tb, b * P:(b + 1) * P] for b in range(4)])
            if n == 3:
                for tb in range(TB):
                    turned(("mk", tb))
                pair_scores("b", 0)
            if n == 4:
                pe.wait_ge(proj_out, 2 * (CB_IN2 + 3))
                pair("b", 0)
        pair("b", 1)

        pe.wait_ge(c_src, 4)
        for tb in range(TB):
            turn(("cq", tb), [cq[:, tb, k * P:(k + 1) * P] for k in range(3)])
        turn(("ckv",), [ckv[:, tb, k * P:(k + 1) * P] for k in range(2) for tb in range(TB)])
        for n in range(2):
            cb = CB_UQ + n
            pe.wait_ge(proj_out, 2 * cb - 2)
            for tb in range(TB):
                turned(("cq", tb))
                mm = products([proj(cb, tb)[:, 0:QR]], hA, 0, 3, tb, U0["uq"] + n, QR, True, True)
                mm.then_inc(unit_used if tb else proj_done, 1)
        pair("b", 2)
        pe.wait_ge(proj_out, 2 * CB_UKV)
        turned(("ckv",))
        for tb in range(TB):
            mm = products([acc(tb, c)[:, :] for c in range(2)], [t[:, 3:5, :] for t in hA], 0, 2, tb, U0["ukv"], D,
                          True, True)
            mm.then_inc(unit_used if tb else proj_done, 1)
        pair("b", 3)
        pe.wait_ge(rot_ready, 1)
        for j in range(MH // 2):
            turn(("q", j), [q_tm[:, tb, h, :] for h in (2 * j, 2 * j + 1) for tb in range(TB)])
        pe.wait_ge(k_full, 1)
        for j in range(MH // 2):
            turn(("k", j), [k_tm[:, tb, h, :] for h in (2 * j, 2 * j + 1) for tb in range(TB)])
        turned(("k", MH // 2 - 2))
        turned(("k", MH // 2 - 1))
        pair_scores("l", 0)
        for j in range(MH // 2):
            pair("l", j)

        turned(("lv", MH - 2))
        turned(("lv", MH - 1))
        turn_rows("cat", src, 0)
        pe.wait_ge(proj_out, 2 * CB_UKV + 2)
        square_product("o2", hB, U0["o2"], "cat", steps={(0, 1): lambda: turn_rows("cat", src, 1)})
        gated("f2", "ffn2", DFF // HALF + FF2 // SUB)

    @block.scalar
    def _(act):
        def hi(u, turns=0):
            if u >= N_UNITS:
                return
            if u >= HI_SLOTS:
                act.wait_ge(unit_used, u - HI_SLOTS + 1 + 12 * turns)
            act.wait_ge(raw_in[u % RAW_SLOTS], 32 * (u // RAW_SLOTS + 1) + 64 * turns)
            w = unit_width(u)
            act.activation(w_hi[u % HI_SLOTS][:, 0:w], raw[u % RAW_SLOTS][:, 0:w], ACT.Copy).then_inc(hi_ready, 1)

        def split(name, di=0):
            act.wait_ge(work_done, WB[name] + 1 + 2 * di)
            (dst, _), b = rows_of(name)
            act.activation(dst, b, ACT.Copy).then_inc(split_hi, 1)

        def split_rows(name, tb):
            for h in range(2):
                split((name, tb, h))

        def squares(name, tb):
            n = SQ[name, tb]
            if name == "mix":
                act.wait_ge(x_in[tb], 16)
            elif name == "ffn1":
                act.wait_ge(mid_ready, tb + 1)
            else:
                act.wait_ge(acc_out, 2 * ACC[NORM_X[name]] + tb + 1)
            if n:
                act.wait_ge(square_sum, n)
            act.activation(junk[:, :], x[:, tb, :], ACT.Square, accum_out=ss[:, n:n + 1]).then_inc(square_sum, 1)

        def inv_rms(name, tb):
            n = SQ[name, tb]
            act.wait_ge(rstd_ready, n + 1)
            return rs[:, n:n + 1]

        def proj_ready(cb, tb, last_unit):
            if tb == 0:
                act.wait_ge(proj_done, cb + 1)
            else:
                act.wait_ge(unit_used, last_unit + 1)

        def proj_copy(cb):
            dst = [(qk_tm[cb % 2], 0)] * 4 + [(va, 0), (va, HALF)] + [(qk_tm[cb % 2], 0)] * 2
            dst += [(b, c) for b in (vr, gr, ga, gg) for c in (0, HALF)]
            buf, c0 = dst[cb]
            for tb in range(TB):
                proj_ready(cb, tb, U0["in"] + 2 * cb + 1)
                act.activation(buf[:, tb, c0:c0 + HALF], proj(cb, tb)[:, :], ACT.Copy, scale=inv_rms("mix", tb))\
                   .then_inc(proj_out, 1)

        def exps(m, ready):
            act.wait_ge(score_out, ready + 1)
            for tb, c in enumerate((slice(0, P), slice(P, 384))):
                e = act.activation(L[:, m % 4, c], L[:, m % 4, c], ACT.Exp, bias=mn[:, m, tb:tb + 1], scale=-1.0,
                                   accum_out=sm[:, m, tb:tb + 1])
            e.then_inc(exp_ready, 1)

        def weights_copy(name, h):
            n = WB[name, h]
            act.wait_ge(work_done, n + 1)
            act.activation(aT[h % 2][:, :], work((name, h))[:, 0:384], ACT.Copy).then_inc(work_out[n % 2], 1)

        def diff_y(h):
            n = WB["v", h]
            act.wait_ge(work_done, n + 1)
            for tb in range(TB):
                y = act.activation(src[:, tb, h * P:(h + 1) * P], work(("v", h))[:, tb * P:(tb + 1) * P], ACT.Copy,
                                   scale=rsm[:, 2 * h, tb:tb + 1])
            y.then_inc(work_out[n % 2], 1)

        def ret_y(h):
            n = WB["rv", h]
            act.wait_ge(work_done, n + 1)
            act.activation(yr[:, :, h * RV:(h + 1) * RV], work(("rv", h))[:, :].rearrange("p (t n) -> p t n", n=RV),
                           ACT.Copy).then_inc(work_out[n % 2], 1)

        act.dma_start(masks[:, :], masks_d).then_inc(mask_in, 16)
        for n, lam in enumerate((lam_q1, lam_k1, lam_q2, lam_k2)):
            act.dma_start(lam_v[:, n, :], lam[0].partition_broadcast(P)).then_inc(lam_in, 16)
        squares("mix", 0)
        split_rows("mix", 0)
        hi(0)
        squares("mix", 1)
        hi(1)
        split_rows("mix", 1)
        hi(2)
        act.wait_ge(lam_prod, 2)
        act.activation(lam_s[:, 2:4], lam_s[:, 0:2], ACT.Exp).then_inc(lam_exp, 1)
        for k in range(IN_CB + 1):
            step = k - 1
            if 6 <= step < 14:
                weights_copy("a", step - 6)
            if step >= 0:
                proj_copy(step)
            if k < IN_CB:
                hi(2 * k + 3)
            if 6 <= step < 14:
                diff_y(step - 6)
            if step >= 12:
                ret_y(step - 12)
            if 5 <= step < 13:
                for c in range(2):
                    exps(SOFT["d", step - 5, c], SM["d", step - 5, c])
            if k == 14:
                act.wait_ge(proj_out, 24)
                act.activation(gr[:, :, :], gr[:, :, :], ACT.Silu).then_inc(gates_ready, 1)
            if k < IN_CB:
                hi(2 * k + 4)
        for tb in range(TB):
            split_rows("ya", tb)
        act.wait_ge(proj_out, 2 * IN_CB)
        act.activation(ga[:, :, :], ga[:, :, :], ACT.Sigmoid).then_inc(gates_ready, 1)
        hi(35)
        act.activation(gg[:, :, :], gg[:, :, :], ACT.Sigmoid).then_inc(gates_ready, 1)
        hi(36)
        split_rows("yr", 0)
        for n in range(37, 40):
            hi(n)
        split_rows("yr", 1)
        for n in range(40, 43):
            hi(n)
        split_rows("m", 0)
        hi(43)
        split_rows("m", 1)
        hi(44)
        squares("mlp", 0)
        hi(45)
        hi(46)
        split_rows("mlp", 0)
        squares("mlp", 1)
        split_rows("mlp", 1)
        hi(47)

        def step_ready(i, tb, last_unit, di=0, du=0):
            if tb == 0:
                act.wait_ge(up_done, i + 1 + di)
            else:
                act.wait_ge(unit_used, last_unit + 1 + du)

        def relu(i, tb, r=0):
            step_ready(i, tb, U0["ff"] + 1 + (4 * i - 2 if i else 0), 3 * r, 12 * r)
            act.activation(act_r[:, tb, :], up(tb)[:, :], ACT.Relu, scale=rs2[:, tb:tb + 1]).then_inc(act_ready, 1)

        act.wait_ge(rs2_ready, 1)
        relu(0, 0)
        hi(48)
        relu(0, 1)
        split(("p",))

        def relu_step(i, r=0):
            v = U0["ff"] + 2 + 4 * (i - 1)
            hi(v + 3, r)
            for tb in range(TB):
                split(("ff", i - 1, tb), 3 * r)
            hi(v + 4, r)
            for tb in range(TB):
                relu(i, tb, r)
            hi(v + 5, r)
            hi(v + 6, r)
        relu_step(1)
        with act.Fori(0, 2) as r:
            for j in range(3):
                relu_step(2 + j, r)
        for tb in range(TB):
            split(("ff", 7, tb))
        hi(77)
        squares("ple", 0)
        hi(78)
        hi(79)
        squares("ple", 1)
        for tb in range(TB):
            if tb == 0:
                act.wait_ge(pl_done, 1)
            else:
                split_rows("ple", 0)
                act.wait_ge(unit_used, U0["pl"] + 1)
            for c in range(2):
                mm = act.activation(pl_s[:, tb, c * HALF:(c + 1) * HALF], bank[(4, 2)[tb] + c][:, :], ACT.Copy)
            mm.then_inc(pl_out, 1)
        hi(80)
        split_rows("ple", 1)
        hi(81)
        for tb in range(TB):
            if tb == 0:
                act.wait_ge(acc_done, ACC["pg"] + 1)
            else:
                act.wait_ge(unit_used, U0["pg"] + 4)
            scale = inv_rms("ple", tb)
            for c in range(2):
                s = act.activation(sg[:, tb, c * HALF:(c + 1) * HALF], acc(tb, c)[:, :], ACT.Sigmoid, scale=scale)
            s.then_inc(pg_sig, 1)
            if tb == 0:
                squares("mid", 0)
                hi(82)
                squares("ffn1", 0)
                hi(83)
                split_rows("ffn1", 0)
        hi(84)
        squares("mid", 1)
        split_rows("ffn1", 1)
        squares("ffn1", 1)

        def gated(name, norm, base):
            u, n = U0[name], FF2 // SUB

            def silu(i, tb, r=0):
                step_ready(base + i, tb, u + 1 + (3 * i - 1 if i else 0), 4 * r, 12 * r)
                act.activation(act_r[:, tb, 0:SUB], up(tb)[:, 0:SUB], ACT.Silu, scale=inv_rms(norm, tb))\
                   .then_inc(act_ready, 1)

            silu(0, 0)
            hi(u + 4)
            silu(0, 1)

            def step(i, r=0):
                v = u + 2 + 3 * (i - 1)
                hi(v + 3, r)
                for tb in range(TB):
                    split((name, i - 1, tb), 4 * r)
                hi(v + 4, r)
                for tb in range(TB):
                    silu(i, tb, r)
                hi(v + 5, r)
            step(1)
            with act.Fori(0, 2) as r:
                for i in range(2, 6):
                    step(i, r)
            v, i = u + 2 + 3 * (n - 2), n - 1
            for tb in range(TB):
                split((name, i - 1, tb))
            hi(v + 3)
            silu(i, 0)
            split((name, i, 0))
            hi(v + 4)
            silu(i, 1)
            split((name, i, 1))
            hi(v + 5)

        gated("f1", "ffn1", DFF // HALF)

        def in2_copy(n):
            buf, cols = [(mq_tm, 512), (mk_tm, 512), (mv, 512), (cq, QR), (ckv, KVR + ROPE)][n]
            for tb in range(TB):
                proj_ready(CB_IN2 + n, tb, U0["in2"] + 2 * n + 1)
                act.activation(buf[:, tb, :], proj(CB_IN2 + n, tb)[:, 0:cols], ACT.Copy, scale=inv_rms("mix2", tb))\
                   .then_inc(proj_out, 1)

        def head_y(kind, h):
            n, m = WB[kind + "v", h], SOFT[kind, h]
            act.wait_ge(work_done, n + 1)
            act.wait_ge(rsm_ready, m - 2 * DH + 1)
            c0 = (h + (MH if kind == "b" else 0)) * BD
            for tb in range(TB):
                y = act.activation(src[:, tb, c0:c0 + BD], work((kind + "v", h))[:, tb * BD:(tb + 1) * BD], ACT.Copy,
                                   scale=rsm[:, m, tb:tb + 1])
            y.then_inc(work_out[n % 2], 1)

        def pair(kind, j):
            for h in (2 * j, 2 * j + 1):
                weights_copy(kind + "a", h)
            for h in (2 * j, 2 * j + 1):
                head_y(kind, h)
            if 2 * j + 2 < BH:
                for h in (2 * j + 2, 2 * j + 3):
                    exps(SOFT[kind, h], SM[kind, h])

        squares("mix2", 0)
        hi(116)
        split_rows("mix2", 0)
        hi(117)
        squares("mix2", 1)
        split_rows("mix2", 1)
        for n in range(1, 5):
            in2_copy(n - 1)
            hi(116 + 2 * n)
            if n == 1:
                act.wait_ge(ang_ready, 1)
                act.activation(sin2[:, :, 16:32], sin2[:, :, 16:32], ACT.Sin).then_inc(trig_ready, 1)
                act.activation(cos2[:, :, 0:16], cos2[:, :, 0:16], ACT.Sin).then_inc(trig_ready, 1)
            if n == 4:
                for h in range(2):
                    exps(SOFT["b", h], SM["b", h])
            hi(117 + 2 * n)
        in2_copy(4)
        hi(126)
        act.wait_ge(proj_out, 2 * (CB_IN2 + 5))
        for tb in range(TB):
            for n, (buf, cols) in enumerate(((cq, QR), (ckv, KVR))):
                k = 2 * n + tb
                if tb or n:
                    act.wait_ge(csq, 2 * tb + n)
                act.activation(junk[:, 0:cols], buf[:, tb, 0:cols], ACT.Square, accum_out=ssc[:, k:k + 1])\
                   .then_inc(csq, 1)
        pair("b", 0)
        pair("b", 1)
        split(("cq", 0))
        split(("cq", 1))
        split(("ckv",))
        act.wait_ge(cstd, 1)
        for n in range(2):
            for tb in range(TB):
                proj_ready(CB_UQ + n, tb, U0["uq"] + n)
                act.activation(q_tm[:, tb, 4 * n:4 * n + 4, :],
                               proj(CB_UQ + n, tb)[:, 0:QR].rearrange("p (h c) -> p h c", c=MQ), ACT.Copy,
                               scale=rsc[:, tb:tb + 1])\
                   .then_inc(proj_out, 1)
            hi(127 + n)
        pair("b", 2)
        for tb in range(TB):
            proj_ready(CB_UKV, tb, U0["ukv"])
            for c in range(2):
                heads = acc(tb, c)[:, :].rearrange("p (h c) -> p h c", c=NOPE + MV)
                act.activation(k_tm[:, tb, 4 * c:4 * c + 4, 0:NOPE], heads[:, :, 0:NOPE], ACT.Copy,
                               scale=rsc[:, 2 + tb:3 + tb])
                kv = act.activation(v_tm[:, tb, 4 * c:4 * c + 4, :], heads[:, :, NOPE:NOPE + MV], ACT.Copy,
                                    scale=rsc[:, 2 + tb:3 + tb])
            kv.then_inc(proj_out, 1)
        hi(129)
        act.wait_ge(kr_ready, 1)
        for tb in range(TB):
            k = act.activation(k_tm[:, tb, :, NOPE:MQ], kr[:, tb, :].unsqueeze(1).to_broadcast([P, MH, ROPE]), ACT.Copy)
        k.then_inc(k_full, 1)
        pair("b", 3)
        for name, buf in (("q", qT), ("k", kT)):
            for j in (1, 3):
                n = WB[name, j]
                act.wait_ge(work_done, n + 1)
                act.activation(buf[:, 2 * j:2 * j + 2, :],
                               work((name, j))[0:MQ, :].rearrange("p (h t) -> p h t", t=SEQ), ACT.Copy)\
                   .then_inc(work_out[n % 2], 1)
        for h in range(2):
            exps(SOFT["l", h], SM["l", h])
        for j in range(MH // 2):
            pair("l", j)
        hi(130)
        for tb in range(TB):
            split_rows("cat", tb)
        hi(131)
        hi(132)
        hi(133)
        squares("ffn2", 0)
        split_rows("ffn2", 0)
        hi(134)
        squares("ffn2", 1)
        split_rows("ffn2", 1)
        gated("f2", "ffn2", DFF // HALF + FF2 // SUB)
        for tb in range(TB):
            squares("final", tb)

    @block.vector
    def _(vec):
        chain = [0]

        def link(ins):
            chain[0] += 1
            ins.then_inc(vec_step, 1)
            vec.wait_ge(vec_step, chain[0])

        def lo(u, du=0):
            if u >= N_UNITS:
                return
            vec.wait_ge(hi_ready, u + 1 + du)
            w = unit_width(u)
            vec.tensor_tensor(w_lo[u % RAW_SLOTS][:, 0:w], raw[u % RAW_SLOTS][:, 0:w],
                              w_hi[u % HI_SLOTS][:, 0:w].bitcast(f32), ALU.subtract).then_inc(lo_ready, 1)

        def split(name, di=0):
            vec.wait_ge(split_hi, SPLIT[name] + 1 + 2 * di)
            (hi, dst), b = rows_of(name)
            vec.tensor_tensor(dst, b, hi.bitcast(f32), ALU.subtract).then_inc(work_out[WB[name] % 2], 1)

        def split_rows(name, tb):
            for h in range(2):
                split((name, tb, h))

        def sums_ready(name, tb):
            if tb == 0:
                vec.wait_ge(acc_done, ACC[name] + 1)
            else:
                vec.wait_ge(unit_used, U0[name] + dict(UNITS)[name])

        def by_gain(name, tb, c):
            cols = slice(c * HALF, (c + 1) * HALF)
            vec.wait_ge(gain_in, GAIN[name])
            vec.tensor_tensor(src[:, tb, cols], x[:, tb, cols], gain[:, cols], ALU.mult).then_inc(src_ready, 1)

        def x_add(name, tb, scale, norm):
            sums_ready(name, tb)
            for c in range(2):
                xs = x[:, tb, c * HALF:(c + 1) * HALF]
                a = vec.scalar_tensor_tensor(out=xs, in0=acc(tb, c)[:, :], scalar=scale, in1=xs,
                                             op0=ALU.mult, op1=ALU.add)
                if c == 0:
                    link(a)
                else:
                    a.then_inc(acc_out, 1)
                    vec.wait_ge(acc_out, 2 * ACC[name] + tb + 1)
                by_gain(norm, tb, c)

        def logits(name, b, scale):
            m = SOFT[name]
            vec.wait_ge(score_done, SM[name] + 1)
            for tb, c in enumerate((slice(0, P), slice(P, 384))):
                t = vec.tensor_tensor_reduce(out=L[:, m % 4, c], in0=score(name)[:, c], in1=b[:, c], scale=-scale,
                                             scalar=3e38, op0=ALU.add, op1=ALU.min, accum_out=mn[:, m, tb:tb + 1])
            t.then_inc(score_out, 1)

        def diff_logits(h):
            vec.wait_ge(bias_ready, h + 1)
            for c in range(2):
                logits(("d", h, c), bias[h % 2], DHD ** -0.5)

        def combine(h):
            m = 2 * h
            vec.wait_ge(exp_ready, m + 2)
            link(vec.reciprocal(rsm[:, m:m + 2, :], sm[:, m:m + 2, :]))
            link(vec.scalar_tensor_tensor(out=qc[:, h, :], in0=rsm[:, m + 1, :], scalar=neglam[:, 0:1],
                                          in1=sm[:, m, :], op0=ALU.mult, op1=ALU.mult))
            for tb, c in enumerate((slice(0, P), slice(P, 384))):
                t = vec.scalar_tensor_tensor(out=L[:, (m + 1) % 4, c], in0=L[:, (m + 1) % 4, c],
                                             scalar=qc[:, h, tb:tb + 1], in1=L[:, m % 4, c],
                                             op0=ALU.mult, op1=ALU.add)
            t.then_inc(comb_ready, 1)

        def head_squares(name, h, buf, width, heads, sums, counter, scratch):
            n = WB[name, h]
            vec.wait_ge(work_out[n % 2], n // 2 + 1)
            for tb in range(TB):
                y = buf[:, tb, h * width:(h + 1) * width]
                k = 2 * h + tb
                if k:
                    vec.wait_ge(counter, k)
                vec.tensor_tensor_reduce(out=scratch[:, 0:width], in0=y, in1=y, scale=1.0, scalar=0.0, op0=ALU.mult,
                                         op1=ALU.add, accum_out=sums[:, tb * heads + h:tb * heads + h + 1])\
                   .then_inc(counter, 1)

        for tb in range(TB):
            vec.wait_ge(x_in[tb], 16)
            for c in range(2):
                by_gain("mix", tb, c)
            if tb == 0:
                split_rows("mix", 0)
            lo(tb)
        split_rows("mix", 1)
        lo(2)
        vec.wait_ge(lam_in, 64)
        for n in range(2):
            vec.tensor_tensor_reduce(out=lam_w[:, n, :], in0=lam_v[:, 2 * n, :], in1=lam_v[:, 2 * n + 1, :], scale=1.0,
                                     scalar=0.0, op0=ALU.mult, op1=ALU.add, accum_out=lam_s[:, n:n + 1])\
               .then_inc(lam_prod, 1)
        vec.wait_ge(lam_exp, 1)
        link(vec.tensor_tensor(lam_s[:, 0:1], lam_s[:, 3:4], lam_s[:, 2:3], ALU.subtract))
        link(vec.tensor_scalar(neglam[:, :], lam_s[:, 0:1], -LAM_INIT, None, ALU.add))
        for k in range(IN_CB):
            step = k - 1
            if 5 <= step < 13:
                diff_logits(step - 5)
            if 11 <= step < 15:
                h = step - 11
                vec.wait_ge(decay_in[h % 2], 16 * (h // 2 + 1))
                vec.wait_ge(score_done, SM["r", h] + 1)
                vec.tensor_tensor(sT[h % 2][:, :], score(("r", h))[:, 0:384], decay[h % 2][:, :], ALU.mult)\
                   .then_inc(score_out, 1)
            if step in (1, 2, 3, 4, 7, 8):
                cb = step - 1
                dst, b0 = {0: (qaT, 0), 1: (qaT, 4), 2: (kaT, 0), 3: (kaT, 4), 6: (qrT, 0), 7: (krT, 0)}[cb]
                for tb in range(TB):
                    n = WB["qk", cb, tb]
                    vec.wait_ge(work_done, n + 1)
                    vec.tensor_copy(dst[:, b0:b0 + 4, tb * P:(tb + 1) * P],
                                    bank[6 + n % 2][:, :].rearrange("p (b t) -> p b t", t=P))\
                       .then_inc(work_out[n % 2], 1)
            lo(2 * k + 3)
            if 6 <= step < 14:
                head_squares("v", step - 6, src, P, DH, ssy, ysq, vjunk)
            if step >= 12:
                head_squares("rv", step - 12, yr, RV, RH, ssr, rsq, rjunk)
            if 5 <= step < 13:
                combine(step - 5)
            if k == 15:
                vec.wait_ge(ystd, 1)
                vec.wait_ge(gd_in, 16)
                for n in range(2 * TB):
                    y = src[:, n // 2, n % 2 * HALF:(n % 2 + 1) * HALF].rearrange("p (h c) -> p h c", c=P)
                    r = rsy[:, n * DH // 2:(n + 1) * DH // 2]
                    link(vec.tensor_tensor(y, y, r.unsqueeze(2).to_broadcast([P, DH // 2, P]), ALU.mult))
                    vec.scalar_tensor_tensor(out=y, in0=y, scalar=1.0 - LAM_INIT,
                                             in1=gd[:, :].unsqueeze(1).to_broadcast([P, DH // 2, P]),
                                             op0=ALU.mult, op1=ALU.mult).then_inc(src_ready, 1)
            lo(2 * k + 4)
        head_squares("rv", 3, yr, RV, RH, ssr, rsq, rjunk)
        for tb in range(TB):
            split_rows("ya", tb)
        vec.wait_ge(rstd_r, 1)
        vec.wait_ge(gsg_ready, 1)
        for tb in range(TB):
            y = yr[:, tb, :].rearrange("p (h c) -> p h c", c=RV)
            r = rsr[:, tb * RH:(tb + 1) * RH]
            link(vec.tensor_tensor(y, y, r.unsqueeze(2).to_broadcast([P, RH, RV]), ALU.mult))
            vec.tensor_tensor(yr[:, tb, :], yr[:, tb, :], gr[:, tb, :], ALU.mult).then_inc(yr_src, 1)

        def gate(name, tb, g, dst):
            sums_ready(name, tb)
            for c in range(2):
                cols = slice(c * HALF, (c + 1) * HALF)
                t = vec.tensor_tensor(dst[:, tb, cols], acc(tb, c)[:, :], g[:, tb, cols], ALU.mult)
            t.then_inc(acc_out, 1)

        def mix(tb):
            gate("br", tb, gg, mix_t)
            vec.wait_ge(acc_out, 2 * ACC["br"] + tb + 1)
            for c in range(2):
                cols = slice(c * HALF, (c + 1) * HALF)
                vec.tensor_tensor(src[:, tb, cols], src[:, tb, cols], mix_t[:, tb, cols], ALU.add)\
                   .then_inc(src_ready, 1)

        lo(35)
        vec.wait_ge(gates_ready, 2)
        gate("bd", 0, ga, src)
        lo(36)
        split_rows("yr", 0)
        lo(37)
        lo(38)
        gate("bd", 1, ga, src)
        lo(39)
        split_rows("yr", 1)
        vec.wait_ge(gates_ready, 3)
        mix(0)
        lo(40)
        lo(41)
        split_rows("m", 0)
        mix(1)
        lo(42)
        lo(43)
        split_rows("m", 1)
        x_add("out", 0, 1.0, "mlp")
        lo(44)
        lo(45)
        split_rows("mlp", 0)
        x_add("out", 1, 1.0, "mlp")
        split_rows("mlp", 1)
        lo(46)
        lo(47)

        def square(i, tb, r=0):
            vec.wait_ge(act_ready, 2 * i + tb + 1 + 6 * r)
            vec.scalar_tensor_tensor(out=act_f[:, tb, :], in0=up(tb)[:, :], scalar=0.0, in1=act_r[:, tb, :],
                                     op0=ALU.max, op1=ALU.mult).then_inc(up_out, 1)

        square(0, 0)
        lo(48)
        square(0, 1)
        split(("p",))

        def relu_step(i, r=0):
            v = U0["ff"] + 2 + 4 * (i - 1)
            lo(v + 3, 12 * r)
            for tb in range(TB):
                split(("ff", i - 1, tb), 3 * r)
            lo(v + 4, 12 * r)
            for tb in range(TB):
                square(i, tb, r)
            lo(v + 5, 12 * r)
            lo(v + 6, 12 * r)
        relu_step(1)
        with vec.Fori(0, 2) as r:
            for j in range(3):
                relu_step(2 + j, r)
        for tb in range(TB):
            split(("ff", 7, tb))
        lo(77)
        x_add("ff", 0, 1.0, "ple")
        lo(78)
        x_add("ff", 1, 1.0, "ple")
        lo(79)
        split_rows("ple", 0)
        lo(80)
        split_rows("ple", 1)
        lo(81)

        def mid(tb):
            vec.wait_ge(pg_sig, tb + 1)
            for c in range(2):
                cols = slice(c * HALF, (c + 1) * HALF)
                link(vec.tensor_tensor(sg[:, tb, cols], sg[:, tb, cols], pl_s[:, tb, cols], ALU.mult))
                a = vec.tensor_tensor(x[:, tb, cols], x[:, tb, cols], sg[:, tb, cols], ALU.add)
                if c == 0:
                    link(a)
                    vec.wait_ge(gains_ready, 1)
                else:
                    a.then_inc(acc_out, 1)
                    vec.wait_ge(acc_out, 2 * ACC["pg"] + tb + 1)
                by_gain("ffn1", tb, c)
            n = SQ["mid", tb]
            vec.wait_ge(rstd_ready, n + 1)
            vec.wait_ge(src_ready, SRC["ffn1"] + 2 * tb + 2)
            vec.scalar_tensor_tensor(out=x[:, tb, :], in0=x[:, tb, :], scalar=rs[:, n:n + 1], in1=gain_mid[:, :],
                                     op0=ALU.mult, op1=ALU.mult).then_inc(mid_ready, 1)

        mid(0)
        lo(82)
        lo(83)
        split_rows("ffn1", 0)
        mid(1)
        split_rows("ffn1", 1)
        lo(84)

        def gated(name, norm_in, base, norm_out):
            u, n = U0[name], FF2 // SUB

            def multiply(i, tb, r=0):
                n = SQ[norm_in, tb]
                vec.wait_ge(act_ready, 2 * (base + i) + tb + 1 + 8 * r)
                vec.scalar_tensor_tensor(out=act_f[:, tb, 0:SUB], in0=up(tb)[:, SUB:2 * SUB], scalar=rs[:, n:n + 1],
                                         in1=act_r[:, tb, 0:SUB], op0=ALU.mult, op1=ALU.mult).then_inc(up_out, 1)

            multiply(0, 0)
            lo(u + 4)
            multiply(0, 1)

            def step(i, r=0):
                v = u + 2 + 3 * (i - 1)
                lo(v + 3, 12 * r)
                for tb in range(TB):
                    split((name, i - 1, tb), 4 * r)
                lo(v + 4, 12 * r)
                for tb in range(TB):
                    multiply(i, tb, r)
                lo(v + 5, 12 * r)
            step(1)
            with vec.Fori(0, 2) as r:
                for i in range(2, 6):
                    step(i, r)
            v, i = u + 2 + 3 * (n - 2), n - 1
            for tb in range(TB):
                split((name, i - 1, tb))
            lo(v + 3)
            multiply(i, 0)
            split((name, i, 0))
            lo(v + 4)
            multiply(i, 1)
            split((name, i, 1))
            lo(v + 5)
            if norm_out == "final":
                final_norm()
            else:
                x_add(name, 0, 0.5, norm_out)
                split_rows(norm_out, 0)
                x_add(name, 1, 0.5, norm_out)
                split_rows(norm_out, 1)
                lo(v + 6)

        def final_norm():
            for tb in range(TB):
                sums_ready("f2", tb)
                for c in range(2):
                    xs = x[:, tb, c * HALF:(c + 1) * HALF]
                    a = vec.scalar_tensor_tensor(out=xs, in0=acc(tb, c)[:, :], scalar=0.5, in1=xs,
                                                 op0=ALU.mult, op1=ALU.add)
                a.then_inc(acc_out, 1)
            vec.wait_ge(gain_in, GAIN["final"])
            for tb in range(TB):
                n = SQ["final", tb]
                vec.wait_ge(rstd_ready, n + 1)
                vec.wait_ge(acc_out, 2 * ACC["f2"] + tb + 1)
                for c in range(2):
                    cols = slice(c * HALF, (c + 1) * HALF)
                    vec.scalar_tensor_tensor(out=src[:, tb, cols], in0=x[:, tb, cols], scalar=rs[:, n:n + 1],
                                             in1=gain[:, cols], op0=ALU.mult, op1=ALU.mult).then_inc(src_ready, 1)

        gated("f1", "ffn1", DFF // HALF, "mix2")

        def positions():
            vec.wait_ge(pos_in, 64)
            link(vec.tensor_copy(pos_k[:, :], pos_ki[:, :]))
            link(vec.tensor_copy(pos_q[:, :], pos_qi[:, :]))
            vec.tensor_scalar(posdist[:, 0:P], pos_k[:, 0:P], pos_q[:, 0:1], None, ALU.subtract)
            link(vec.tensor_scalar(posdist[:, P:384], pos_k[:, :], pos_q[:, 1:2], None, ALU.subtract))
            link(vec.scalar_tensor_tensor(out=posdist[:, :], in0=posdist[:, :], scalar=-1.0, in1=posdist[:, :],
                                          op0=ALU.mult, op1=ALU.min))
            vec.tensor_tensor(posdist[:, :], posdist[:, :], mask, ALU.add).then_inc(pos_ready, 1)
            for tb in range(TB):
                link(vec.tensor_scalar(ang[:, tb, :], freq[:, :], pos_q[:, tb:tb + 1], None, ALU.mult))
            link(vec.tensor_scalar(turns_[:, :, :], ang[:, :, :], 1 / (2 * math.pi), None, ALU.mult))
            link(vec.tensor_scalar(turns_[:, :, :], turns_[:, :, :], 1.5 * 2 ** 23, None, ALU.add))
            link(vec.tensor_scalar(turns_[:, :, :], turns_[:, :, :], -1.5 * 2 ** 23, None, ALU.add))
            part1 = 6.28125
            part2 = float(np.float32(round((2 * math.pi - part1) * 2 ** 21) / 2 ** 21))
            for part in (part1, part2, 2 * math.pi - part1 - part2):
                link(vec.scalar_tensor_tensor(out=ang[:, :, :], in0=turns_[:, :, :], scalar=-part, in1=ang[:, :, :],
                                              op0=ALU.mult, op1=ALU.add))
            edge = float(np.nextafter(np.float32(math.pi), np.float32(0)))
            link(vec.tensor_scalar(sin2[:, :, 16:32], ang[:, :, :], edge, -edge, ALU.min, ALU.max))
            link(vec.scalar_tensor_tensor(out=cos2[:, :, 0:16], in0=sin2[:, :, 16:32], scalar=-1.0,
                                          in1=sin2[:, :, 16:32], op0=ALU.mult, op1=ALU.min))
            vec.tensor_scalar(cos2[:, :, 0:16], cos2[:, :, 0:16], math.pi / 2, None, ALU.add).then_inc(ang_ready, 1)

        def trig_pairs():
            vec.wait_ge(trig_ready, 2)
            link(vec.tensor_copy(cos2[:, :, 16:32], cos2[:, :, 0:16]))
            link(vec.tensor_scalar(sin2[:, :, 0:16], sin2[:, :, 16:32], -1.0, None, ALU.mult))

        def rotate(v, out, t, cos, sin):
            half = ROPE // 2
            link(vec.tensor_tensor(t[..., 0:half], v[..., half:ROPE], sin[..., 0:half], ALU.mult))
            link(vec.tensor_tensor(t[..., half:ROPE], v[..., 0:half], sin[..., half:ROPE], ALU.mult))
            link(vec.tensor_tensor(out, v, cos, ALU.mult))
            return vec.tensor_tensor(out, out, t, ALU.add)

        def block_logits(kind, h):
            if kind == "b":
                vec.wait_ge(bias_ready, DH + h + 1)
                logits(("b", h), bias[h % 2], BD ** -0.5)
            else:
                logits(("l", h), mask, MQ ** -0.5)

        def reciprocals(kind, h):
            m = SOFT[kind, h]
            vec.wait_ge(exp_ready, m + 1)
            vec.reciprocal(rsm[:, m, :], sm[:, m, :]).then_inc(rsm_ready, 1)

        def next_pair(kind, j):
            for h in (2 * j, 2 * j + 1):
                block_logits(kind, h)

        def turned_copy(name, dst):
            n = WB[name]
            vec.wait_ge(work_done, n + 1)
            rows = dst.shape[0]
            vec.tensor_copy(dst, work(name)[0:rows, :].rearrange("p (b t) -> p b t", t=dst.shape[-1]))\
               .then_inc(work_out[n % 2], 1)

        lo(117)
        positions()
        lo(118)
        trig_pairs()
        lo(119)
        for n, (name, dst) in enumerate((("mq", mqT), ("mk", mkT))):
            for tb in range(TB):
                turned_copy((name, tb), dst[:, :, tb * P:(tb + 1) * P])
            lo(120 + 2 * n)
            lo(121 + 2 * n)
        next_pair("b", 0)
        lo(124)
        for h in range(2):
            reciprocals("b", h)
        lo(125)
        next_pair("b", 1)
        lo(126)
        vec.wait_ge(csq, 4)
        vec.wait_ge(gain_in, GAIN["c"])
        for tb in range(TB):
            for n, (buf, c0, cols) in enumerate(((cq, 0, QR), (ckv, QR, KVR))):
                vec.tensor_tensor(buf[:, tb, 0:cols], buf[:, tb, 0:cols], gain[:, c0:c0 + cols], ALU.mult)\
                   .then_inc(c_src, 1)
        for h in range(2, 4):
            reciprocals("b", h)
        next_pair("b", 2)
        vec.wait_ge(proj_out, 2 * (CB_IN2 + 5))
        rotate(ckv[:, :, KVR:KVR + ROPE], kr[:, :, :], rope_t[:, :, :], cos2[:, :, :], sin2[:, :, :])\
            .then_inc(kr_ready, 1)
        for h in range(4, 6):
            reciprocals("b", h)
        split(("cq", 0))
        split(("cq", 1))
        split(("ckv",))
        lo(127)
        lo(128)
        next_pair("b", 3)
        vec.wait_ge(proj_out, 2 * CB_UKV)
        heads = lambda t: t[:, :, :].unsqueeze(2).to_broadcast([P, TB, MH, ROPE])
        q_rot = q_tm[:, :, :, NOPE:MQ]
        rotate(q_rot, q_rot, rot_t[:, :, :, :], heads(cos2), heads(sin2)).then_inc(rot_ready, 1)
        for h in range(6, 8):
            reciprocals("b", h)
        lo(129)
        for name, buf in (("q", qT), ("k", kT)):
            for j in (0, 2):
                turned_copy((name, j), buf[:, 2 * j:2 * j + 2, :])
        for j in range(MH // 2):
            next_pair("l", j)
            for h in (2 * j, 2 * j + 1):
                reciprocals("l", h)
        lo(130)
        for tb in range(TB):
            split_rows("cat", tb)
        x_add("o2", 0, 1.0, "ffn2")
        lo(131)
        lo(132)
        split_rows("ffn2", 0)
        x_add("o2", 1, 1.0, "ffn2")
        split_rows("ffn2", 1)
        lo(133)
        lo(134)
        gated("f2", "ffn2", DFF // HALF + FF2 // SUB, "final")

    @block.gpsimd
    def _(pool):
        chain = [0]

        def link(ins):
            chain[0] += 1
            ins.then_inc(pool_step, 1)
            pool.wait_ge(pool_step, chain[0])

        def load_gain(name, *parts):
            c0 = 0
            for g in parts:
                n = g.shape[-1]
                pool.dma_start(gain[:, c0:c0 + n], g.partition_broadcast(P)).then_inc(gain_in, 16)
                c0 += n

        def inverse_rms(s, m, r, width):
            link(pool.tensor_scalar(m, s, 1.0 / width, EPS, ALU.mult, ALU.add))
            return pool.tensor_tensor(r, m, nhalf[:, 0:r.shape[-1]], ALU.pow)

        def rstd(name):
            for tb in range(TB):
                n = SQ[name, tb]
                pool.wait_ge(square_sum, n + 1)
                inverse_rms(ss[:, n:n + 1], ms[:, n:n + 1], rs[:, n:n + 1], D).then_inc(rstd_ready, 1)

        def head_bias(k, base, slope, scale):
            pool.tensor_scalar(bias[k % 2][:, :], base, slope / scale, 1.0, ALU.mult, ALU.mult).then_inc(bias_ready, 1)

        load_gain("mix", g_mix[0])
        link(pool.memset(nhalf[:, :], -0.5))
        pool.dma_start(gd[:, :], g_diff[0].partition_broadcast(P)).then_inc(gd_in, 16)
        pool.dma_start(decay[0][:, :], decay_d[0]).then_inc(decay_in[0], 16)
        pool.dma_start(decay[1][:, :], decay_d[1]).then_inc(decay_in[1], 16)
        rstd("mix")
        pool.wait_ge(mask_in, 16)
        for h in range(DH):
            if h >= 2:
                pool.wait_ge(score_out, SM["d", h - 2, 1] + 1)
            head_bias(h, negdist, alibi(h), DHD ** -0.5)
        pool.wait_ge(src_ready, SRC["mix"] + 2 * TB)
        load_gain("ret", g_ret[0])
        for h in (2, 3):
            pool.wait_ge(score_out, SM["r", h - 2] + 1)
            pool.dma_start(decay[h % 2][:, :], decay_d[h]).then_inc(decay_in[h % 2], 16)
        pool.wait_ge(ysq, TB * DH)
        inverse_rms(ssy[:, :], msy[:, :], rsy[:, :], P).then_inc(ystd, 1)
        pool.wait_ge(gates_ready, 1)
        pool.wait_ge(gain_in, GAIN["ret"])
        pool.tensor_tensor(gr[:, :, :], gr[:, :, :], gain[:, :].unsqueeze(1).to_broadcast([P, TB, D]), ALU.mult)\
            .then_inc(gsg_ready, 1)
        pool.wait_ge(rsq, TB * RH)
        inverse_rms(ssr[:, :], msr[:, :], rsr[:, 0:TB * RH], RV).then_inc(rstd_r, 1)
        pool.wait_ge(gsg_ready, 1)
        load_gain("mlp", g_mlp[0])
        pool.wait_ge(square_sum, SQ["mlp", 0] + 1)
        pool.dma_start(p_sb[:, :, :], p_d.rearrange("(b p) n -> p b n", p=P)).then_inc(p_in, 16)
        rstd("mlp")
        n = SQ["mlp", 0]
        pool.wait_ge(rstd_ready, n + 2)
        pool.tensor_tensor(rs2[:, :], rs[:, n:n + 2], rs[:, n:n + 2], ALU.mult).then_inc(rs2_ready, 1)
        pool.wait_ge(src_ready, SRC["mlp"] + 2 * TB)
        load_gain("ple", g_ple[0])
        pool.dma_start(gain_mid[:, :], g_fin1.partition_broadcast(P)).then_inc(mid_in, 16)
        pool.dma_start(pos_ki[:, :], pos_d[0].partition_broadcast(P)).then_inc(pos_in, 16)
        for tb in range(TB):
            pool.dma_start(pos_qi[:, tb:tb + 1], pos_d[0, tb * P:(tb + 1) * P].rearrange("(p o) -> p o", o=1))\
                .then_inc(pos_in, 16)
        pool.dma_start(freq[:, :], freq_d.partition_broadcast(P)).then_inc(pos_in, 16)
        rstd("ple")
        pool.wait_ge(src_ready, SRC["ple"] + 2 * TB)
        load_gain("ffn1", g_ffn1[0])
        pool.wait_ge(gain_in, GAIN["ffn1"])
        pool.wait_ge(mid_in, 16)
        pool.tensor_tensor(gain[:, :], gain[:, :], gain_mid[:, :], ALU.mult).then_inc(gains_ready, 1)
        for tb in range(TB):
            m, n = SQ["mid", tb], SQ["ffn1", tb]
            pool.wait_ge(square_sum, m + 1)
            inverse_rms(ss[:, m:m + 1], ms[:, m:m + 1], rs[:, m:m + 1], D).then_inc(rstd_ready, 1)
            pool.wait_ge(rstd_ready, m + 1)
            pool.wait_ge(square_sum, n + 1)
            link(inverse_rms(ss[:, n:n + 1], ms[:, n:n + 1], rs[:, n:n + 1], D))
            pool.tensor_tensor(rs[:, n:n + 1], rs[:, n:n + 1], rs[:, m:m + 1], ALU.mult).then_inc(rstd_ready, 1)
        pool.wait_ge(src_ready, SRC["ffn1"] + 2 * TB)
        load_gain("mix2", g_mix2[0])
        rstd("mix2")
        pool.wait_ge(src_ready, SRC["mix2"] + 2 * TB)
        load_gain("c", g_q[0], g_kv[0])
        pool.wait_ge(pos_ready, 1)

        def block_bias(h):
            if h >= 2:
                pool.wait_ge(score_out, SM["b", h - 2] + 1)
            head_bias(DH + h, posdist[:, :], alibi(h), BD ** -0.5)
        for h in range(4):
            block_bias(h)
        pool.wait_ge(csq, 4)
        for n, cols in enumerate((QR, KVR)):
            r = inverse_rms(ssc[:, 2 * n:2 * n + 2], msc[:, 2 * n:2 * n + 2], rsc[:, 2 * n:2 * n + 2], cols)
        r.then_inc(cstd, 1)
        for h in range(4, BH):
            block_bias(h)
        pool.wait_ge(c_src, 4)
        load_gain("ffn2", g_ffn2[0])
        rstd("ffn2")
        pool.wait_ge(src_ready, SRC["ffn2"] + 2 * TB)
        load_gain("final", g_final)
        rstd("final")

    ctx.close()


_INS = ["x", "p", "g_mix", "w_in", "lam_q1", "lam_k1", "lam_q2", "lam_k2", "g_diff_sub", "g_ret_sub",
        "w_branch_diff", "w_branch_ret", "w_out", "g_mlp", "w_ff1", "w_ff2", "g_ple", "w_ple_gate", "w_ple", "g_final",
        "positions_2", "ffn1_norm_2", "ffn1_w_gate_2", "ffn1_w_up_2", "ffn1_w_down_2", "mix_norm_2",
        "w_in_2", "mla_q_norm_2", "mla_w_uq_2", "mla_kv_norm_2", "mla_w_ukv_2", "w_out_2", "ffn2_norm_2",
        "ffn2_w_gate_2", "ffn2_w_up_2", "ffn2_w_down_2", "final_norm_2"]


def _constants():
    t = np.arange(SEQ)
    dist = t[:, None] - t[None, :]
    causal = lambda m: np.concatenate([m[0:P, 0:P], m[P:SEQ, :]], 1)
    mask = causal(np.where(dist >= 0, 0.0, -BIG))
    negdist = causal(np.where(dist >= 0, -dist, -BIG))
    masks = np.concatenate([np.eye(P), mask, negdist], 1).astype(np.float32)
    log_gamma = np.log(1.0 - 2.0 ** (-5.0 - np.arange(RH)))
    decay = []
    for h in range(RH):
        m = np.where(dist >= 0, np.exp(log_gamma[h] * dist), 0.0).T * RK ** -0.5
        decay.append(np.concatenate([m[0:P, :], m[P:SEQ, P:SEQ]], 1))
    half = ROPE // 2
    freq = np.power(np.float32(10000.0), -np.arange(half, dtype=np.float32) * np.float32(2.0) / np.float32(ROPE))
    return {"masks": masks, "decay": np.stack(decay).astype(np.float32), "freq": freq.astype(np.float32)}


def kernel(**inputs):
    import concourse.bacc as bacc
    from concourse.bass_utils import run_bass_kernel_spmd

    nc = bacc.Bacc("TRN2", target_bir_lowering=False, num_devices=1)
    arrays = {}
    for name in _INS:
        a = np.asarray(inputs[name])
        if name in ("x", "p") or name.startswith(("w_", "ffn1_w", "ffn2_w", "mla_w")) or name == "g_ret_sub":
            a = a.reshape(-1, a.shape[-1]) if name != "g_ret_sub" else a.reshape(1, -1)
        arrays[f"in_{name}"] = np.ascontiguousarray(a)
    for name, a in _constants().items():
        arrays[f"const_{name}"] = a
    d = {n: nc.dram_tensor(n, a.shape, mybir.dt.from_np(a.dtype), kind="ExternalInput").ap() for n, a in arrays.items()}
    out = nc.dram_tensor("out", (SEQ, D), mybir.dt.float32, kind="ExternalOutput").ap()
    args = [d[f"in_{n}"] for n in _INS] + [d["const_masks"], d["const_decay"], d["const_freq"], out]
    two_blocks(nc, *args)
    r = run_bass_kernel_spmd(nc, [arrays], core_ids=[0])
    return r.results[0]["out"].reshape(1, SEQ, D)
```

```python
import math
from contextlib import ExitStack

import numpy as np
import concourse.bass as bass
from concourse import mybir

P = 128
D, TB, SEQ = 1024, 2, 256
KT = D // P
EPS = 1e-6
BIG = 1e30
RAW_SLOTS, HI_SLOTS = 6, 4
UNIT = 2048
HALF = 512

DH, DHD = 8, 64
RH, RK, RV = 4, 128, 256
DFF = 4096
LAM_INIT = 0.8 - 0.6 * math.exp(-0.3 * 0)
IN_CB = 16
FF2 = 2816
SUB = 256
MH, NOPE, ROPE, MV = 8, 64, 32, 64
QR, KVR = 384, 256
BH, BD = 8, 64
MQ = NOPE + ROPE

UNITS = [("in", 32), ("bd", 4), ("br", 4), ("out", 4), ("ff", 32), ("pl", 1), ("pg", 4),
         ("f1", 33), ("in2", 10), ("uq", 2), ("ukv", 1), ("o2", 4), ("f2", 33)]
U0, _n = {}, 0
for _name, _count in UNITS:
    U0[_name] = _n
    _n += _count
N_UNITS = _n

IN2 = [(0, QR), (QR, KVR + ROPE), (QR + KVR + ROPE, 512), (QR + KVR + ROPE + 512, 512),
       (QR + KVR + ROPE + 1024, 512)]
O2_ROWS = (2, 3, 0, 1)
CB_IN2, CB_UQ, CB_UKV = IN_CB, IN_CB + len(IN2), IN_CB + len(IN2) + 2

ACC = {name: n for n, name in enumerate(["bd", "br", "out", "ff", "pg", "f1", "o2", "f2"])}
NORMS = ["mix", "mlp", "ple", "mid", "ffn1", "mix2", "ffn2", "final"]
NORM_X = {"mlp": "out", "ple": "ff", "mid": "pg", "mix2": "f1", "ffn2": "o2", "final": "f2"}


SQ = {item: n for n, item in enumerate(
    [(name, tb) for name in NORMS[:3] for tb in range(TB)]
    + [(name, tb) for tb in range(TB) for name in ("mid", "ffn1")]
    + [(name, tb) for name in NORMS[5:] for tb in range(TB)])}


def unit_width(u):
    if U0["in2"] <= u < U0["in2"] + 2:
        return 4 * QR
    if U0["in2"] + 2 <= u < U0["in2"] + 4:
        return 4 * (KVR + ROPE)
    if U0["uq"] <= u < U0["ukv"]:
        return 3 * QR
    return UNIT


def work_batches():
    order = [("mix", 0, 0), ("mix", 1, 0), ("mix", 0, 1), ("mix", 1, 1)]
    for k in range(IN_CB):
        if k in (1, 2, 3, 4, 7, 8):
            order += [("qk", k - 1, tb) for tb in range(TB)]
        if 6 <= k < 14:
            order += [("a", k - 6), ("v", k - 6)]
        if k == IN_CB - 1:
            order += [("ya", 0, 0)]
        if 12 <= k:
            order += [("rv", k - 12)]
    order += [("ya", 0, 1)]
    order += [("ya", 1, h) for h in range(2)]
    order += [("yr", tb, h) for tb in range(TB) for h in range(2)]
    order += [("m", tb, h) for tb in range(TB) for h in range(2)]
    order += [("mlp", tb, h) for tb in range(TB) for h in range(2)]
    order += [("p",)]
    order += [("ff", i, tb) for i in range(DFF // HALF) for tb in range(TB)]
    order += [("ple", tb, h) for tb in range(TB) for h in range(2)]
    order += [("ffn1", tb, h) for tb in range(TB) for h in range(2)]
    order += [("f1", i, tb) for i in range(FF2 // SUB) for tb in range(TB)]
    order += [("mix2", tb, h) for tb in range(TB) for h in range(2)]
    order += [("mq", tb) for tb in range(TB)] + [("cq", 0), ("cq", 1), ("ckv",)] + [("mk", tb) for tb in range(TB)]
    for j in range(BH // 2):
        order += [("ba", 2 * j), ("ba", 2 * j + 1), ("bv", j)]
    order += [("cat", tb, 1) for tb in range(TB)]
    for j in range(MH // 2):
        order += [("la", 2 * j), ("la", 2 * j + 1), ("lv", j)]
    order += [("cat", tb, 0) for tb in range(TB)]
    order += [("ffn2", tb, h) for tb in range(TB) for h in range(2)]
    order += [("f2", i, tb) for i in range(FF2 // SUB) for tb in range(TB)]
    return {name: n for n, name in enumerate(order)}


def score_maps():
    order = [("d", 0, 0), ("d", 0, 1)]
    for k in range(6, IN_CB):
        if k - 5 < DH:
            order += [("d", k - 5, 0), ("d", k - 5, 1)]
        if 11 <= k < 15:
            order += [("r", k - 11)]
    order += [("b", h) for h in range(BH)] + [("l", h) for h in range(MH)]
    return {name: n for n, name in enumerate(order)}


WB, SM = work_batches(), score_maps()
SRC = {name: 4 * n for n, name in enumerate(["mix", "ya", "m", "mlp", "ple", "ffn1", "mix2", "ffn2", "final"])}
GAIN = {name: 16 * n for n, name in enumerate(["ret", "mlp", "ple", "ffn1", "mix2"], 1)}
GAIN |= {"c": GAIN["mix2"] + 32, "ffn2": GAIN["mix2"] + 48, "final": GAIN["mix2"] + 64}
SOFT = {("d", h, c): 2 * h + c for h in range(DH) for c in range(2)}
SOFT.update({("b", h): 2 * DH + h for h in range(BH)})
SOFT.update({("l", h): 2 * DH + BH + h for h in range(MH)})
SPLIT = {name: n for n, name in enumerate(
    [x for x in WB if x[0] in ("p", "ya", "yr", "m", "ff", "f1", "f2", "cq", "ckv", "cat", *NORMS)])}


def alibi(h):
    return 2.0 ** (-8.0 * (h + 1) / 8)


def two_blocks(nc, x_d, p_d, g_mix, w_in, lam_q1, lam_k1, lam_q2, lam_k2, g_diff, g_ret, w_bd, w_br, w_out,
               g_mlp, w_ff1, w_ff2, g_ple, w_pg, w_pl, g_fin1, pos_d, g_ffn1, w_g1, w_u1, w_d1, g_mix2,
               w_in2, g_q, w_uq, g_kv, w_ukv, w_out2, g_ffn2, w_g2, w_u2, w_d2, g_final,
               masks_d, decay_d, freq_d, out_d):
    f32, f32r, bf16, i32 = mybir.dt.float32, mybir.dt.float32r, mybir.dt.bfloat16, mybir.dt.int32
    ALU, ACT = mybir.AluOpType, mybir.ActivationFunctionType

    at = [-(-nc.sbuf_base // 128) * 128]
    named = {}

    def sb(name, shape, dt=f32, where=None):
        size = (2 if dt == bf16 else 4) * int(np.prod(shape[1:]))
        if where is None:
            where = at[0]
            at[0] += -(-size // 32) * 32
        named[name] = where
        return nc.alloc_sbuf_tensor_at(name, shape, dt, offset=where)

    raw = [sb(f"raw{s}", [P, UNIT]) for s in range(RAW_SLOTS)]
    w_lo = [sb(f"w_lo{s}", [P, UNIT], f32r, named[f"raw{s}"]) for s in range(RAW_SLOTS)]
    w_hi = [sb(f"w_hi{s}", [P, UNIT], f32r) for s in range(HI_SLOTS)]
    hA = [sb(f"hA_{s}", [P, KT, SEQ], f32r) for s in ("hi", "lo")]
    hB = [sb(f"hB_{s}", [P, KT, SEQ], f32r) for s in ("hi", "lo")]
    x = sb("x", [P, TB, D])
    src = sb("src", [P, TB, D])
    gain = sb("gain", [P, D])
    junk = sb("junk", [P, D], bf16)
    vjunk = sb("vjunk", [P, P], bf16)
    rjunk = sb("rjunk", [P, RV], bf16)
    masks = sb("masks", [P, P + 2 * 384])
    ident, mask, negdist = masks[:, 0:P], masks[:, P:P + 384], masks[:, P + 384:P + 768]
    ss = sb("ss", [P, 2 * len(NORMS)])
    rs = sb("rs", [P, 2 * len(NORMS)])
    ms = sb("ms", [P, 2 * len(NORMS)])
    rs2 = sb("rs2", [P, TB])
    nhalf = sb("nhalf", [P, 16])
    lam_s = sb("lam_s", [P, 4])
    neglam = sb("neglam", [P, 1])
    ssy, msy, rsy = (sb(n, [P, TB * DH]) for n in ("ssy", "msy", "rsy"))
    ssr, msr, rsr = (sb(n, [P, TB * RH]) for n in ("ssr", "msr", "rsr"))
    ssc, msc, rsc = (sb(n, [P, 4]) for n in ("ssc", "msc", "rsc"))
    mn = sb("mn", [P, 32, TB])
    sm = sb("sm", [P, 32, TB])
    rsm = sb("rsm", [P, 32, TB])
    qc = sb("qc", [P, DH, TB])
    gd = sb("gd", [P, P])
    arena = at[0]

    def lay(start, *parts):
        out = []
        for name, shape, *dt in parts:
            out.append(sb(name, shape, dt[0] if dt else f32, start))
            start += -(-4 * int(np.prod(shape[1:])) // 32) * 32
        assert start <= nc.sbuf_usable_end, (name, start)
        return out

    qaT, kaT, va, qrT, krT, vr, gr, ga, yr, sT0, sT1 = lay(
        arena, ("qaT", [P, DH, SEQ]), ("kaT", [P, DH, SEQ]), ("va", [P, TB, D]), ("qrT", [P, RH, SEQ]),
        ("krT", [P, RH, SEQ]), ("vr", [P, TB, D]), ("gr", [P, TB, D]), ("ga", [P, TB, D]),
        ("yr", [P, TB, D]), ("sT0", [P, 384]), ("sT1", [P, 384]))
    (gg,) = lay(arena, ("gg", [P, TB, D]))
    qk_tm = lay(named["yr"], ("qk_tm0", [P, TB, HALF]), ("qk_tm1", [P, TB, HALF]))
    lam_v, lam_w = lay(named["ga"], ("lam_v", [P, 4, DHD]), ("lam_w", [P, 2, DHD]))
    L, aT0, aT1, bias0, bias1 = lay(named["hB_hi"], ("L", [P, 4, 384]), ("aT0", [P, 384]), ("aT1", [P, 384]),
                                    ("bias0", [P, 384]), ("bias1", [P, 384]))
    decay0, decay1 = lay(named["bias1"] + 4 * 384, ("decay0", [P, 384]), ("decay1", [P, 384]))
    aT, bias, decay, sT = [aT0, aT1], [bias0, bias1], [decay0, decay1], [sT0, sT1]
    fT0, fT1, act_r, act_f, pl_s, sg, pT0, pT1, p_sb, gain_mid = lay(
        arena, ("fT_hi", [P, 4, SEQ], f32r), ("fT_lo", [P, 4, SEQ], f32r), ("act_r", [P, TB, HALF]),
        ("act_f", [P, TB, HALF]), ("pl_s", [P, TB, D]), ("sg", [P, TB, D]),
        ("pT_hi", [P, 2, SEQ], f32r), ("pT_lo", [P, 2, SEQ], f32r), ("p_sb", [P, TB, 256]), ("gain_mid", [P, D]))
    fT, pT = [fT0, fT1], [pT0, pT1]
    (mix_t,) = lay(named["va"], ("mix_t", [P, TB, D]))
    (mq_tm, mk_tm, mv, mqT, mkT, cq, ckv, q_tm, k_tm, v_tm, qT, kT, pos_k, posdist, kr) = lay(
        arena, ("mq_tm", [P, TB, 512]), ("mk_tm", [P, TB, 512]), ("mv", [P, TB, 512]), ("mqT", [P, 4, SEQ]),
        ("mkT", [P, 4, SEQ]), ("cq", [P, TB, QR]), ("ckv", [P, TB, KVR + ROPE]),
        ("q_tm", [P, TB, MH, MQ]), ("k_tm", [P, TB, MH, MQ]), ("v_tm", [P, TB, MH, MV]),
        ("qT", [MQ, MH, SEQ]), ("kT", [MQ, MH, SEQ]), ("pos_k", [P, SEQ]), ("posdist", [P, 384]),
        ("kr", [P, TB, ROPE]))
    (cT0,), (cT1,) = (lay(named[where], (name, [P, 5, SEQ], f32r)) for where, name in (("qT", "cT_hi"), ("kT", "cT_lo")))
    cT = [cT0, cT1]
    (rope_t, rot_t) = lay(named["kr"] + 4 * TB * ROPE, ("rope_t", [P, TB, ROPE]), ("rot_t", [P, TB, MH, ROPE]))
    cos2, sin2, ang, turns_ = lay(named["rot_t"] + 4 * TB * MH * ROPE, ("cos2", [P, TB, ROPE]), ("sin2", [P, TB, ROPE]),
                                  ("ang", [P, TB, 16]), ("turns_", [P, TB, 16]))
    pos_ki, pos_qi, pos_q, freq = lay(named["turns_"] + 4 * TB * 16, ("pos_ki", [P, SEQ], i32), ("pos_qi", [P, TB], i32),
                                      ("pos_q", [P, TB]), ("freq", [P, 16]))

    ctx = ExitStack()
    bank = [ctx.enter_context(nc.psum_tensor(f"bank{i}", [P, HALF], f32)) for i in range(8)]
    acc = lambda tb, c: bank[2 * tb + c]
    proj = lambda cb, tb: bank[2 * (cb % 2) + tb]
    up = lambda tb: bank[4 + tb]
    score = lambda name: bank[4 + SM[name] % 2]
    work = lambda name: bank[6 + WB[name] % 2]

    sems = {}

    def sem(name):
        sems[name] = ctx.enter_context(nc.semaphore(name))
        return sems[name]

    raw_in = [sem(f"raw_in{s}") for s in range(RAW_SLOTS)]
    first_in = [sem("first_in0"), sem("first_in1")]
    first_hi, first_lo = sem("first_hi"), sem("first_lo")
    nhalf_ready, act_warm = sem("nhalf_ready"), sem("act_warm")
    hi_ready = sem("hi_ready")
    lo_ready = sem("lo_ready")
    unit_used = sem("unit_used")
    x_in = [sem(f"x_in{n}") for n in range(4)]
    p_in, ident_in, mask_in, lam_in, gd_in = (sem(n) for n in ("p_in", "ident_in", "mask_in", "lam_in", "gd_in"))
    gain_in = sem("gain_in")
    mix_in = [sem("mix_in0"), sem("mix_in1")]
    mid_in, gains_ready = sem("mid_in"), sem("gains_ready")
    rs2_ready = sem("rs2_ready")
    decay_in, pos_in = [sem("decay_in0"), sem("decay_in1")], sem("pos_in")
    square_sum = sem("square_sum")
    rstd_ready = sem("rstd_ready")
    mid_ready = sem("mid_ready")
    src_ready = sem("src_ready")
    work_done = sem("work_done")
    work_out = [sem("work_out0"), sem("work_out1")]
    split_hi = sem("split_hi")
    proj_done, proj_out = sem("proj_done"), sem("proj_out")
    acc_done, acc_out = sem("acc_done"), sem("acc_out")
    up_done, act_ready, up_out = sem("up_done"), sem("act_ready"), sem("up_out")
    score_done, score_out = sem("score_done"), sem("score_out")
    bias_ready = sem("bias_ready")
    exp_ready = sem("exp_ready")
    comb_ready = sem("comb_ready")
    ysq, rsq = sem("ysq"), sem("rsq")
    ystd, rstd_r, cstd = sem("ystd"), sem("rstd_r"), sem("cstd")
    gates_ready = sem("gates_ready")
    gsg_ready = sem("gsg_ready")
    yr_src = sem("yr_src")
    lam_prod, lam_exp = sem("lam_prod"), sem("lam_exp")
    pl_done, pl_out, pg_sig = sem("pl_done"), sem("pl_out"), sem("pg_sig")
    csq, c_src = sem("csq"), sem("c_src")
    pos_ready, ang_ready, trig_ready = sem("pos_ready"), sem("ang_ready"), sem("trig_ready")
    rot_ready, kr_ready = sem("rot_ready"), sem("kr_ready")
    heads_done = sem("heads_done")
    heads_out = [sem("heads_out0"), sem("heads_out1")]
    k_full = sem("k_full")
    vec_step, pool_step = sem("vec_step"), sem("pool_step")
    out_done = sem("out_done")

    def unit_view(buf, n, cols):
        return buf[:, 0:n * cols].rearrange("p (t n) -> p t n", n=cols)

    block = ctx.enter_context(nc.Block())

    @block.sync
    def _(sp):
        def load(u, pieces, turns=0):
            if u >= RAW_SLOTS:
                sp.wait_ge(unit_used, u - RAW_SLOTS + 1 + 12 * turns)
            for dst, w in pieces:
                sp.dma_start(dst, w).then_inc(raw_in[u % RAW_SLOTS], 16)

        def narrow(u, w, kt0, n, c0, cols, turns=0):
            view = unit_view(raw[u % RAW_SLOTS], n, cols)
            h = -(-n // 2)
            load(u, [(view[:, a:b, :], w[(kt0 + a) * P:(kt0 + b) * P, bass.ds(c0, cols)]
                      .rearrange("(t p) n -> p t n", p=P)) for a, b in ((0, h), (h, n))], turns)

        def wide(u, w, row0, turns=0):
            view = unit_view(raw[u % RAW_SLOTS], 2, D)
            load(u, [(view[:, j, :], w[bass.ds(row0 + j * P, P), :]) for j in range(2)], turns)

        def gate_up(u, w_g, w_u, kt0, c0, turns=0):
            view = unit_view(raw[u % RAW_SLOTS], 4, 2 * SUB)
            load(u, [(view[:, :, s * SUB:(s + 1) * SUB], w[kt0 * P:(kt0 + 4) * P, bass.ds(c0, SUB)]
                      .rearrange("(t p) n -> p t n", p=P)) for s, w in enumerate((w_g, w_u))], turns)

        def load_x(tb, c):
            cols = slice(c * HALF, (c + 1) * HALF)
            sp.dma_start(x[:, tb, cols], x_d[tb * P:(tb + 1) * P, cols]).then_inc(x_in[2 * tb + c], 16)

        load_x(0, 0)
        for c in range(2):
            sp.dma_start(unit_view(raw[0], 4, HALF)[:, 2 * c:2 * c + 2, :],
                         w_in[2 * c * P:(2 * c + 2) * P, 0:HALF].rearrange("(t p) n -> p t n", p=P))\
              .then_inc(first_in[c], 16)
        load_x(1, 0)
        load_x(0, 1)
        sp.dma_start(gain[:, HALF:D], g_mix[0, HALF:D].partition_broadcast(P)).then_inc(mix_in[1], 16)
        load_x(1, 1)
        for cb in range(IN_CB):
            for j in range(1 if cb == 0 else 0, 2):
                narrow(U0["in"] + 2 * cb + j, w_in, 4 * j, 4, cb * HALF, HALF)
        for name, w in (("bd", w_bd), ("br", w_br), ("out", w_out)):
            for j in range(4):
                wide(U0[name] + j, w, 2 * j * P)

        u = U0["ff"]
        for j in range(2):
            narrow(u + j, w_ff1, 4 * j, 4, 0, HALF)

        def ff_step(u, i, turns=0):
            for j in range(2):
                narrow(u + j, w_ff1, 4 * j, 4, i * HALF, HALF, turns)
            for j in range(2):
                wide(u + 2 + j, w_ff2, i * HALF - HALF + 2 * j * P, turns)
        ff_step(u + 2, 1)
        with sp.Fori(0, 2) as r:
            for j in range(3):
                ff_step(u + 6 + 4 * j, 3 * r + 2 + j, r)
        for j in range(2):
            wide(u + 30 + j, w_ff2, DFF - HALF + 2 * j * P)

        wide(U0["pl"], w_pl, 0)
        for j in range(4):
            wide(U0["pg"] + j, w_pg, 2 * j * P)

        def gated(u, w_g, w_u, w_d):
            for j in range(2):
                gate_up(u + j, w_g, w_u, 4 * j, 0)

            def step(i, r=0, turns=0):
                v = u + 2 + 3 * (i - 1)
                for j in range(2):
                    gate_up(v + j, w_g, w_u, 4 * j, r * (4 * SUB) + i * SUB, turns)
                wide(v + 2, w_d, r * (4 * SUB) + (i - 1) * SUB, turns)
            step(1)
            with sp.Fori(0, 2) as r:
                for i in range(2, 6):
                    step(i, r, r)
            step(FF2 // SUB - 1)
            wide(u + 32, w_d, FF2 - SUB)

        gated(U0["f1"], w_g1, w_u1, w_d1)
        for n, (c0, cols) in enumerate(IN2):
            for j in range(2):
                narrow(U0["in2"] + 2 * n + j, w_in2, 4 * j, 4, c0, cols)
        for j in range(2):
            narrow(U0["uq"] + j, w_uq, 0, 3, j * QR, QR)
        wide(U0["ukv"], w_ukv, 0)
        for n, j in enumerate(O2_ROWS):
            wide(U0["o2"] + n, w_out2, 2 * j * P)
        gated(U0["f2"], w_g2, w_u2, w_d2)

        for n in range(2 * TB):
            tb, cols = n // 2, slice(n % 2 * HALF, (n % 2 + 1) * HALF)
            sp.wait_ge(src_ready, SRC["final"] + n + 1)
            sp.dma_start(out_d[tb * P:(tb + 1) * P, cols], src[:, tb, cols]).then_inc(out_done, 16)
        sp.wait_ge(out_done, 16 * 2 * TB)

    def rows_of(name):
        kind, b = name[0], work(name)
        if kind == "p":
            return [t[:, :, :] for t in pT], b[:, :].rearrange("p (k t) -> p k t", t=SEQ)
        if kind == "ckv":
            return [t[:, 3:5, :] for t in cT], b[:, :].rearrange("p (k t) -> p k t", t=SEQ)
        if kind in ("ff", "f1", "f2"):
            tb, k0, n, pair = name[2], 0 if kind == "ff" else 2 * (name[1] % 2), 4 if kind == "ff" else 2, fT
        elif kind == "cq":
            tb, k0, n, pair = name[1], 0, 3, cT
        else:
            tb, k0, n, pair = name[1], 4 * name[2], 4, hB if kind in ("ya", "m", "ple") else hA
        return ([t[:, k0:k0 + n, tb * P:(tb + 1) * P] for t in pair],
                b[:, 0:n * P].rearrange("p (k t) -> p k t", t=P))

    def rotate(engine, link, v, out, t, cos, sin):
        half = ROPE // 2
        link(engine.tensor_tensor(t[..., 0:half], v[..., half:ROPE], sin[..., 0:half], ALU.mult))
        link(engine.tensor_tensor(t[..., half:ROPE], v[..., 0:half], sin[..., half:ROPE], ALU.mult))
        link(engine.tensor_tensor(out, v, cos, ALU.mult))
        return engine.tensor_tensor(out, out, t, ALU.add)

    @block.tensor
    def _(pe):
        def product(outs, h, kt, tb, u, col):
            hi, lo = (t[:, kt, tb * P:(tb + 1) * P] for t in h)
            spans = [(o, slice(col + n * HALF, col + n * HALF + o.shape[-1])) for n, o in enumerate(outs)]
            part = {"hi": w_hi[u % HI_SLOTS], "lo": w_lo[u % RAW_SLOTS]}
            return [(o, x_part, part[p][:, c]) for x_part, p in ((hi, "hi"), (hi, "lo"), (lo, "hi"))
                    for o, c in spans]

        def products(outs, h, kt0, n, tb, u, cols, first, last, du=0, t0=0):
            if (u, n) == (0, 2):
                pe.wait_ge(first_lo, 1)
            else:
                pe.wait_ge(lo_ready, u + 1 + du)
            for t in range(t0, n):
                todo = product(outs, h, kt0 + t, tb, u, t * cols)
                for m, (o, a, w) in enumerate(todo):
                    mm = pe.matmul(o, a, w, start=first and t == 0 and m < len(outs),
                                   stop=last and t == n - 1 and m >= len(todo) - len(outs))
            return mm

        def work_free(n, dw=0):
            if n >= 2:
                pe.wait_ge(work_out[n % 2], n // 2 + dw)

        def turn(name, blocks, dw=0):
            work_free(WB[name], dw)
            col = 0
            for blk in blocks:
                rows, cols = blk.shape[0], blk.shape[-1]
                mm = pe.transpose(work(name)[0:cols, col:col + rows], blk, ident)
                col += rows
            mm.then_inc(work_done, 1)

        def turned(name, dw=0):
            n = WB[name]
            pe.wait_ge(work_out[n % 2], n // 2 + 1 + dw)

        def turn_rows(name, buf, tb, halves=range(2)):
            for h in halves:
                if name in SRC:
                    pe.wait_ge(src_ready, SRC[name] + 2 * tb + h + 1)
                turn((name, tb, h), [buf[:, tb, (4 * h + j) * P:(4 * h + j + 1) * P] for j in range(4)])

        def src_turn(name, tb):
            turn_rows(name, src, tb)

        def narrow_block(out, name, u, tb, cols, middle=None):
            for j in range(2):
                if name:
                    turned((name, tb, j))
                mm = products([out], hA, 4 * j, 4, tb, u + j, cols, j == 0, j == 1)
                if tb:
                    mm.then_inc(unit_used, 1)
                if middle and j == 0:
                    middle()
            return mm

        def scores(name, q, k, h):
            m, b = SM[name], score(name)
            if m >= 2:
                pe.wait_ge(score_out, m - 1)
            pe.matmul(b[:, 0:P], q[:, h, 0:P], k[:, h, 0:P], start=True, stop=True)
            pe.matmul(b[:, P:384], q[:, h, P:SEQ], k[:, h, :], start=True, stop=True).then_inc(score_done, 1)

        def diff_scores(h):
            for c in range(2):
                half = slice(c * DHD, (c + 1) * DHD)
                scores(("d", h, c), qaT[half], kaT[half], h)

        def apply_weights(name, a, v, cols):
            b = work(name)
            work_free(WB[name])
            pe.matmul(b[:, 0:cols], a[:, 0:P], v[0], start=True, stop=True)
            pe.matmul(b[:, cols:2 * cols], a[:, P:2 * P], v[0], start=True, stop=False)
            pe.matmul(b[:, cols:2 * cols], a[:, 2 * P:384], v[1], start=False, stop=True).then_inc(work_done, 1)

        def diff_turn(h):
            pe.wait_ge(comb_ready, h + 1)
            w = L[:, SOFT["d", h, 1] % 4, :]
            turn(("a", h), [w[:, j * P:(j + 1) * P] for j in range(3)])

        def diff_out(h):
            pe.wait_ge(proj_out, 12)
            turned(("a", h))
            apply_weights(("v", h), aT[h % 2], [va[:, tb, h * P:(h + 1) * P] for tb in range(TB)], P)

        def ret_scores(h):
            if h == 0:
                turned(("qk", 6, 1))
                turned(("qk", 7, 1))
            pe.wait_ge(score_out, SM["r", h] - 1)
            b = score(("r", h))
            pe.matmul(b[:, 0:SEQ], krT[:, h, 0:P], qrT[:, h, :], start=True, stop=True)
            pe.matmul(b[:, SEQ:384], krT[:, h, P:SEQ], qrT[:, h, P:SEQ], start=True, stop=True)\
              .then_inc(score_done, 1)

        def ret_out(h):
            pe.wait_ge(score_out, SM["r", h] + 1)
            pe.wait_ge(proj_out, 20)
            apply_weights(("rv", h), sT[h % 2], [vr[:, tb, h * RV:(h + 1) * RV] for tb in range(TB)], RV)

        def mix_turn(tb, half):
            pe.wait_ge(src_ready, 2 * half + tb + 1)
            turn(("mix", tb, half), [src[:, tb, (4 * half + j) * P:(4 * half + j + 1) * P] for j in range(4)])

        pe.wait_ge(ident_in, 16)
        for cb in range(IN_CB):
            u = U0["in"] + 2 * cb
            if cb >= 2:
                pe.wait_ge(proj_out, 2 * cb - 2)
            if cb == 0:
                sums = [[proj(0, tb)[:, :]] for tb in range(TB)]
                mix_turn(0, 0)
                turned(("mix", 0, 0))
                products(sums[0], hA, 0, 2, 0, 0, HALF, True, False)
                mix_turn(1, 0)
                products(sums[0], hA, 0, 4, 0, 0, HALF, False, False, t0=2)
                mix_turn(0, 1)
                turned(("mix", 1, 0))
                products(sums[1], hA, 0, 4, 1, 0, HALF, True, False).then_inc(unit_used, 1)
                mix_turn(1, 1)
                for tb in range(TB):
                    turned(("mix", tb, 1))
                    mm = products(sums[tb], hA, 4, 4, tb, 1, HALF, False, True)
                    mm.then_inc(unit_used if tb else proj_done, 1)
            else:
                for j in range(2):
                    for tb in range(TB):
                        mm = products([proj(cb, tb)[:, :]], hA, 4 * j, 4, tb, u + j, HALF, j == 0, j == 1)
                        if j and tb == 0:
                            mm.then_inc(proj_done, 1)
                    mm.then_inc(unit_used, 1)
            if cb in (1, 2, 3, 4, 7, 8):
                pe.wait_ge(proj_out, 2 * cb)
                for tb in range(TB):
                    turn(("qk", cb - 1, tb),
                         [qk_tm[(cb - 1) % 2][:, tb, j * P:(j + 1) * P] for j in range(4)])
            if cb == 5:
                turned(("qk", 3, 0))
                turned(("qk", 3, 1))
                diff_scores(0)
            if 6 <= cb < 14:
                diff_turn(cb - 6)
                if cb < 13:
                    diff_scores(cb - 5)
                diff_out(cb - 6)
            if cb == IN_CB - 1:
                turn_rows("ya", src, 0, (0,))
            if cb >= 12:
                ret_out(cb - 12)
            if cb == IN_CB - 1:
                turn_rows("ya", src, 0, (1,))
            if 11 <= cb < 15:
                ret_scores(cb - 11)

        def acc_free(name, tb):
            if n := 2 * ACC[name]:
                pe.wait_ge(acc_out, n - 1 + tb)

        def unit(h, u0, j, tb):
            return products([acc(tb, c)[:, :] for c in range(2)], h, 2 * j, 2, tb, u0 + j, D, j == 0, j == 3)

        def square_product(name, h, u0, operand, before=None, steps=()):
            steps = dict(steps)
            for tb in range(TB):
                acc_free(name, tb)
                for j in range(4):
                    if j % 2 == 0:
                        turned((operand, tb, j // 2))
                    if j == 0 and before:
                        before(tb)
                    mm = unit(h, u0, j, tb)
                    if tb:
                        mm.then_inc(unit_used, 1)
                    elif j == 3:
                        mm.then_inc(acc_done, 1)
                    if (tb, j) in steps:
                        steps[tb, j]()

        def yr_turn(tb):
            pe.wait_ge(yr_src, tb + 1)
            turn_rows("yr", yr, tb)

        pe.wait_ge(proj_out, 2 * IN_CB)
        square_product("bd", hB, U0["bd"], "ya",
                       steps={(0, 1): lambda: src_turn("ya", 1), (1, 1): lambda: yr_turn(0)})
        square_product("br", hA, U0["br"], "yr", steps={(0, 1): lambda: yr_turn(1), (1, 2): lambda: src_turn("m", 0)})
        square_product("out", hB, U0["out"], "m",
                       steps={(0, 2): lambda: src_turn("m", 1), (1, 2): lambda: src_turn("mlp", 0)})

        def ff_up0(u0, norm):
            narrow_block(up(0)[:, :], norm, u0, 0, HALF, lambda: src_turn(norm, 1)).then_inc(up_done, 1)
            narrow_block(up(1)[:, :], norm, u0, 1, HALF)

        def ff_turn(name, i, done, cols, di=0, blocks=range(TB)):
            for tb in blocks:
                pe.wait_ge(up_out, done - 1 + tb + 2 * di)
                turn((name, i, tb), [act_f[:, tb, j * P:(j + 1) * P] for j in range(cols // P)], di)

        def ff_up(u, name, i, steps, cols, du=0, di=0):
            for j in range(2):
                for tb in range(TB):
                    if j == 0:
                        pe.wait_ge(up_out, 2 * steps - 1 + tb + 2 * di)
                    mm = products([up(tb)[:, :]], hA, 4 * j, 4, tb, u + j, HALF, j == 0, j == 1, du)
                    if j and tb == 0:
                        mm.then_inc(up_done, 1)
                mm.then_inc(unit_used, 1)
                if j == 0:
                    ff_turn(name, i - 1, 2 * steps, cols, di)

        u = U0["ff"]
        ff_up0(u, "mlp")
        pe.wait_ge(p_in, 16)
        turn(("p",), [p_sb[:, tb, k * P:(k + 1) * P] for k in range(2) for tb in range(TB)])

        def relu_step(i, r=0, start=False):
            v = U0["ff"] + 2 + 4 * (i - 1)
            ff_up(v, "ff", i, i, HALF, 12 * r, 3 * r)
            for j in range(2):
                for tb in range(TB):
                    if j == 0:
                        turned(("ff", i - 1, tb), 3 * r)
                    if start and j == 0:
                        acc_free("ff", tb)
                    mm = products([acc(tb, c)[:, :] for c in range(2)], fT, 2 * j, 2, tb, v + 2 + j, D,
                                  start and j == 0, False, 12 * r)
                mm.then_inc(unit_used, 1)
        relu_step(1, start=True)
        with pe.Fori(0, 2) as r:
            for j in range(3):
                relu_step(2 + j, r)
        last = DFF // HALF - 1
        ff_turn("ff", last, 2 * (last + 1), HALF)

        def ple_product(tb):
            if tb:
                pe.wait_ge(pl_out, 1)
            turned(("p",))
            mm = products([bank[4 + c][:, :] for c in range(2)], pT, 0, 2, tb, U0["pl"], D, True, True)
            mm.then_inc(unit_used if tb else pl_done, 1)

        ple_product(0)
        for tb in range(TB):
            turned(("ff", last, tb))
            for j in range(2):
                mm = products([acc(tb, c)[:, :] for c in range(2)], fT, 2 * j, 2, tb, u + 30 + j, D, False, j == 1)
                if tb:
                    mm.then_inc(unit_used, 1)
            if tb == 0:
                mm.then_inc(acc_done, 1)

        src_turn("ple", 0)
        ple_product(1)
        square_product("pg", hB, U0["pg"], "ple",
                       before=lambda tb: tb and pe.wait_ge(pl_out, 2),
                       steps={(0, 1): lambda: src_turn("ple", 1), (1, 2): lambda: src_turn("ffn1", 0)})

        def gated(name, norm, base):
            u, n = U0[name], FF2 // SUB
            ff_up0(u, norm)

            def down(v, i, tb, r=0, first=False, last=False):
                turned((name, i, tb), 4 * r)
                return products([acc(tb, c)[:, :] for c in range(2)], fT, 2 * (i % 2), 2, tb, v, D, first, last,
                                12 * r)

            def step(i, r=0):
                v = u + 2 + 3 * (i - 1)
                ff_up(v, name, i, base + i, SUB, 12 * r, 4 * r)
                for tb in range(TB):
                    if i == 1:
                        acc_free(name, tb)
                    mm = down(v + 2, i - 1, tb, r, i == 1)
                mm.then_inc(unit_used, 1)
            step(1)
            with pe.Fori(0, 2) as r:
                for i in range(2, 6):
                    step(i, r)
            v, i = u + 2 + 3 * (n - 2), n - 1
            pe.wait_ge(up_out, 2 * (base + i))
            narrow_block(up(0)[:, :], None, v, 0, HALF, lambda: ff_turn(name, i - 1, 2 * (base + i), SUB))\
                .then_inc(up_done, 1)
            narrow_block(up(1)[:, :], None, v, 1, HALF, lambda: ff_turn(name, i, 2 * (base + n), SUB, blocks=(0,)))
            down(v + 2, i - 1, 0)
            ff_turn(name, i, 2 * (base + n), SUB, blocks=(1,))
            down(v + 3, i, 0, last=True).then_inc(acc_done, 1)
            down(v + 2, i - 1, 1).then_inc(unit_used, 1)
            if name == "f1":
                src_turn("mix2", 0)
            down(v + 3, i, 1, last=True).then_inc(unit_used, 1)

        gated("f1", "ffn1", DFF // HALF)

        def head_scores(kind, h):
            if kind == "b":
                half = slice(h % 2 * BD, h % 2 * BD + BD)
                scores(("b", h), mqT[half], mkT[half], h // 2)
            else:
                scores(("l", h), qT, kT, h)

        def pair(kind, j, beside):
            for h in (2 * j, 2 * j + 1):
                m = SOFT[kind, h]
                pe.wait_ge(exp_ready, m + 1)
                turn((kind + "a", h), [L[:, m % 4, b * P:(b + 1) * P] for b in range(3)])
                if 2 * j + 2 < BH:
                    head_scores(kind, h + 2)
            if beside:
                beside()
            name = (kind + "v", j)
            b = work(name)
            work_free(WB[name])
            for h in (2 * j, 2 * j + 1):
                turned((kind + "a", h))
                v = [mv[:, tb, h * BD:(h + 1) * BD] if kind == "b" else v_tm[:, tb, h, :] for tb in range(TB)]
                a, c = aT[h % 2], h % 2 * 2 * BD
                pe.matmul(b[:, c:c + BD], a[:, 0:P], v[0], start=True, stop=True)
                pe.matmul(b[:, c + BD:c + 2 * BD], a[:, P:2 * P], v[0], start=True, stop=False)
                mm = pe.matmul(b[:, c + BD:c + 2 * BD], a[:, 2 * P:384], v[1], start=False, stop=True)
            mm.then_inc(work_done, 1)

        for n, (_, cols) in enumerate(IN2):
            cb, u = CB_IN2 + n, U0["in2"] + 2 * n
            if n >= 2:
                pe.wait_ge(proj_out, 2 * cb - 2)
            if n == 0:
                pe.wait_ge(acc_out, 2 * ACC["f1"] + 1)
                narrow_block(proj(cb, 0)[:, :], "mix2", u, 0, cols, lambda: src_turn("mix2", 1))\
                    .then_inc(proj_done, 1)
                pe.wait_ge(acc_out, 2 * ACC["f1"] + 2)
                narrow_block(proj(cb, 1)[:, :], "mix2", u, 1, cols)
            else:
                for j in range(2):
                    for tb in range(TB):
                        mm = products([proj(cb, tb)[:, 0:cols]], hA, 4 * j, 4, tb, u + j, cols, j == 0, j == 1)
                        if j and tb == 0:
                            mm.then_inc(proj_done, 1)
                    mm.then_inc(unit_used, 1)
            if n in (3, 4):
                name, buf = (("mq", mq_tm), ("mk", mk_tm))[n - 3]
                pe.wait_ge(proj_out, 2 * cb)
                for tb in range(TB):
                    turn((name, tb), [buf[:, tb, b * P:(b + 1) * P] for b in range(4)])
            if n == 3:
                pe.wait_ge(c_src, 4)
                for tb in range(TB):
                    turn(("cq", tb), [cq[:, tb, k * P:(k + 1) * P] for k in range(3)])
                turn(("ckv",), [ckv[:, tb, k * P:(k + 1) * P] for k in range(2) for tb in range(TB)])

        def queries(n):
            cb = CB_UQ + n
            pe.wait_ge(proj_out, 2 * cb - 2)
            for tb in range(TB):
                turned(("cq", tb))
                mm = products([proj(cb, tb)[:, 0:QR]], cT, 0, 3, tb, U0["uq"] + n, QR, True, True)
                mm.then_inc(unit_used if tb else proj_done, 1)

        def keys_values(tb):
            pe.wait_ge(proj_out, 2 * CB_UKV)
            turned(("ckv",))
            mm = products([acc(tb, c)[:, :] for c in range(2)], [t[:, 3:5, :] for t in cT], 0, 2, tb, U0["ukv"], D,
                          True, True)
            mm.then_inc(unit_used if tb else proj_done, 1)

        def turn_heads(buf):
            for j in range(MH // 2):
                for n, (h, tb) in enumerate((h, tb) for h in (2 * j, 2 * j + 1) for tb in range(TB)):
                    mm = pe.transpose(bank[j][0:MQ, n * P:(n + 1) * P], buf[:, tb, h, :], ident)
                mm.then_inc(heads_done, 1)

        def turn_queries():
            pe.wait_ge(rot_ready, 1)
            pe.wait_ge(proj_out, 2 * CB_UKV + 2)
            turn_heads(q_tm)

        def turn_keys():
            pe.wait_ge(k_full, 1)
            for copied in heads_out:
                pe.wait_ge(copied, MH // 4)
            turn_heads(k_tm)

        def output(n, tb, t0=0, t1=2):
            if n == 0:
                pe.wait_ge(proj_out, 2 * CB_UKV + 1 + tb)
            if n % 2 == 0:
                turned(("cat", tb, 1 - n // 2))
            return products([acc(tb, c)[:, :] for c in range(2)], hA, 2 * O2_ROWS[n], t1, tb, U0["o2"] + n, D,
                            n == 0, n == 3, t0=t0)

        def output_step(n, tb):
            mm = output(n, tb)
            if tb:
                mm.then_inc(unit_used, 1)

        queries(0)
        for tb in range(TB):
            turned(("mk", tb))
        for h in range(2):
            head_scores("b", h)
        queries(1)
        pe.wait_ge(proj_out, 2 * (CB_IN2 + 5))
        for j, beside in enumerate((lambda: keys_values(0), lambda: keys_values(1), turn_queries, turn_keys)):
            pair("b", j, beside)
        for copied in heads_out:
            pe.wait_ge(copied, MH // 2)
        for h in range(2):
            head_scores("l", h)
        turned(("bv", BH // 2 - 1))
        for tb in range(TB):
            turn(("cat", tb, 1), [src[:, tb, (4 + k) * P:(5 + k) * P] for k in range(4)])
        output_step(0, 0)
        for j, beside in enumerate((lambda: output_step(0, 1), lambda: output_step(1, 0), lambda: output(1, 1, t1=1),
                                    None)):
            pair("l", j, beside)
        turned(("lv", MH // 2 - 1))
        for tb in range(TB):
            turn(("cat", tb, 0), [src[:, tb, k * P:(k + 1) * P] for k in range(4)])
        output(1, 1, t0=1).then_inc(unit_used, 1)
        output(2, 0)
        output(3, 0).then_inc(acc_done, 1)
        output(2, 1).then_inc(unit_used, 1)
        src_turn("ffn2", 0)
        output(3, 1).then_inc(unit_used, 1)
        gated("f2", "ffn2", DFF // HALF + FF2 // SUB)

    @block.scalar
    def _(act):
        def loads(u):
            return 32 * (u // RAW_SLOTS + (u % RAW_SLOTS > 0))

        def hi(u, turns=0):
            if u >= N_UNITS:
                return
            if u >= HI_SLOTS:
                act.wait_ge(unit_used, u - HI_SLOTS + 1 + 12 * turns)
            act.wait_ge(raw_in[u % RAW_SLOTS], loads(u) + 64 * turns)
            w = unit_width(u)
            act.activation(w_hi[u % HI_SLOTS][:, 0:w], raw[u % RAW_SLOTS][:, 0:w], ACT.Copy).then_inc(hi_ready, 1)

        def split(name, di=0):
            act.wait_ge(work_done, WB[name] + 1 + 2 * di)
            (dst, _), b = rows_of(name)
            act.activation(dst, b, ACT.Copy).then_inc(split_hi, 1)

        def split_rows(name, tb):
            for h in range(2):
                split((name, tb, h))

        def squares(name, tb):
            n = SQ[name, tb]
            if name == "mix":
                for half in range(2):
                    act.wait_ge(x_in[2 * tb + half], 16)
            elif name == "ffn1":
                act.wait_ge(mid_ready, tb + 1)
            else:
                act.wait_ge(acc_out, 2 * ACC[NORM_X[name]] + tb + 1)
            if n:
                act.wait_ge(square_sum, n)
            act.activation(junk[:, :], x[:, tb, :], ACT.Square, accum_out=ss[:, n:n + 1]).then_inc(square_sum, 1)

        def inv_rms(name, tb):
            n = SQ[name, tb]
            act.wait_ge(rstd_ready, n + 1)
            return rs[:, n:n + 1]

        def proj_ready(cb, tb, last_unit):
            if tb == 0:
                act.wait_ge(proj_done, cb + 1)
            else:
                act.wait_ge(unit_used, last_unit + 1)

        def proj_copy(cb):
            dst = [(qk_tm[cb % 2], 0)] * 4 + [(va, 0), (va, HALF)] + [(qk_tm[cb % 2], 0)] * 2
            dst += [(b, c) for b in (vr, gr, ga, gg) for c in (0, HALF)]
            buf, c0 = dst[cb]
            for tb in range(TB):
                proj_ready(cb, tb, U0["in"] + 2 * cb + 1)
                f = ACT.Sigmoid if cb > 12 else ACT.Copy
                act.activation(buf[:, tb, c0:c0 + HALF], proj(cb, tb)[:, :], f, scale=inv_rms("mix", tb))\
                   .then_inc(proj_out, 1)

        def exps(m, ready):
            act.wait_ge(score_out, ready + 1)
            for tb, c in enumerate((slice(0, P), slice(P, 384))):
                e = act.activation(L[:, m % 4, c], L[:, m % 4, c], ACT.Exp, bias=mn[:, m, tb:tb + 1], scale=-1.0,
                                   accum_out=sm[:, m, tb:tb + 1])
            e.then_inc(exp_ready, 1)

        def weights_copy(name, h):
            n = WB[name, h]
            act.wait_ge(work_done, n + 1)
            act.activation(aT[h % 2][:, :], work((name, h))[:, 0:384], ACT.Copy).then_inc(work_out[n % 2], 1)

        def diff_y(h):
            n = WB["v", h]
            act.wait_ge(work_done, n + 1)
            for tb in range(TB):
                y = act.activation(src[:, tb, h * P:(h + 1) * P], work(("v", h))[:, tb * P:(tb + 1) * P], ACT.Copy,
                                   scale=rsm[:, 2 * h, tb:tb + 1])
            y.then_inc(work_out[n % 2], 1)

        def ret_y(h):
            n = WB["rv", h]
            act.wait_ge(work_done, n + 1)
            act.activation(yr[:, :, h * RV:(h + 1) * RV], work(("rv", h))[:, :].rearrange("p (t n) -> p t n", n=RV),
                           ACT.Copy).then_inc(work_out[n % 2], 1)

        act.dma_start(gain[:, 0:HALF], g_mix[0, 0:HALF].partition_broadcast(P)).then_inc(mix_in[0], 16)
        act.dma_start(ident, masks_d[:, 0:P]).then_inc(ident_in, 16)
        act.wait_ge(nhalf_ready, 1)
        act.activation(junk[:, 0:1], nhalf[:, 0:1], ACT.Square).then_inc(act_warm, 1)
        act.wait_ge(act_warm, 1)
        split(("mix", 0, 0))
        for c, signal in enumerate((first_hi, hi_ready)):
            act.wait_ge(first_in[c], 16)
            cols = slice(c * UNIT // 2, (c + 1) * UNIT // 2)
            act.activation(w_hi[0][:, cols], raw[0][:, cols], ACT.Copy).then_inc(signal, 1)
        split(("mix", 1, 0))
        hi(1)
        split(("mix", 0, 1))
        squares("mix", 0)
        split(("mix", 1, 1))
        hi(2)
        squares("mix", 1)
        for k in range(IN_CB + 1):
            step = k - 1
            if 6 <= step < 14:
                weights_copy("a", step - 6)
            if k == 14:
                act.wait_ge(proj_out, 26)
                act.activation(gr[:, :, :], gr[:, :, :], ACT.Silu).then_inc(gates_ready, 1)
                act.activation(ga[:, :, 0:HALF], ga[:, :, 0:HALF], ACT.Sigmoid).then_inc(gates_ready, 1)
            if step >= 0:
                proj_copy(step)
            if k == IN_CB:
                split(("ya", 0, 0))
            if k < IN_CB:
                hi(2 * k + 3)
            if 6 <= step < 14:
                diff_y(step - 6)
            if step >= 12:
                ret_y(step - 12)
            if k == IN_CB:
                split(("ya", 0, 1))
            if step == 5:
                act.wait_ge(lam_prod, 2)
                act.activation(lam_s[:, 2:4], lam_s[:, 0:2], ACT.Exp).then_inc(lam_exp, 1)
            if 5 <= step < 13:
                for c in range(2):
                    exps(SOFT["d", step - 5, c], SM["d", step - 5, c])
            if k < IN_CB:
                hi(2 * k + 4)
        hi(U0["bd"] + 3)
        split_rows("ya", 1)
        hi(U0["br"])
        split_rows("yr", 0)
        for n in range(U0["br"] + 1, U0["br"] + 4):
            hi(n)
        split_rows("yr", 1)
        for n in range(U0["out"], U0["out"] + 3):
            hi(n)
        split_rows("m", 0)
        hi(U0["out"] + 3)
        split_rows("m", 1)
        hi(U0["ff"])
        squares("mlp", 0)
        hi(U0["ff"] + 1)
        split_rows("mlp", 0)
        hi(U0["ff"] + 2)
        squares("mlp", 1)
        split_rows("mlp", 1)
        hi(U0["ff"] + 3)

        def step_ready(i, tb, last_unit, di=0, du=0):
            if tb == 0:
                act.wait_ge(up_done, i + 1 + di)
            else:
                act.wait_ge(unit_used, last_unit + 1 + du)

        def relu(i, tb, r=0):
            step_ready(i, tb, U0["ff"] + 1 + (4 * i - 2 if i else 0), 3 * r, 12 * r)
            act.activation(act_r[:, tb, :], up(tb)[:, :], ACT.Relu, scale=rs2[:, tb:tb + 1]).then_inc(act_ready, 1)

        act.wait_ge(rs2_ready, 1)
        relu(0, 0)
        hi(U0["ff"] + 4)
        relu(0, 1)
        split(("p",))

        def relu_step(i, r=0):
            v = U0["ff"] + 2 + 4 * (i - 1)
            hi(v + 3, r)
            for tb in range(TB):
                split(("ff", i - 1, tb), 3 * r)
            hi(v + 4, r)
            for tb in range(TB):
                relu(i, tb, r)
            hi(v + 5, r)
            hi(v + 6, r)
        relu_step(1)
        with act.Fori(0, 2) as r:
            for j in range(3):
                relu_step(2 + j, r)
        for tb in range(TB):
            split(("ff", 7, tb))

        def ple_copy(tb):
            if tb == 0:
                act.wait_ge(pl_done, 1)
            else:
                act.wait_ge(unit_used, U0["pl"] + 1)
            for c in range(2):
                s = act.activation(pl_s[:, tb, c * HALF:(c + 1) * HALF], bank[4 + c][:, :], ACT.Copy)
            s.then_inc(pl_out, 1)

        def ple_gate(tb):
            if tb == 0:
                act.wait_ge(acc_done, ACC["pg"] + 1)
            else:
                act.wait_ge(unit_used, U0["pg"] + 4)
            scale = inv_rms("ple", tb)
            for c in range(2):
                s = act.activation(sg[:, tb, c * HALF:(c + 1) * HALF], acc(tb, c)[:, :], ACT.Sigmoid, scale=scale)
            s.then_inc(pg_sig, 1)

        ple_copy(0)
        hi(U0["pg"])
        squares("ple", 0)
        hi(U0["pg"] + 1)
        split_rows("ple", 0)
        hi(U0["pg"] + 2)
        ple_copy(1)
        hi(U0["pg"] + 3)
        squares("ple", 1)
        split_rows("ple", 1)
        ple_gate(0)
        hi(U0["f1"])
        squares("mid", 0)
        hi(U0["f1"] + 1)
        squares("ffn1", 0)
        split_rows("ffn1", 0)
        ple_gate(1)
        hi(U0["f1"] + 2)
        squares("mid", 1)
        split_rows("ffn1", 1)
        hi(U0["f1"] + 3)
        squares("ffn1", 1)

        def gated(name, norm, base):
            u, n = U0[name], FF2 // SUB

            def silu(i, tb, r=0):
                step_ready(base + i, tb, u + 1 + (3 * i - 1 if i else 0), 4 * r, 12 * r)
                act.activation(act_r[:, tb, 0:SUB], up(tb)[:, 0:SUB], ACT.Silu, scale=inv_rms(norm, tb))\
                   .then_inc(act_ready, 1)

            silu(0, 0)
            hi(u + 4)
            silu(0, 1)

            def step(i, r=0):
                v = u + 2 + 3 * (i - 1)
                hi(v + 3, r)
                for tb in range(TB):
                    split((name, i - 1, tb), 4 * r)
                hi(v + 4, r)
                for tb in range(TB):
                    silu(i, tb, r)
                hi(v + 5, r)
            step(1)
            with act.Fori(0, 2) as r:
                for i in range(2, 6):
                    step(i, r)
            v, i = u + 2 + 3 * (n - 2), n - 1
            for tb in range(TB):
                split((name, i - 1, tb))
            hi(v + 3)
            silu(i, 0)
            split((name, i, 0))
            hi(v + 4)
            silu(i, 1)
            split((name, i, 1))
            hi(v + 5)

        gated("f1", "ffn1", DFF // HALF)

        def in2_copy(n):
            buf, cols = [(cq, QR), (ckv, KVR + ROPE), (mq_tm, 512), (mk_tm, 512), (mv, 512)][n]
            for tb in range(TB):
                proj_ready(CB_IN2 + n, tb, U0["in2"] + 2 * n + 1)
                act.activation(buf[:, tb, :], proj(CB_IN2 + n, tb)[:, 0:cols], ACT.Copy, scale=inv_rms("mix2", tb))\
                   .then_inc(proj_out, 1)

        def pair(kind, j, last):
            weights_copy(kind + "a", 2 * j)
            if not last:
                for h in (2 * j + 2, 2 * j + 3):
                    exps(SOFT[kind, h], SM[kind, h])

        squares("mix2", 0)
        split_rows("mix2", 0)
        hi(U0["in2"] + 2)
        squares("mix2", 1)
        split_rows("mix2", 1)
        hi(U0["in2"] + 3)
        for n in range(1, 5):
            in2_copy(n - 1)
            hi(U0["in2"] + 2 + 2 * n)
            if n == 1:
                act.wait_ge(ang_ready, 1)
                act.activation(sin2[:, :, 16:32], sin2[:, :, 16:32], ACT.Sin).then_inc(trig_ready, 1)
                act.activation(cos2[:, :, 0:16], cos2[:, :, 0:16], ACT.Sin).then_inc(trig_ready, 1)
            if n == 2:
                act.wait_ge(proj_out, 2 * (CB_IN2 + 2))
                for tb in range(TB):
                    for m, (buf, cols) in enumerate(((cq, QR), (ckv, KVR))):
                        if tb or m:
                            act.wait_ge(csq, 2 * tb + m)
                        k = 2 * m + tb
                        act.activation(junk[:, 0:cols], buf[:, tb, 0:cols], ACT.Square, accum_out=ssc[:, k:k + 1])\
                           .then_inc(csq, 1)
            if n == 4:
                split(("cq", 0))
                split(("cq", 1))
                split(("ckv",))
            hi(U0["in2"] + 3 + 2 * n)
        in2_copy(4)
        hi(U0["ukv"])
        act.wait_ge(cstd, 1)

        def queries_copy(n):
            for tb in range(TB):
                proj_ready(CB_UQ + n, tb, U0["uq"] + n)
                act.activation(q_tm[:, tb, 4 * n:4 * n + 4, :],
                               proj(CB_UQ + n, tb)[:, 0:QR].rearrange("p (h c) -> p h c", c=MQ), ACT.Copy,
                               scale=rsc[:, tb:tb + 1]).then_inc(proj_out, 1)

        def keys_values_copy(tb):
            proj_ready(CB_UKV, tb, U0["ukv"])
            scale = rsc[:, 2 + tb:3 + tb]
            for c in range(2):
                heads = acc(tb, c)[:, :].rearrange("p (h c) -> p h c", c=NOPE + MV)
                act.activation(k_tm[:, tb, 4 * c:4 * c + 4, 0:NOPE], heads[:, :, 0:NOPE], ACT.Copy, scale=scale)
                kv = act.activation(v_tm[:, tb, 4 * c:4 * c + 4, :], heads[:, :, NOPE:NOPE + MV], ACT.Copy, scale=scale)
            kv.then_inc(proj_out, 1)

        def heads_copy(first, buf):
            for j in (1, 3):
                act.wait_ge(heads_done, first + j + 1)
                act.activation(buf[:, 2 * j:2 * j + 2, :], bank[j][0:MQ, :].rearrange("p (h t) -> p h t", t=SEQ),
                               ACT.Copy).then_inc(heads_out[1], 1)

        queries_copy(0)
        hi(U0["o2"])
        for h in range(2):
            exps(SOFT["b", h], SM["b", h])
        queries_copy(1)
        hi(U0["o2"] + 1)
        pair("b", 0, False)
        keys_values_copy(0)
        pair("b", 1, False)
        keys_values_copy(1)
        act.wait_ge(kr_ready, 1)
        for tb in range(TB):
            k = act.activation(k_tm[:, tb, :, NOPE:MQ], kr[:, tb, :].unsqueeze(1).to_broadcast([P, MH, ROPE]), ACT.Copy)
        k.then_inc(k_full, 1)
        pair("b", 2, False)
        heads_copy(0, qT)
        hi(U0["o2"] + 2)
        pair("b", 3, True)
        heads_copy(MH // 2, kT)
        hi(U0["o2"] + 3)
        for tb in range(TB):
            split(("cat", tb, 1))
        for h in range(2):
            exps(SOFT["l", h], SM["l", h])
        for j in range(MH // 2):
            pair("l", j, j == MH // 2 - 1)
            if j == 1:
                hi(U0["f2"])
        for tb in range(TB):
            split(("cat", tb, 0))
        hi(U0["f2"] + 1)
        squares("ffn2", 0)
        split_rows("ffn2", 0)
        hi(U0["f2"] + 2)
        squares("ffn2", 1)
        split_rows("ffn2", 1)
        hi(U0["f2"] + 3)
        gated("f2", "ffn2", DFF // HALF + FF2 // SUB)
        for tb in range(TB):
            squares("final", tb)

    @block.vector
    def _(vec):
        chain = [0]

        def link(ins):
            chain[0] += 1
            ins.then_inc(vec_step, 1)
            vec.wait_ge(vec_step, chain[0])

        def lo(u, du=0):
            if u >= N_UNITS:
                return
            vec.wait_ge(hi_ready, u + 1 + du)
            w = unit_width(u)
            vec.tensor_tensor(w_lo[u % RAW_SLOTS][:, 0:w], raw[u % RAW_SLOTS][:, 0:w],
                              w_hi[u % HI_SLOTS][:, 0:w].bitcast(f32), ALU.subtract).then_inc(lo_ready, 1)

        def split(name, di=0):
            vec.wait_ge(split_hi, SPLIT[name] + 1 + 2 * di)
            (hi, dst), b = rows_of(name)
            vec.tensor_tensor(dst, b, hi.bitcast(f32), ALU.subtract).then_inc(work_out[WB[name] % 2], 1)

        def split_rows(name, tb):
            for h in range(2):
                split((name, tb, h))

        def sums_ready(name, tb):
            if tb == 0:
                vec.wait_ge(acc_done, ACC[name] + 1)
            else:
                vec.wait_ge(unit_used, U0[name] + dict(UNITS)[name])

        def by_gain(name, tb, c):
            cols = slice(c * HALF, (c + 1) * HALF)
            if name == "mix":
                vec.wait_ge(mix_in[c], 16)
            else:
                vec.wait_ge(gain_in, GAIN[name])
            vec.tensor_tensor(src[:, tb, cols], x[:, tb, cols], gain[:, cols], ALU.mult).then_inc(src_ready, 1)

        def x_add(name, tb, scale, norm):
            sums_ready(name, tb)
            for c in range(2):
                xs = x[:, tb, c * HALF:(c + 1) * HALF]
                a = vec.scalar_tensor_tensor(out=xs, in0=acc(tb, c)[:, :], scalar=scale, in1=xs,
                                             op0=ALU.mult, op1=ALU.add)
                if c == 0:
                    link(a)
                else:
                    a.then_inc(acc_out, 1)
                    vec.wait_ge(acc_out, 2 * ACC[name] + tb + 1)
                by_gain(norm, tb, c)

        def logits(name, b, scale):
            m = SOFT[name]
            vec.wait_ge(score_done, SM[name] + 1)
            for tb, c in enumerate((slice(0, P), slice(P, 384))):
                t = vec.tensor_tensor_reduce(out=L[:, m % 4, c], in0=score(name)[:, c], in1=b[:, c], scale=-scale,
                                             scalar=3e38, op0=ALU.add, op1=ALU.min, accum_out=mn[:, m, tb:tb + 1])
            t.then_inc(score_out, 1)

        def diff_logits(h):
            vec.wait_ge(bias_ready, h + 1)
            for c in range(2):
                logits(("d", h, c), bias[h % 2], DHD ** -0.5)

        def combine(h):
            m = 2 * h
            vec.wait_ge(exp_ready, m + 2)
            link(vec.reciprocal(rsm[:, m:m + 2, :], sm[:, m:m + 2, :]))
            link(vec.scalar_tensor_tensor(out=qc[:, h, :], in0=rsm[:, m + 1, :], scalar=neglam[:, 0:1],
                                          in1=sm[:, m, :], op0=ALU.mult, op1=ALU.mult))
            for tb, c in enumerate((slice(0, P), slice(P, 384))):
                t = vec.scalar_tensor_tensor(out=L[:, (m + 1) % 4, c], in0=L[:, (m + 1) % 4, c],
                                             scalar=qc[:, h, tb:tb + 1], in1=L[:, m % 4, c],
                                             op0=ALU.mult, op1=ALU.add)
            t.then_inc(comb_ready, 1)

        def head_squares(name, h, buf, width, heads, sums, counter, scratch):
            n = WB[name, h]
            vec.wait_ge(work_out[n % 2], n // 2 + 1)
            for tb in range(TB):
                y = buf[:, tb, h * width:(h + 1) * width]
                k = 2 * h + tb
                if k:
                    vec.wait_ge(counter, k)
                vec.tensor_tensor_reduce(out=scratch[:, 0:width], in0=y, in1=y, scale=1.0, scalar=0.0, op0=ALU.mult,
                                         op1=ALU.add, accum_out=sums[:, tb * heads + h:tb * heads + h + 1])\
                   .then_inc(counter, 1)

        def first_operand(tb, half):
            vec.wait_ge(x_in[2 * tb + half], 16)
            by_gain("mix", tb, half)

        def first_unit(c, source, signal):
            vec.wait_ge(source, 1)
            cols = slice(c * UNIT // 2, (c + 1) * UNIT // 2)
            vec.tensor_tensor(w_lo[0][:, cols], raw[0][:, cols], w_hi[0][:, cols].bitcast(f32), ALU.subtract)\
               .then_inc(signal, 1)

        first_operand(0, 0)
        split(("mix", 0, 0))
        first_unit(0, first_hi, first_lo)
        first_operand(1, 0)
        first_unit(1, hi_ready, lo_ready)
        first_operand(0, 1)
        split(("mix", 1, 0))
        first_operand(1, 1)
        lo(1)
        split(("mix", 0, 1))
        split(("mix", 1, 1))
        lo(2)
        for k in range(IN_CB):
            step = k - 1
            if k == 3:
                vec.wait_ge(lam_in, 64)
                for n in range(2):
                    vec.tensor_tensor_reduce(out=lam_w[:, n, :], in0=lam_v[:, 2 * n, :], in1=lam_v[:, 2 * n + 1, :],
                                             scale=1.0, scalar=0.0, op0=ALU.mult, op1=ALU.add,
                                             accum_out=lam_s[:, n:n + 1]).then_inc(lam_prod, 1)
            if step in (1, 2, 3, 4, 7, 8):
                cb = step - 1
                dst, b0 = {0: (qaT, 0), 1: (qaT, 4), 2: (kaT, 0), 3: (kaT, 4), 6: (qrT, 0), 7: (krT, 0)}[cb]
                for tb in range(TB):
                    n = WB["qk", cb, tb]
                    vec.wait_ge(work_done, n + 1)
                    vec.tensor_copy(dst[:, b0:b0 + 4, tb * P:(tb + 1) * P],
                                    bank[6 + n % 2][:, :].rearrange("p (b t) -> p b t", t=P))\
                       .then_inc(work_out[n % 2], 1)
            if 5 <= step < 13:
                diff_logits(step - 5)
            if 11 <= step < 15:
                h = step - 11
                vec.wait_ge(decay_in[h % 2], 16 * (h // 2 + 1))
                vec.wait_ge(score_done, SM["r", h] + 1)
                vec.tensor_tensor(sT[h % 2][:, :], score(("r", h))[:, 0:384], decay[h % 2][:, :], ALU.mult)\
                   .then_inc(score_out, 1)
            lo(2 * k + 3)
            if 6 <= step < 14:
                head_squares("v", step - 6, src, P, DH, ssy, ysq, vjunk)
            if step >= 12:
                head_squares("rv", step - 12, yr, RV, RH, ssr, rsq, rjunk)
            if step == 5:
                vec.wait_ge(lam_exp, 1)
                link(vec.tensor_tensor(lam_s[:, 0:1], lam_s[:, 3:4], lam_s[:, 2:3], ALU.subtract))
                link(vec.tensor_scalar(neglam[:, :], lam_s[:, 0:1], -LAM_INIT, None, ALU.add))
            if 5 <= step < 13:
                combine(step - 5)
            if k == 15:
                vec.wait_ge(ystd, 1)
                vec.wait_ge(gd_in, 16)
                for n in range(2 * TB):
                    y = src[:, n // 2, n % 2 * HALF:(n % 2 + 1) * HALF].rearrange("p (h c) -> p h c", c=P)
                    r = rsy[:, n * DH // 2:(n + 1) * DH // 2]
                    link(vec.tensor_tensor(y, y, r.unsqueeze(2).to_broadcast([P, DH // 2, P]), ALU.mult))
                    vec.scalar_tensor_tensor(out=y, in0=y, scalar=1.0 - LAM_INIT,
                                             in1=gd[:, :].unsqueeze(1).to_broadcast([P, DH // 2, P]),
                                             op0=ALU.mult, op1=ALU.mult).then_inc(src_ready, 1)
                split(("ya", 0, 0))
            lo(2 * k + 4)
        split(("ya", 0, 1))
        head_squares("rv", 3, yr, RV, RH, ssr, rsq, rjunk)
        lo(U0["bd"] + 3)
        split_rows("ya", 1)
        vec.wait_ge(rstd_r, 1)
        vec.wait_ge(gsg_ready, 1)
        for tb in range(TB):
            y = yr[:, tb, :].rearrange("p (h c) -> p h c", c=RV)
            r = rsr[:, tb * RH:(tb + 1) * RH]
            link(vec.tensor_tensor(y, y, r.unsqueeze(2).to_broadcast([P, RH, RV]), ALU.mult))
            vec.tensor_tensor(yr[:, tb, :], yr[:, tb, :], gr[:, tb, :], ALU.mult).then_inc(yr_src, 1)

        def gate(name, tb, g, dst):
            sums_ready(name, tb)
            for c in range(2):
                cols = slice(c * HALF, (c + 1) * HALF)
                t = vec.tensor_tensor(dst[:, tb, cols], acc(tb, c)[:, :], g[:, tb, cols], ALU.mult)
            t.then_inc(acc_out, 1)

        vec.wait_ge(proj_out, 2 * IN_CB)

        def mix(tb):
            gate("br", tb, gg, mix_t)
            vec.wait_ge(acc_out, 2 * ACC["br"] + tb + 1)
            for c in range(2):
                cols = slice(c * HALF, (c + 1) * HALF)
                vec.tensor_tensor(src[:, tb, cols], src[:, tb, cols], mix_t[:, tb, cols], ALU.add)\
                   .then_inc(src_ready, 1)

        vec.wait_ge(gates_ready, 2)
        gate("bd", 0, ga, src)
        lo(U0["br"])
        split_rows("yr", 0)
        lo(U0["br"] + 1)
        lo(U0["br"] + 2)
        gate("bd", 1, ga, src)
        lo(U0["br"] + 3)
        split_rows("yr", 1)
        mix(0)
        lo(U0["out"])
        lo(U0["out"] + 1)
        split_rows("m", 0)
        mix(1)
        lo(U0["out"] + 2)
        lo(U0["out"] + 3)
        split_rows("m", 1)
        x_add("out", 0, 1.0, "mlp")
        lo(U0["ff"])
        lo(U0["ff"] + 1)
        split_rows("mlp", 0)
        x_add("out", 1, 1.0, "mlp")
        split_rows("mlp", 1)
        lo(U0["ff"] + 2)
        lo(U0["ff"] + 3)

        def square(i, tb, r=0):
            vec.wait_ge(act_ready, 2 * i + tb + 1 + 6 * r)
            vec.scalar_tensor_tensor(out=act_f[:, tb, :], in0=up(tb)[:, :], scalar=0.0, in1=act_r[:, tb, :],
                                     op0=ALU.max, op1=ALU.mult).then_inc(up_out, 1)

        square(0, 0)
        lo(U0["ff"] + 4)
        square(0, 1)
        split(("p",))

        def relu_step(i, r=0):
            v = U0["ff"] + 2 + 4 * (i - 1)
            lo(v + 3, 12 * r)
            for tb in range(TB):
                split(("ff", i - 1, tb), 3 * r)
            lo(v + 4, 12 * r)
            for tb in range(TB):
                square(i, tb, r)
            lo(v + 5, 12 * r)
            lo(v + 6, 12 * r)
        relu_step(1)
        with vec.Fori(0, 2) as r:
            for j in range(3):
                relu_step(2 + j, r)
        for tb in range(TB):
            split(("ff", 7, tb))
        lo(U0["pg"])
        x_add("ff", 0, 1.0, "ple")
        lo(U0["pg"] + 1)
        split_rows("ple", 0)
        x_add("ff", 1, 1.0, "ple")
        lo(U0["pg"] + 2)
        lo(U0["pg"] + 3)
        split_rows("ple", 1)

        def mid(tb):
            vec.wait_ge(pg_sig, tb + 1)
            for c in range(2):
                cols = slice(c * HALF, (c + 1) * HALF)
                link(vec.tensor_tensor(sg[:, tb, cols], sg[:, tb, cols], pl_s[:, tb, cols], ALU.mult))
                a = vec.tensor_tensor(x[:, tb, cols], x[:, tb, cols], sg[:, tb, cols], ALU.add)
                if c == 0:
                    link(a)
                    vec.wait_ge(gains_ready, 1)
                else:
                    a.then_inc(acc_out, 1)
                    vec.wait_ge(acc_out, 2 * ACC["pg"] + tb + 1)
                by_gain("ffn1", tb, c)

        def mid_norm(tb):
            n = SQ["mid", tb]
            vec.wait_ge(rstd_ready, n + 1)
            vec.wait_ge(src_ready, SRC["ffn1"] + 2 * tb + 2)
            vec.scalar_tensor_tensor(out=x[:, tb, :], in0=x[:, tb, :], scalar=rs[:, n:n + 1], in1=gain_mid[:, :],
                                     op0=ALU.mult, op1=ALU.mult).then_inc(mid_ready, 1)

        mid(0)
        lo(U0["f1"])
        mid_norm(0)
        lo(U0["f1"] + 1)
        split_rows("ffn1", 0)
        mid(1)
        split_rows("ffn1", 1)
        mid_norm(1)
        lo(U0["f1"] + 2)
        lo(U0["f1"] + 3)

        def gated(name, norm_in, base, norm_out):
            u, n = U0[name], FF2 // SUB

            def multiply(i, tb, r=0):
                n = SQ[norm_in, tb]
                vec.wait_ge(act_ready, 2 * (base + i) + tb + 1 + 8 * r)
                vec.scalar_tensor_tensor(out=act_f[:, tb, 0:SUB], in0=up(tb)[:, SUB:2 * SUB], scalar=rs[:, n:n + 1],
                                         in1=act_r[:, tb, 0:SUB], op0=ALU.mult, op1=ALU.mult).then_inc(up_out, 1)

            multiply(0, 0)
            lo(u + 4)
            multiply(0, 1)

            def step(i, r=0):
                v = u + 2 + 3 * (i - 1)
                lo(v + 3, 12 * r)
                for tb in range(TB):
                    split((name, i - 1, tb), 4 * r)
                lo(v + 4, 12 * r)
                for tb in range(TB):
                    multiply(i, tb, r)
                lo(v + 5, 12 * r)
            step(1)
            with vec.Fori(0, 2) as r:
                for i in range(2, 6):
                    step(i, r)
            v, i = u + 2 + 3 * (n - 2), n - 1
            for tb in range(TB):
                split((name, i - 1, tb))
            lo(v + 3)
            multiply(i, 0)
            split((name, i, 0))
            lo(v + 4)
            multiply(i, 1)
            split((name, i, 1))
            lo(v + 5)
            if norm_out == "final":
                final_norm()
            else:
                x_add(name, 0, 0.5, norm_out)
                split_rows(norm_out, 0)
                x_add(name, 1, 0.5, norm_out)
                split_rows(norm_out, 1)
                lo(v + 6)

        def final_norm():
            for tb in range(TB):
                sums_ready("f2", tb)
                for c in range(2):
                    xs = x[:, tb, c * HALF:(c + 1) * HALF]
                    a = vec.scalar_tensor_tensor(out=xs, in0=acc(tb, c)[:, :], scalar=0.5, in1=xs,
                                                 op0=ALU.mult, op1=ALU.add)
                a.then_inc(acc_out, 1)
                vec.wait_ge(gain_in, GAIN["final"])
                n = SQ["final", tb]
                vec.wait_ge(rstd_ready, n + 1)
                vec.wait_ge(acc_out, 2 * ACC["f2"] + tb + 1)
                for c in range(2):
                    cols = slice(c * HALF, (c + 1) * HALF)
                    vec.scalar_tensor_tensor(out=src[:, tb, cols], in0=x[:, tb, cols], scalar=rs[:, n:n + 1],
                                             in1=gain[:, cols], op0=ALU.mult, op1=ALU.mult).then_inc(src_ready, 1)

        gated("f1", "ffn1", DFF // HALF, "mix2")

        def positions():
            vec.wait_ge(pos_in, 64)
            link(vec.tensor_copy(pos_k[:, :], pos_ki[:, :]))
            link(vec.tensor_copy(pos_q[:, :], pos_qi[:, :]))
            vec.tensor_scalar(posdist[:, 0:P], pos_k[:, 0:P], pos_q[:, 0:1], None, ALU.subtract)
            link(vec.tensor_scalar(posdist[:, P:384], pos_k[:, :], pos_q[:, 1:2], None, ALU.subtract))
            link(vec.scalar_tensor_tensor(out=posdist[:, :], in0=posdist[:, :], scalar=-1.0, in1=posdist[:, :],
                                          op0=ALU.mult, op1=ALU.min))
            vec.tensor_tensor(posdist[:, :], posdist[:, :], mask, ALU.add).then_inc(pos_ready, 1)
            for tb in range(TB):
                link(vec.tensor_scalar(ang[:, tb, :], freq[:, :], pos_q[:, tb:tb + 1], None, ALU.mult))
            link(vec.tensor_scalar(turns_[:, :, :], ang[:, :, :], 1 / (2 * math.pi), None, ALU.mult))
            link(vec.tensor_scalar(turns_[:, :, :], turns_[:, :, :], 1.5 * 2 ** 23, None, ALU.add))
            link(vec.tensor_scalar(turns_[:, :, :], turns_[:, :, :], -1.5 * 2 ** 23, None, ALU.add))
            part1 = 6.28125
            part2 = float(np.float32(round((2 * math.pi - part1) * 2 ** 21) / 2 ** 21))
            for part in (part1, part2, 2 * math.pi - part1 - part2):
                link(vec.scalar_tensor_tensor(out=ang[:, :, :], in0=turns_[:, :, :], scalar=-part, in1=ang[:, :, :],
                                              op0=ALU.mult, op1=ALU.add))
            edge = float(np.nextafter(np.float32(math.pi), np.float32(0)))
            link(vec.tensor_scalar(sin2[:, :, 16:32], ang[:, :, :], edge, -edge, ALU.min, ALU.max))
            link(vec.scalar_tensor_tensor(out=cos2[:, :, 0:16], in0=sin2[:, :, 16:32], scalar=-1.0,
                                          in1=sin2[:, :, 16:32], op0=ALU.mult, op1=ALU.min))
            vec.tensor_scalar(cos2[:, :, 0:16], cos2[:, :, 0:16], math.pi / 2, None, ALU.add).then_inc(ang_ready, 1)

        def trig_pairs():
            vec.wait_ge(trig_ready, 2)
            link(vec.tensor_copy(cos2[:, :, 16:32], cos2[:, :, 0:16]))
            link(vec.tensor_scalar(sin2[:, :, 0:16], sin2[:, :, 16:32], -1.0, None, ALU.mult))

        def block_logits(kind, h):
            if kind == "b":
                vec.wait_ge(bias_ready, DH + h + 1)
                logits(("b", h), bias[h % 2], BD ** -0.5)
            else:
                logits(("l", h), mask, MQ ** -0.5)

        def next_pair(kind, j):
            for h in (2 * j, 2 * j + 1):
                block_logits(kind, h)

        def pair_y(kind, j):
            m, n = SOFT[kind, 2 * j], WB[kind + "v", j]
            vec.wait_ge(exp_ready, m + 2)
            link(vec.reciprocal(rsm[:, m:m + 2, :], sm[:, m:m + 2, :]))
            vec.wait_ge(work_done, n + 1)
            c0 = (2 * j + (MH if kind == "b" else 0)) * BD
            vec.tensor_tensor(src[:, :, c0:c0 + 2 * BD].rearrange("p t (h c) -> p h t c", c=BD),
                              work((kind + "v", j))[:, 0:4 * BD].rearrange("p (h t c) -> p h t c", h=2, t=TB),
                              rsm[:, m:m + 2, :].unsqueeze(3).to_broadcast([P, 2, TB, BD]), ALU.mult)\
               .then_inc(work_out[n % 2], 1)

        def pair(kind, j, last):
            n = WB[kind + "a", 2 * j + 1]
            vec.wait_ge(work_done, n + 1)
            vec.tensor_copy(aT[1][:, :], work((kind + "a", 2 * j + 1))[:, 0:384]).then_inc(work_out[n % 2], 1)
            if not last:
                next_pair(kind, j + 1)

        def heads_copy(first, buf):
            for j in (0, 2):
                vec.wait_ge(heads_done, first + j + 1)
                vec.tensor_copy(buf[:, 2 * j:2 * j + 2, :], bank[j][0:MQ, :].rearrange("p (h t) -> p h t", t=SEQ))\
                   .then_inc(heads_out[0], 1)

        def turned_copy(name, dst):
            n = WB[name]
            vec.wait_ge(work_done, n + 1)
            rows = dst.shape[0]
            vec.tensor_copy(dst, work(name)[0:rows, :].rearrange("p (b t) -> p b t", t=dst.shape[-1]))\
               .then_inc(work_out[n % 2], 1)

        lo(U0["in2"] + 3)
        positions()
        lo(U0["in2"] + 4)
        trig_pairs()
        lo(U0["in2"] + 5)
        vec.wait_ge(csq, 4)
        vec.wait_ge(gain_in, GAIN["c"])
        for tb in range(TB):
            for n, (buf, c0, cols) in enumerate(((cq, 0, QR), (ckv, QR, KVR))):
                vec.tensor_tensor(buf[:, tb, 0:cols], buf[:, tb, 0:cols], gain[:, c0:c0 + cols], ALU.mult)\
                   .then_inc(c_src, 1)
        lo(U0["in2"] + 6)
        rotate(vec, link, ckv[:, :, KVR:KVR + ROPE], kr[:, :, :], rope_t[:, :, :], cos2[:, :, :], sin2[:, :, :])\
            .then_inc(kr_ready, 1)
        lo(U0["in2"] + 7)
        lo(U0["in2"] + 8)
        for tb in range(TB):
            turned_copy(("mq", tb), mqT[:, :, tb * P:(tb + 1) * P])
        split(("cq", 0))
        split(("cq", 1))
        split(("ckv",))
        lo(U0["in2"] + 9)
        lo(U0["uq"])
        for tb in range(TB):
            turned_copy(("mk", tb), mkT[:, :, tb * P:(tb + 1) * P])
        lo(U0["uq"] + 1)
        next_pair("b", 0)
        lo(U0["ukv"])
        pair("b", 0, False)
        pair_y("b", 0)
        pair("b", 1, False)
        pair_y("b", 1)
        pair("b", 2, False)
        heads_copy(0, qT)
        pair_y("b", 2)
        lo(U0["o2"])
        pair("b", 3, True)
        heads_copy(MH // 2, kT)
        pair_y("b", 3)
        next_pair("l", 0)
        for tb in range(TB):
            split(("cat", tb, 1))
        lo(U0["o2"] + 1)
        for j in range(MH // 2):
            pair("l", j, j == MH // 2 - 1)
            pair_y("l", j)
            if j < 2:
                lo(U0["o2"] + 2 + j)
        for tb in range(TB):
            split(("cat", tb, 0))
        lo(U0["f2"])
        lo(U0["f2"] + 1)
        x_add("o2", 0, 1.0, "ffn2")
        split_rows("ffn2", 0)
        x_add("o2", 1, 1.0, "ffn2")
        split_rows("ffn2", 1)
        lo(U0["f2"] + 2)
        lo(U0["f2"] + 3)
        gated("f2", "ffn2", DFF // HALF + FF2 // SUB, "final")

    @block.gpsimd
    def _(pool):
        chain = [0]

        def link(ins):
            chain[0] += 1
            ins.then_inc(pool_step, 1)
            pool.wait_ge(pool_step, chain[0])

        def load_gain(name, *parts):
            c0 = 0
            for g in parts:
                n = g.shape[-1]
                pool.dma_start(gain[:, c0:c0 + n], g.partition_broadcast(P)).then_inc(gain_in, 16)
                c0 += n

        def inverse_rms(s, m, r, width):
            link(pool.tensor_scalar(m, s, 1.0 / width, EPS, ALU.mult, ALU.add))
            return pool.tensor_tensor(r, m, nhalf[:, 0:r.shape[-1]], ALU.pow)

        def rstd(name):
            for tb in range(TB):
                n = SQ[name, tb]
                pool.wait_ge(square_sum, n + 1)
                inverse_rms(ss[:, n:n + 1], ms[:, n:n + 1], rs[:, n:n + 1], D).then_inc(rstd_ready, 1)

        def head_bias(k, base, slope, scale):
            pool.tensor_scalar(bias[k % 2][:, :], base, slope / scale, 1.0, ALU.mult, ALU.mult).then_inc(bias_ready, 1)

        pool.memset(nhalf[:, :], -0.5).then_inc(nhalf_ready, 1)
        pool.wait_ge(nhalf_ready, 1)
        pool.wait_ge(x_in[3], 16)
        pool.dma_start(masks[:, P:], masks_d[:, P:]).then_inc(mask_in, 16)
        for n, lam in enumerate((lam_q1, lam_k1, lam_q2, lam_k2)):
            pool.dma_start(lam_v[:, n, :], lam[0].partition_broadcast(P)).then_inc(lam_in, 16)
        pool.dma_start(gd[:, :], g_diff[0].partition_broadcast(P)).then_inc(gd_in, 16)
        pool.dma_start(decay[0][:, :], decay_d[0]).then_inc(decay_in[0], 16)
        pool.dma_start(decay[1][:, :], decay_d[1]).then_inc(decay_in[1], 16)
        rstd("mix")
        pool.wait_ge(mask_in, 16)
        for h in range(DH):
            if h >= 2:
                pool.wait_ge(score_out, SM["d", h - 2, 1] + 1)
            head_bias(h, negdist, alibi(h), DHD ** -0.5)
        pool.wait_ge(src_ready, SRC["mix"] + 2 * TB)
        load_gain("ret", g_ret[0])
        for h in (2, 3):
            pool.wait_ge(score_out, SM["r", h - 2] + 1)
            pool.dma_start(decay[h % 2][:, :], decay_d[h]).then_inc(decay_in[h % 2], 16)
        pool.wait_ge(ysq, TB * DH)
        inverse_rms(ssy[:, :], msy[:, :], rsy[:, :], P).then_inc(ystd, 1)
        pool.wait_ge(gates_ready, 1)
        pool.wait_ge(gain_in, GAIN["ret"])
        pool.tensor_tensor(gr[:, :, :], gr[:, :, :], gain[:, :].unsqueeze(1).to_broadcast([P, TB, D]), ALU.mult)\
            .then_inc(gsg_ready, 1)
        pool.wait_ge(rsq, TB * RH)
        inverse_rms(ssr[:, :], msr[:, :], rsr[:, 0:TB * RH], RV).then_inc(rstd_r, 1)
        pool.wait_ge(gsg_ready, 1)
        load_gain("mlp", g_mlp[0])
        pool.wait_ge(square_sum, SQ["mlp", 0] + 1)
        pool.dma_start(p_sb[:, :, :], p_d.rearrange("(b p) n -> p b n", p=P)).then_inc(p_in, 16)
        rstd("mlp")
        n = SQ["mlp", 0]
        pool.wait_ge(rstd_ready, n + 2)
        pool.tensor_tensor(rs2[:, :], rs[:, n:n + 2], rs[:, n:n + 2], ALU.mult).then_inc(rs2_ready, 1)
        pool.wait_ge(src_ready, SRC["mlp"] + 2 * TB)
        load_gain("ple", g_ple[0])
        pool.dma_start(gain_mid[:, :], g_fin1.partition_broadcast(P)).then_inc(mid_in, 16)
        pool.dma_start(pos_ki[:, :], pos_d[0].partition_broadcast(P)).then_inc(pos_in, 16)
        for tb in range(TB):
            pool.dma_start(pos_qi[:, tb:tb + 1], pos_d[0, tb * P:(tb + 1) * P].rearrange("(p o) -> p o", o=1))\
                .then_inc(pos_in, 16)
        pool.dma_start(freq[:, :], freq_d.partition_broadcast(P)).then_inc(pos_in, 16)
        rstd("ple")
        pool.wait_ge(src_ready, SRC["ple"] + 2 * TB)
        load_gain("ffn1", g_ffn1[0])
        pool.wait_ge(gain_in, GAIN["ffn1"])
        pool.wait_ge(mid_in, 16)
        pool.tensor_tensor(gain[:, :], gain[:, :], gain_mid[:, :], ALU.mult).then_inc(gains_ready, 1)
        for tb in range(TB):
            m, n = SQ["mid", tb], SQ["ffn1", tb]
            pool.wait_ge(square_sum, m + 1)
            inverse_rms(ss[:, m:m + 1], ms[:, m:m + 1], rs[:, m:m + 1], D).then_inc(rstd_ready, 1)
            pool.wait_ge(rstd_ready, m + 1)
            pool.wait_ge(square_sum, n + 1)
            link(inverse_rms(ss[:, n:n + 1], ms[:, n:n + 1], rs[:, n:n + 1], D))
            pool.tensor_tensor(rs[:, n:n + 1], rs[:, n:n + 1], rs[:, m:m + 1], ALU.mult).then_inc(rstd_ready, 1)
        pool.wait_ge(src_ready, SRC["ffn1"] + 2 * TB)
        load_gain("mix2", g_mix2[0])
        rstd("mix2")
        pool.wait_ge(src_ready, SRC["mix2"] + 2 * TB)
        load_gain("c", g_q[0], g_kv[0])
        pool.wait_ge(pos_ready, 1)

        def block_bias(h):
            if h >= 2:
                pool.wait_ge(score_out, SM["b", h - 2] + 1)
            head_bias(DH + h, posdist[:, :], alibi(h), BD ** -0.5)
        for h in range(2):
            block_bias(h)
        pool.wait_ge(csq, 4)
        for n, cols in enumerate((QR, KVR)):
            r = inverse_rms(ssc[:, 2 * n:2 * n + 2], msc[:, 2 * n:2 * n + 2], rsc[:, 2 * n:2 * n + 2], cols)
        r.then_inc(cstd, 1)
        for h in range(2, 4):
            block_bias(h)
        pool.wait_ge(proj_out, 2 * CB_UKV)
        heads = lambda t: t[:, :, :].unsqueeze(2).to_broadcast([P, TB, MH, ROPE])
        q_rot = q_tm[:, :, :, NOPE:MQ]
        pool.wait_ge(kr_ready, 1)
        rotate(pool, link, q_rot, q_rot, rot_t[:, :, :, :], heads(cos2), heads(sin2)).then_inc(rot_ready, 1)
        for h in range(4, BH):
            block_bias(h)
        pool.wait_ge(c_src, 4)
        load_gain("ffn2", g_ffn2[0])
        rstd("ffn2")
        pool.wait_ge(src_ready, SRC["ffn2"] + 2 * TB)
        load_gain("final", g_final)
        rstd("final")

    ctx.close()


_INS = ["x", "p", "g_mix", "w_in", "lam_q1", "lam_k1", "lam_q2", "lam_k2", "g_diff_sub", "g_ret_sub",
        "w_branch_diff", "w_branch_ret", "w_out", "g_mlp", "w_ff1", "w_ff2", "g_ple", "w_ple_gate", "w_ple", "g_final",
        "positions_2", "ffn1_norm_2", "ffn1_w_gate_2", "ffn1_w_up_2", "ffn1_w_down_2", "mix_norm_2",
        "w_in_2", "mla_q_norm_2", "mla_w_uq_2", "mla_kv_norm_2", "mla_w_ukv_2", "w_out_2", "ffn2_norm_2",
        "ffn2_w_gate_2", "ffn2_w_up_2", "ffn2_w_down_2", "final_norm_2"]


def _constants():
    t = np.arange(SEQ)
    dist = t[:, None] - t[None, :]
    causal = lambda m: np.concatenate([m[0:P, 0:P], m[P:SEQ, :]], 1)
    mask = causal(np.where(dist >= 0, 0.0, -BIG))
    negdist = causal(np.where(dist >= 0, -dist, -BIG))
    masks = np.concatenate([np.eye(P), mask, negdist], 1).astype(np.float32)
    log_gamma = np.log(1.0 - 2.0 ** (-5.0 - np.arange(RH)))
    decay = []
    for h in range(RH):
        m = np.where(dist >= 0, np.exp(log_gamma[h] * dist), 0.0).T * RK ** -0.5
        decay.append(np.concatenate([m[0:P, :], m[P:SEQ, P:SEQ]], 1))
    half = ROPE // 2
    freq = np.power(np.float32(10000.0), -np.arange(half, dtype=np.float32) * np.float32(2.0) / np.float32(ROPE))
    return {"masks": masks, "decay": np.stack(decay).astype(np.float32), "freq": freq.astype(np.float32)}


def kernel(**inputs):
    import concourse.bacc as bacc
    from concourse.bass_utils import run_bass_kernel_spmd

    nc = bacc.Bacc("TRN2", target_bir_lowering=False, num_devices=1)
    arrays = {}
    for name in _INS:
        a = np.asarray(inputs[name])
        if name in ("x", "p") or name.startswith(("w_", "ffn1_w", "ffn2_w", "mla_w")) or name == "g_ret_sub":
            a = a.reshape(-1, a.shape[-1]) if name != "g_ret_sub" else a.reshape(1, -1)
        arrays[f"in_{name}"] = np.ascontiguousarray(a)
    for name, a in _constants().items():
        arrays[f"const_{name}"] = a
    d = {n: nc.dram_tensor(n, a.shape, mybir.dt.from_np(a.dtype), kind="ExternalInput").ap() for n, a in arrays.items()}
    out = nc.dram_tensor("out", (SEQ, D), mybir.dt.float32, kind="ExternalOutput").ap()
    args = [d[f"in_{n}"] for n in _INS] + [d["const_masks"], d["const_decay"], d["const_freq"], out]
    two_blocks(nc, *args)
    r = run_bass_kernel_spmd(nc, [arrays], core_ids=[0])
    return r.results[0]["out"].reshape(1, SEQ, D)
```
